# Optimizing a Trainium2 kernel written in Bass

```python
import jax, jax.numpy as jnp
from jax import lax
import numpy as np
import jax
import jax.numpy as jnp

D_MODEL = 1024
BATCH = 1
SEQ = 512
DEPTH = 1

POOL_WINDOWS = (2, 4, 8, 16)
POOL_GROUPS = len(POOL_WINDOWS)
POOL_WIDTH = D_MODEL // 2
POOL_GW = POOL_WIDTH // POOL_GROUPS
N_HEADS = 16
HEAD_DIM = 64
N_KV_GROUPS = 2
HPG = N_HEADS // N_KV_GROUPS
NSA_WIDTH = N_HEADS * HEAD_DIM
KV_WIDTH = N_KV_GROUPS * HEAD_DIM
CMP_LEN = 32
CMP_STRIDE = 16
CMP_HIDDEN = 256
SEL_BLOCK = 64
N_SEL = 16
WINDOW = 512
Q_BLOCK = 64
SEL_BONUS = 1e4
NEG_INF = -1e30
ROPE_THETA = 10000.0
D_FF = 4 * D_MODEL
RMS_EPS = 1e-6
IN_SIZES = (POOL_WIDTH, NSA_WIDTH, KV_WIDTH, KV_WIDTH, KV_WIDTH, KV_WIDTH, KV_WIDTH, KV_WIDTH, 3 * N_HEADS, 2 * D_MODEL)
N_IN = sum(IN_SIZES)
IN_SPLITS = tuple(int(v) for v in np.cumsum(IN_SIZES)[:-1])


def rms_norm(x, g):
    xf = x.astype(jnp.float32)
    y = xf * lax.rsqrt(jnp.mean(xf * xf, axis=-1, keepdims=True) + RMS_EPS)
    return (y * g.astype(jnp.float32)).astype(x.dtype)

def rope_tables(pos):
    inv = ROPE_THETA ** (-jnp.arange(0, HEAD_DIM, 2, dtype=jnp.float32) / HEAD_DIM)
    ang = pos.astype(jnp.float32)[:, None] * inv[None, :]
    ang = jnp.concatenate([ang, ang], axis=-1)
    return jnp.cos(ang), jnp.sin(ang)

def apply_rope(x, cos, sin):
    x1, x2 = jnp.split(x, 2, axis=-1)
    rot = jnp.concatenate([-x2, x1], axis=-1)
    y = x.astype(jnp.float32) * cos[:, None, :] + rot.astype(jnp.float32) * sin[:, None, :]
    return y.astype(x.dtype)

def masked_softmax(s, mask):
    s = jnp.where(mask, s.astype(jnp.float32), NEG_INF)
    return jnp.where(mask, jax.nn.softmax(s, axis=-1), 0.0)

def pool_mixer(u, w_pool, pool_scale):
    B, S, _ = u.shape
    uf = u.astype(jnp.float32)
    csum = jnp.pad(jnp.cumsum(uf, axis=1), ((0, 0), (1, 0), (0, 0)))
    t = jnp.arange(S)
    diffs = []
    for g, w in enumerate(POOL_WINDOWS):
        c = csum[:, :, g * POOL_GW:(g + 1) * POOL_GW]
        upper = c[:, 1:]
        lower = jnp.pad(c, ((0, 0), (w - 1, 0), (0, 0)))[:, :S]
        count = jnp.minimum(t + 1, w).astype(jnp.float32)[None, :, None]
        diffs.append((upper - lower) / count - uf[:, :, g * POOL_GW:(g + 1) * POOL_GW])
    d = jnp.stack(diffs, axis=2)
    y = jnp.einsum('bsgc,gcd->bsgd', d, w_pool.astype(jnp.float32)).reshape(B, S, POOL_WIDTH)
    return (y * pool_scale.astype(jnp.float32)).astype(u.dtype)

def compress(k, pe, w1, w2):
    B, S, G, dh = k.shape
    r = CMP_LEN // CMP_STRIDE
    n_chunks = S // CMP_STRIDE
    n_cmp = n_chunks - r + 1
    ch = k.reshape(B, n_chunks, CMP_STRIDE, G, dh)
    blocks = jnp.concatenate([ch[:, j:j + n_cmp] for j in range(r)], axis=2)
    blocks = blocks + pe[None, None, :, None, :]
    flat = blocks.transpose(0, 1, 3, 2, 4).reshape(B, n_cmp, G, CMP_LEN * dh)
    return jax.nn.gelu(flat @ w1) @ w2

def nsa_mixer(q, kc, vc, ks, vs, kw, vw, g_nsa, pe_k, pe_v, w_ck1, w_ck2, w_cv1, w_cv2):
    B, S = q.shape[:2]
    G, dh = N_KV_GROUPS, HEAD_DIM
    cos, sin = rope_tables(jnp.arange(S))
    q = apply_rope(q.reshape(B, S, N_HEADS, dh), cos, sin).reshape(B, S, G, HPG, dh)
    ks = apply_rope(ks.reshape(B, S, G, dh), cos, sin)
    kw = apply_rope(kw.reshape(B, S, G, dh), cos, sin)
    vs = vs.reshape(B, S, G, dh)
    vw = vw.reshape(B, S, G, dh)
    k_cmp = compress(kc.reshape(B, S, G, dh), pe_k, w_ck1, w_ck2)
    v_cmp = compress(vc.reshape(B, S, G, dh), pe_v, w_cv1, w_cv2)
    n_cmp = k_cmp.shape[1]
    cmp_start = jnp.arange(n_cmp) * CMP_STRIDE
    cmp_end = cmp_start + CMP_LEN - 1
    ccos, csin = rope_tables(cmp_end)
    k_cmp = apply_rope(k_cmp, ccos, csin)
    n_slc = S // SEL_BLOCK
    k_blk = ks.reshape(B, n_slc, SEL_BLOCK, G, dh).transpose(0, 3, 1, 2, 4)
    v_blk = vs.reshape(B, n_slc, SEL_BLOCK, G, dh).transpose(0, 3, 1, 2, 4)
    slc_start = jnp.arange(n_slc) * SEL_BLOCK
    slc_idx = jnp.arange(n_slc)
    overlap = ((cmp_start[:, None] <= slc_start[None, :] + SEL_BLOCK - 1)
               & (cmp_end[:, None] >= slc_start[None, :])).astype(jnp.float32)
    n_pick = min(N_SEL, n_slc)
    gather_blocks = jax.vmap(jax.vmap(lambda kb, i: kb[i]))
    win_len = Q_BLOCK + WINDOW - 1
    kw_pad = jnp.pad(kw, ((0, 0), (WINDOW - 1, 0), (0, 0), (0, 0)))
    vw_pad = jnp.pad(vw, ((0, 0), (WINDOW - 1, 0), (0, 0), (0, 0)))
    scale = HEAD_DIM ** -0.5
    gates = jax.nn.sigmoid(g_nsa.astype(jnp.float32)).reshape(B, S, G, HPG, 3)

    def block(s0):
        t = s0 + jnp.arange(Q_BLOCK)
        qb = lax.dynamic_slice_in_dim(q, s0, Q_BLOCK, axis=1)
        gb = lax.dynamic_slice_in_dim(gates, s0, Q_BLOCK, axis=1)
        s_c = jnp.einsum('bqghd,bngd->bghqn', qb, k_cmp) * scale
        p_c = masked_softmax(s_c, cmp_end[None, :] <= t[:, None])
        o_c = jnp.einsum('bghqn,bngd->bqghd', p_c, v_cmp)
        imp = jnp.einsum('bghqn,nj->bgqj', p_c, overlap)
        causal = slc_start[None, :] <= t[:, None]
        cur = t // SEL_BLOCK
        forced = causal & ((slc_idx[None, :] == 0) | (slc_idx[None, :] >= cur[:, None] - 1))
        score = jnp.where(forced, SEL_BONUS, jnp.where(causal, imp, NEG_INF))
        top_v, idx = lax.top_k(score, n_pick)
        sel_ok = top_v > 0.5 * NEG_INF
        idx_flat = idx.reshape(B, G, Q_BLOCK * n_pick)
        k_sel = gather_blocks(k_blk, idx_flat).reshape(B, G, Q_BLOCK, n_pick * SEL_BLOCK, dh)
        v_sel = gather_blocks(v_blk, idx_flat).reshape(B, G, Q_BLOCK, n_pick * SEL_BLOCK, dh)
        key_pos = idx[..., None] * SEL_BLOCK + jnp.arange(SEL_BLOCK)
        ok = (sel_ok[..., None] & (key_pos <= t[:, None, None])).reshape(B, G, Q_BLOCK, n_pick * SEL_BLOCK)
        s_s = jnp.einsum('bqghd,bgqkd->bghqk', qb, k_sel) * scale
        p_s = masked_softmax(s_s, ok[:, :, None])
        o_s = jnp.einsum('bghqk,bgqkd->bqghd', p_s, v_sel)
        kwb = lax.dynamic_slice_in_dim(kw_pad, s0, win_len, axis=1)
        vwb = lax.dynamic_slice_in_dim(vw_pad, s0, win_len, axis=1)
        kpos = s0 - (WINDOW - 1) + jnp.arange(win_len)
        wmask = (kpos[None, :] <= t[:, None]) & (kpos[None, :] > t[:, None] - WINDOW) & (kpos[None, :] >= 0)
        s_w = jnp.einsum('bqghd,bkgd->bghqk', qb, kwb) * scale
        p_w = masked_softmax(s_w, wmask)
        o_w = jnp.einsum('bghqk,bkgd->bqghd', p_w, vwb)
        o = gb[..., 0:1] * o_c + gb[..., 1:2] * o_s + gb[..., 2:3] * o_w
        return o.reshape(B, Q_BLOCK, NSA_WIDTH)

    out = lax.map(block, jnp.arange(S // Q_BLOCK) * Q_BLOCK)
    return out.transpose(1, 0, 2, 3).reshape(B, S, NSA_WIDTH)

def first_inputs(seed: int = 0) -> dict:
    key = jax.random.key(seed)
    ks = jax.random.split(key, 20)
    f32 = jnp.float32

    def nrm(k, shape, fan_in):
        return jax.random.normal(k, shape, f32) * (fan_in ** -0.5)

    return {
        'x': jax.random.normal(ks[0], (BATCH, SEQ, D_MODEL), f32),
        'norm_mix': 1.0 + 0.05 * jax.random.normal(ks[1], (DEPTH, D_MODEL), f32),
        'w_in': nrm(ks[2], (DEPTH, D_MODEL, N_IN), D_MODEL),
        'w_pool': nrm(ks[3], (DEPTH, POOL_GROUPS, POOL_GW, POOL_GW), POOL_GW),
        'pool_scale': 1.0 + 0.1 * jax.random.normal(ks[4], (DEPTH, POOL_WIDTH), f32),
        'pe_k': 0.1 * jax.random.normal(ks[5], (DEPTH, CMP_LEN, HEAD_DIM), f32),
        'pe_v': 0.1 * jax.random.normal(ks[6], (DEPTH, CMP_LEN, HEAD_DIM), f32),
        'w_ck1': nrm(ks[7], (DEPTH, CMP_LEN * HEAD_DIM, CMP_HIDDEN), CMP_LEN * HEAD_DIM),
        'w_ck2': nrm(ks[8], (DEPTH, CMP_HIDDEN, HEAD_DIM), CMP_HIDDEN),
        'w_cv1': nrm(ks[9], (DEPTH, CMP_LEN * HEAD_DIM, CMP_HIDDEN), CMP_LEN * HEAD_DIM),
        'w_cv2': nrm(ks[10], (DEPTH, CMP_HIDDEN, HEAD_DIM), CMP_HIDDEN),
        'w_proj_pool': nrm(ks[11], (DEPTH, POOL_WIDTH, D_MODEL), POOL_WIDTH),
        'w_proj_nsa': nrm(ks[12], (DEPTH, NSA_WIDTH, D_MODEL), NSA_WIDTH),
        'w_out': nrm(ks[13], (DEPTH, D_MODEL, D_MODEL), D_MODEL),
        'norm_mlp': 1.0 + 0.05 * jax.random.normal(ks[14], (DEPTH, D_MODEL), f32),
        'w_ff1': nrm(ks[15], (DEPTH, D_MODEL, D_FF), D_MODEL),
        'w_ff2': nrm(ks[16], (DEPTH, D_FF, D_MODEL), D_FF),
        'norm_final': 1.0 + 0.05 * jax.random.normal(ks[17], (D_MODEL,), f32),
    }

def first_block(x, norm_mix, w_in, w_pool, pool_scale, pe_k, pe_v, w_ck1, w_ck2, w_cv1, w_cv2,
              w_proj_pool, w_proj_nsa, w_out, norm_mlp, w_ff1, w_ff2, norm_final):
    for l in range(DEPTH):
        h = rms_norm(x, norm_mix[l])
        proj = h @ w_in[l]
        u, q, kc, vc, ksl, vsl, kwn, vwn, g_nsa, g_merge = jnp.split(proj, IN_SPLITS, axis=-1)
        y_pool = pool_mixer(u, w_pool[l], pool_scale[l])
        y_nsa = nsa_mixer(q, kc, vc, ksl, vsl, kwn, vwn, g_nsa, pe_k[l], pe_v[l],
                          w_ck1[l], w_ck2[l], w_cv1[l], w_cv2[l]).astype(x.dtype)
        g_a, g_b = jnp.split(jax.nn.sigmoid(g_merge.astype(jnp.float32)).astype(x.dtype), 2, axis=-1)
        merged = g_a * (y_pool @ w_proj_pool[l]) + g_b * (y_nsa @ w_proj_nsa[l])
        x = x + merged @ w_out[l]
        h = rms_norm(x, norm_mlp[l])
        x = x + jnp.square(jax.nn.relu(h @ w_ff1[l])) @ w_ff2[l]
    return rms_norm(x, norm_final)


N_FOX_HEADS = 8
N_SB_HEADS = 8
FOX_WIDTH = N_FOX_HEADS * HEAD_DIM
SB_WIDTH = N_SB_HEADS * HEAD_DIM
N_GROUPS = 4
EXPERTS_PER_GROUP = 4
N_EXPERTS = N_GROUPS * EXPERTS_PER_GROUP
TOP_K_EXPERTS = 2
D_FF_EXPERT = D_MODEL // 2
Q_BLOCK_2 = 128
N_MOD = 6
IN_SPLITS_2 = (
    FOX_WIDTH, 2 * FOX_WIDTH, 3 * FOX_WIDTH,
    3 * FOX_WIDTH + N_FOX_HEADS,
    3 * FOX_WIDTH + N_FOX_HEADS + SB_WIDTH,
    3 * FOX_WIDTH + N_FOX_HEADS + 2 * SB_WIDTH,
    3 * FOX_WIDTH + N_FOX_HEADS + 3 * SB_WIDTH,
    3 * FOX_WIDTH + N_FOX_HEADS + 3 * SB_WIDTH + D_MODEL,
)
N_IN_2 = 3 * FOX_WIDTH + N_FOX_HEADS + 3 * SB_WIDTH + 2 * D_MODEL


def rmsnorm(x, g):
    xf = x.astype(jnp.float32)
    xf = xf * lax.rsqrt(jnp.mean(xf * xf, axis=-1, keepdims=True) + RMS_EPS)
    return xf.astype(x.dtype) * g

def to_heads(t, n_heads):
    b, s, _ = t.shape
    return t.reshape(b, s, n_heads, HEAD_DIM).transpose(0, 2, 1, 3)

def from_heads(t):
    b, h, s, d = t.shape
    return t.transpose(0, 2, 1, 3).reshape(b, s, h * d)

def sweep_query_blocks(block_fn, seq):
    n_blocks = seq // Q_BLOCK_2
    out = lax.map(block_fn, jnp.arange(n_blocks))
    nb, b, h, qb, d = out.shape
    return out.transpose(1, 2, 0, 3, 4).reshape(b, h, nb * qb, d)

def forgetting_attention(q, k, v, log_f):
    seq = q.shape[2]
    scale = HEAD_DIM ** -0.5
    F = jnp.cumsum(log_f, axis=-1)
    kpos = jnp.arange(seq)

    def block(i):
        start = i * Q_BLOCK_2
        qs = lax.dynamic_slice_in_dim(q, start, Q_BLOCK_2, axis=2)
        Fq = lax.dynamic_slice_in_dim(F, start, Q_BLOCK_2, axis=2)
        logits = jnp.einsum("bhqd,bhkd->bhqk", qs, k).astype(jnp.float32) * scale
        logits = logits + Fq[..., :, None] - F[..., None, :]
        qpos = start + jnp.arange(Q_BLOCK_2)
        mask = kpos[None, :] <= qpos[:, None]
        logits = jnp.where(mask, logits, -jnp.inf)
        p = jax.nn.softmax(logits, axis=-1)
        return jnp.einsum("bhqk,bhkd->bhqd", p.astype(v.dtype), v)

    return sweep_query_blocks(block, seq)

def stick_breaking_attention(q, k, v):
    seq = q.shape[2]
    scale = HEAD_DIM ** -0.5
    kpos = jnp.arange(seq)

    def block(i):
        start = i * Q_BLOCK_2
        qs = lax.dynamic_slice_in_dim(q, start, Q_BLOCK_2, axis=2)
        z = jnp.einsum("bhqd,bhkd->bhqk", qs, k).astype(jnp.float32) * scale
        qpos = start + jnp.arange(Q_BLOCK_2)
        mask = kpos[None, :] < qpos[:, None]
        log_beta = jax.nn.log_sigmoid(z)
        log_one_minus = jnp.where(mask, jax.nn.log_sigmoid(-z), 0.0)
        suffix = lax.cumsum(log_one_minus, axis=3, reverse=True) - log_one_minus
        A = jnp.where(mask, jnp.exp(log_beta + suffix), 0.0)
        return jnp.einsum("bhqk,bhkd->bhqd", A.astype(v.dtype), v)

    return sweep_query_blocks(block, seq)

def hierarchical_moe(h, rg_w, rg_b, re_w, re_b, w_gate, w_up, w_down):
    b, s, d = h.shape
    hf = h.reshape(b * s, d)
    g_prob = jax.nn.softmax((hf @ rg_w + rg_b).astype(jnp.float32), axis=-1)
    g_top_p, g_idx = lax.top_k(g_prob, 1)
    e_logits = (hf @ re_w + re_b).astype(jnp.float32).reshape(b * s, N_GROUPS, EXPERTS_PER_GROUP)
    e_sel = jnp.take_along_axis(e_logits, g_idx[:, :, None], axis=1)[:, 0, :]
    e_prob = jax.nn.softmax(e_sel, axis=-1)
    e_top_p, e_idx = lax.top_k(e_prob, TOP_K_EXPERTS)
    e_top_p = e_top_p / jnp.sum(e_top_p, axis=-1, keepdims=True)
    within = jnp.sum(jax.nn.one_hot(e_idx, EXPERTS_PER_GROUP, dtype=jnp.float32)
                     * e_top_p[..., None], axis=1)
    combine = (jax.nn.one_hot(g_idx[:, 0], N_GROUPS, dtype=jnp.float32)[:, :, None]
               * within[:, None, :] * g_top_p[:, :, None])
    combine = combine.reshape(b * s, N_EXPERTS).astype(h.dtype)
    out = jnp.zeros_like(hf)
    for e in range(N_EXPERTS):
        act = jax.nn.silu(hf @ w_gate[e]) * (hf @ w_up[e])
        out = out + combine[:, e:e + 1] * (act @ w_down[e])
    return out.reshape(b, s, d)

def second_inputs(seed: int = 0) -> dict:
    key = jax.random.key(seed)
    ks = jax.random.split(key, 20)
    D, L = D_MODEL, DEPTH

    def nrm(k, shape, scale):
        return jax.random.normal(k, shape, jnp.float32) * scale

    return {
        "x": nrm(ks[0], (BATCH, SEQ, D), 1.0),
        "c": nrm(ks[1], (BATCH, D), 1.0),
        "ada_w": nrm(ks[2], (L, D, N_MOD * D), 0.5 * D ** -0.5),
        "ada_b": nrm(ks[3], (L, N_MOD * D), 0.02),
        "norm1_g": 1.0 + nrm(ks[4], (L, D), 0.02),
        "w_in": nrm(ks[5], (L, D, N_IN_2), D ** -0.5),
        "b_forget": 2.0 + nrm(ks[6], (L, N_FOX_HEADS), 0.1),
        "w_branch_fox": nrm(ks[7], (L, FOX_WIDTH, D), FOX_WIDTH ** -0.5),
        "w_branch_sb": nrm(ks[8], (L, SB_WIDTH, D), SB_WIDTH ** -0.5),
        "w_out": nrm(ks[9], (L, D, D), D ** -0.5),
        "norm2_g": 1.0 + nrm(ks[10], (L, D), 0.02),
        "router_group_w": nrm(ks[11], (L, D, N_GROUPS), D ** -0.5),
        "router_group_b": nrm(ks[12], (L, N_GROUPS), 0.01),
        "router_expert_w": nrm(ks[13], (L, D, N_EXPERTS), D ** -0.5),
        "router_expert_b": nrm(ks[14], (L, N_EXPERTS), 0.01),
        "expert_w_gate": nrm(ks[15], (L, N_EXPERTS, D, D_FF_EXPERT), D ** -0.5),
        "expert_w_up": nrm(ks[16], (L, N_EXPERTS, D, D_FF_EXPERT), D ** -0.5),
        "expert_w_down": nrm(ks[17], (L, N_EXPERTS, D_FF_EXPERT, D), D_FF_EXPERT ** -0.5),
        "final_g": 1.0 + nrm(ks[18], (D,), 0.02),
    }

def second_block(x, c, ada_w, ada_b, norm1_g, w_in, b_forget, w_branch_fox, w_branch_sb, w_out,
              norm2_g, router_group_w, router_group_b, router_expert_w, router_expert_b,
              expert_w_gate, expert_w_up, expert_w_down, final_g):
    c_act = jax.nn.silu(c)
    for l in range(DEPTH):
        mod = c_act @ ada_w[l] + ada_b[l]
        shift1, scale1, gate1, shift2, scale2, gate2 = [m[:, None, :] for m in jnp.split(mod, N_MOD, axis=-1)]

        h = rmsnorm(x, norm1_g[l]) * (1.0 + scale1) + shift1
        proj = h @ w_in[l]
        qa, ka, va, fa, qb, kb, vb, ga, gb = jnp.split(proj, IN_SPLITS_2, axis=-1)
        log_f = jax.nn.log_sigmoid((fa + b_forget[l]).astype(jnp.float32)).transpose(0, 2, 1)
        o_fox = forgetting_attention(to_heads(qa, N_FOX_HEADS), to_heads(ka, N_FOX_HEADS),
                                     to_heads(va, N_FOX_HEADS), log_f)
        o_sb = stick_breaking_attention(to_heads(qb, N_SB_HEADS), to_heads(kb, N_SB_HEADS),
                                        to_heads(vb, N_SB_HEADS))
        merged = (jax.nn.sigmoid(ga) * (from_heads(o_fox) @ w_branch_fox[l])
                  + jax.nn.sigmoid(gb) * (from_heads(o_sb) @ w_branch_sb[l]))
        x = x + gate1 * (merged @ w_out[l])

        h2 = rmsnorm(x, norm2_g[l]) * (1.0 + scale2) + shift2
        y = hierarchical_moe(h2, router_group_w[l], router_group_b[l], router_expert_w[l],
                             router_expert_b[l], expert_w_gate[l], expert_w_up[l], expert_w_down[l])
        x = x + gate2 * y
    return rmsnorm(x, final_g)


def setup_inputs(seed=0):
    out = dict(first_inputs(seed))
    for name, value in second_inputs(seed + 1).items():
        if name != "x":
            out[name + "_2"] = value
    return out


def reference(
    x, norm_mix, w_in, w_pool, pool_scale, pe_k, pe_v, w_ck1, w_ck2, w_cv1, w_cv2, w_proj_pool,
    w_proj_nsa, w_out, norm_mlp, w_ff1, w_ff2, norm_final, c_2, ada_w_2, ada_b_2, norm1_g_2,
    w_in_2, b_forget_2, w_branch_fox_2, w_branch_sb_2, w_out_2, norm2_g_2, router_group_w_2,
    router_group_b_2, router_expert_w_2, router_expert_b_2, expert_w_gate_2, expert_w_up_2,
    expert_w_down_2, final_g_2,
):
    x = first_block(
        x, norm_mix, w_in, w_pool, pool_scale, pe_k, pe_v, w_ck1, w_ck2, w_cv1, w_cv2,
        w_proj_pool, w_proj_nsa, w_out, norm_mlp, w_ff1, w_ff2, norm_final,
    )
    return second_block(
        x, c_2, ada_w_2, ada_b_2, norm1_g_2, w_in_2, b_forget_2, w_branch_fox_2, w_branch_sb_2,
        w_out_2, norm2_g_2, router_group_w_2, router_group_b_2, router_expert_w_2,
        router_expert_b_2, expert_w_gate_2, expert_w_up_2, expert_w_down_2, final_g_2,
    )


_drawn_inputs = setup_inputs


def setup_inputs(seed=0):
    import zlib

    import numpy as np

    out = dict(_drawn_inputs(seed))
    spreads = {}
    factors = {'pe_k': 8.0,
     'pe_v': 2.815,
     'ada_b_2': 3.143,
     'norm1_g_2': 8.0,
     'b_forget_2': 8.0,
     'norm2_g_2': 4.841,
     'router_group_b_2': 64.0,
     'router_expert_b_2': 8.0,
     'final_g_2': 7.649}
    for name, (base, spread) in spreads.items():
        noise = np.random.default_rng([zlib.crc32(name.encode()), seed]).standard_normal(out[name].shape)
        drawn = base * np.exp(spread * noise) if base else spread * noise
        out[name] = jnp.asarray(drawn.astype(out[name].dtype))
    for name, factor in factors.items():
        out[name] = (out[name] * factor).astype(out[name].dtype)
    return out
```

```python
from contextlib import ExitStack

import numpy as np

import concourse.bass as bass
from concourse import mybir

F32 = mybir.dt.float32
F32R = mybir.dt.float32r
BF16 = mybir.dt.bfloat16
I32 = mybir.dt.int32
U32 = mybir.dt.uint32
ALU = mybir.AluOpType
ACT = mybir.ActivationFunctionType
AX = mybir.AxisListType.X

S = 512
D = 1024
NEG = -1e30
EPS = 1e-6
NRAW = 5
NSPL = 4
NUNIT = 23
CMP = 31
PACK = (0, 512, 1024, 896)


class Queue:

    def __init__(self, sem):
        self.sem, self.n, self.items, self.seen = sem, 0, [], {}

    def need(self, *tokens):
        for t in tokens:
            if t is None:
                continue
            if isinstance(t, list):
                self.need(*t)
                continue
            sem, value = t
            if self.seen.get(id(sem), 0) < value:
                self.seen[id(sem)] = value
                self.items.append(("wait", sem, value))

    def do(self, fn, *tokens):
        self.need(*tokens)
        self.n += 1
        self.items.append(("op", fn, (self.sem, 1)))
        return (self.sem, self.n)

    def quiet(self, fn, *tokens):
        self.need(*tokens)
        self.items.append(("op", fn, None))

    def dma(self, fn, sem, value, *tokens):
        self.need(*tokens)
        self.items.append(("op", fn, (sem, 16)))
        return (sem, value)

    def emit(self, eng):
        for kind, a, b in self.items:
            if kind == "wait":
                eng.wait_ge(a, b)
            else:
                ins = a(eng)
                if b is not None:
                    ins.then_inc(b[0], b[1])


class Bank:

    def __init__(self, ap):
        self.ap, self.free = ap, []


def program(nc, t, stop=None):
    ctx = ExitStack()
    with ctx:
        def sb(name, shape, dt=F32):
            return ctx.enter_context(nc.sbuf_tensor(name, shape, dt))

        def sem(name):
            return ctx.enter_context(nc.semaphore(name))

        RS = sb("RS", [128, NSPL, 2, 1024], F32R)
        RH = sb("RH", [128, 2, 8, S], F32R)
        RA = sb("RA", [128, 2, 8, S], F32R)
        RAW = sb("RAW", [128, NRAW, 1024])
        X = sb("X", [128, 8, S])
        M = sb("M", [128, 8, S])
        PB = sb("PB", [128, 2, 1280])
        TB = sb("TB", [128, 2, 1280])
        PC = sb("PC", [128, 4, S])
        TAB = sb("TAB", [128, 2, S])
        VV = sb("VV", [128, 2, S])
        TMP = sb("TMP", [128, 4, S])
        identf = sb("identf", [128, 128])
        rotT = sb("rotT", [128, 128])
        onesf = sb("onesf", [128, 128])
        ntri = sb("ntri", [128, 128])
        nones = sb("nones", [128, 128])
        sltm = sb("sltm", [128, 128])
        identb = sb("identb", [128, 128], BF16)
        maskb = sb("maskb", [128, 128], BF16)
        maskt = sb("maskt", [128, 128], BF16)
        trib = sb("trib", [128, 128], BF16)
        onesb = sb("onesb", [128, 128], BF16)
        vecs = sb("vecs", [128, 64])
        modt = sb("modt", [128, 48])
        gsc = sb("gsc", [128, 32])
        small = sb("small", [128, 64])
        RT = sb("RT", [128, 704])
        banks = [Bank(ctx.enter_context(nc.psum_tensor(f"ps{i}", [128, 512], F32))) for i in range(8)]

        pe, act, dve, pool, sp = (Queue(sem("s_" + n)) for n in ("pe", "act", "dve", "pool", "sp"))

        def hiF(ap):
            return ap.bitcast(F32)

        counter = [0]
        every = []

        def load(q, dst, src, *tokens):
            counter[0] += 1
            s = sem(f"d{counter[0]}")
            every.append((s, 16))
            return q.dma(lambda e: e.dma_start(dst, src), s, 16, *tokens)

        def a_act(out, in_, func, *tokens, **kw):
            return act.do(lambda e: e.activation(out, in_, func, **kw), *tokens)

        def tt(q, out, a, b, op, *tokens):
            return q.do(lambda e: e.tensor_tensor(out, a, b, op), *tokens)

        def ts(q, out, a, s1, op0, *tokens, s2=None, op1=None):
            if op1 is None:
                return q.do(lambda e: e.tensor_scalar(out, a, s1, None, op0), *tokens)
            return q.do(lambda e: e.tensor_scalar(out, a, s1, s2, op0, op1), *tokens)

        def stt(out, a, s, b, op0, op1, *tokens):
            return dve.do(lambda e: e.scalar_tensor_tensor(out, a, s, b, op0, op1), *tokens)

        def copy(q, out, in_, *tokens):
            if q is act:
                return a_act(out, in_, ACT.Copy, *tokens)
            return q.do(lambda e: e.tensor_copy(out, in_), *tokens)

        def mm(out, lhsT, rhs, start, stop, *tokens, last=False, shared=False):
            fn = lambda e: e.matmul(out, lhsT, rhs, start=start, stop=stop, skip_group_check=shared)
            return pe.do(fn, *tokens) if last else pe.quiet(fn, *tokens)

        def tr(out, in_, *tokens, last=False, ident=None):
            n = in_.shape[0]
            idn = identf[0:n, 0:n]
            fn = lambda e: e.transpose(out, in_, idn)
            return pe.do(fn, *tokens) if last else pe.quiet(fn, *tokens)

        plan = []

        def add(name, kind):
            for u in range(t[name].shape[0]):
                plan.append((name, u, t[name][u], kind))

        def add1(name, u, kind="split"):
            plan.append((name, u, t[name][u], kind))

        add("w_qkv", "split")
        add("w_c", "raw")
        for m in range(8):
            add1("w_gb", m)
            if m % 2 == 1:
                add1("w_nsa", m - 1)
                add1("w_nsa", m)
        add("w_u", "split")
        for m in range(8):
            add1("w_ga", m)
            if m % 2 == 1:
                add1("w_pp", m // 2)
        add("w_out", "split")
        ada = iter(range(48))
        for f in range(4):
            for m in range(8):
                add1("w_ff1", f * 8 + m)
                for u in [x for _, x in zip(range(1), ada)]:
                    add1("ada", u, "raw")
            for m in range(8):
                add1("w_ff2", f * 8 + m)
                if m % 2:
                    for u in [x for _, x in zip(range(1), ada)]:
                        add1("ada", u, "raw")
        for n in ("w2_qa", "w2_fa", "w2_ka", "w2_va", "w2_qb", "w2_kb", "w2_vb"):
            add(n, "split")
        for m in range(0, 8, 2):
            add1("w2_ga", m)
            add1("w2_ga", m + 1)
            add1("w2_fox", m // 2)
            add1("w2_gb", m)
            add1("w2_gb", m + 1)
            add1("w2_sb", m // 2)
        add("w2_out", "split")
        extra_reg = {}
        for u in range(NUNIT):
            for n in ("w_gate", "w_up"):
                for c in range(4):
                    plan.append((n, (u, c), None, "split"))
            if u:
                for c in range(4):
                    plan.append(("w_down", (u - 1, c), None, "split"))
        for c in range(4):
            plan.append(("w_down", (NUNIT - 1, c), None, "split"))

        raw_sem = [sem(f"raw{i}") for i in range(NRAW)]
        raw_free = [[] for _ in range(NRAW)]
        spl_free = [[] for _ in range(NSPL)]
        st = {"load": 0, "split": 0, "nsplit": 0, "get": 0}
        landed, parts = {}, {}
        lo_engine = [lambda n: pool]
        late = {}

        def stream_load(n):
            name, u, src, kind = plan[n]
            r = n % NRAW
            dst = RAW[:, r, :]
            need = list(raw_free[r])
            if src is None:
                uu, c = u
                if uu < 16:
                    src = t[name][uu, c]
                else:
                    if uu not in late:
                        late[uu] = True
                        need.append(late["tok"])
                        j = uu - 16

                        def ld(e, j=j):
                            extra_reg[j] = e.value_load(EXI[0:1, j:j + 1], min_val=0, max_val=15)
                        sp.need(late["tok"])
                        sp.items.append(("call", ld, None))

                    def fn(e, j=uu - 16, name=name, c=c):
                        w = t[name][bass.ds(extra_reg[j], 1), c, :, :].rearrange("a p n -> (a p) n")
                        return e.dma_start(dst, w)
                    landed[n] = sp.dma(fn, raw_sem[r], 16 * (n // NRAW + 1), need)
                    return
            landed[n] = sp.dma(lambda e: e.dma_start(dst, src), raw_sem[r], 16 * (n // NRAW + 1), need)

        def stream_split(n):
            if plan[n][3] == "raw":
                return
            k = st["nsplit"]
            st["nsplit"] += 1
            s, r = k % NSPL, n % NRAW
            hi = a_act(RS[:, s, 0, :], RAW[:, r, :], ACT.Copy, landed[n], spl_free[s])
            q = lo_engine[0](k)
            lo = tt(q, RS[:, s, 1, :], RAW[:, r, :], hiF(RS[:, s, 0, :]), ALU.subtract,
                    landed[n], hi, spl_free[s])
            raw_free[r] = [hi, lo]
            parts[n] = (s, lo, hi)

        def get(name, u):
            n = st["get"]
            assert plan[n][:2] == (name, u), (plan[n][:2], name, u)
            while st["load"] <= min(n + NRAW - 1, len(plan) - 1):
                stream_load(st["load"])
                st["load"] += 1
                while st["split"] < min(st["load"], n + NSPL):
                    stream_split(st["split"])
                    st["split"] += 1
            while st["split"] <= min(n + NSPL - 1, len(plan) - 1):
                stream_split(st["split"])
                st["split"] += 1
            st["get"] += 1
            return n

        def used(n, tok):
            if plan[n][3] == "raw":
                raw_free[n % NRAW] = [tok]
            else:
                spl_free[parts[n][0]] = [tok]

        ring = [0]

        def bank(pool_=None):
            b = (pool_ or range(8))
            ring[0] += 1
            return banks[b[ring[0] % len(b)]]

        def dense(name, u, acts, K, finish, which=range(8)):
            R, k0, toks = acts
            n = get(name, u)
            s, lo_t, hi_t = parts[n]
            for m in range(8 // K):
                b = bank(which)
                for k in range(K):
                    c = (m * K + k) * 128
                    wh, wl = RS[:, s, 0, c:c + 128], RS[:, s, 1, c:c + 128]
                    xh, xl = R[:, 0, k0 + k, :], R[:, 1, k0 + k, :]
                    mm(b.ap[:, :], wh, xh, k == 0, False, hi_t, toks[k], *(b.free if k == 0 else ()))
                    mm(b.ap[:, :], wh, xl, False, False)
                    tok = mm(b.ap[:, :], wl, xh, False, k == K - 1, lo_t, last=(k == K - 1))
                if m == 8 // K - 1:
                    used(n, tok)
                finish((8 // K) * u + m, b, tok)

        def dense_rows(name, units, acts, finish, which):
            R, k0, toks = acts
            for u in range(units):
                n = get(name, u)
                s, lo_t, hi_t = parts[n]
                for kk in range(2):
                    k = 2 * u + kk
                    wh, wl = (RS[:, s, x, kk * 512:kk * 512 + 512] for x in (0, 1))
                    for i in range(4):
                        b = banks[which[i]]
                        xh, xl = (R[:, x, k0 + k, 128 * i:128 * i + 128] for x in (0, 1))
                        mm(b.ap[:, :], xh, wh, k == 0, False, hi_t, toks[k], *(b.free if k == 0 else ()))
                        mm(b.ap[:, :], xl, wh, False, False)
                        tok = mm(b.ap[:, :], xh, wl, False, k == 7, lo_t, last=True)
                        if k == 7:
                            finish(i, b, tok)
                used(n, tok)

        def split_to(R, k, src, hi_q, lo_q, free, *tokens):
            hi = copy(hi_q, R[:, 0, k, :], src, free, *tokens)
            lo = tt(lo_q, R[:, 1, k, :], src, hiF(R[:, 0, k, :]), ALU.subtract, hi, free, *tokens)
            return hi, lo

        tmp_free = [[] for _ in range(4)]
        cst = {}
        xt = [load(act, X[:, 2 * i:2 * i + 2, :], t["xT"][:, 2 * i:2 * i + 2, :]) for i in range(4)]
        cst["onesf"] = load(act, onesf[:, :], t["onesf"])
        cst["vecs"] = load(act, vecs[:, :], t["vecs"])
        for name, dst in (("identf", identf), ("rotT", rotT)):
            cst[name] = load(act, dst[:, :], t[name])
        cst["tab"] = load(act, TAB[:, :, :], t["tab"])
        for name, dst in (("ntri", ntri), ("nones", nones), ("sltm", sltm), ("maskb", PC[:, 2, 0:128]),
                          ("maskt", PC[:, 2, 128:256])):
            cst[name] = load(act, dst[:, :], t[name])
        for name, dst, src in (("identb", identb, "identf"), ("maskb", maskb, "maskb"), ("maskt", maskt, "maskt"),
                               ("trib", trib, "sltm"), ("onesb", onesb, "onesf")):
            frm = {"identf": identf, "sltm": sltm, "onesf": onesf, "maskb": PC[:, 2, 0:128],
                   "maskt": PC[:, 2, 128:256]}[src]
            cst[name] = copy(pool, dst[:, :], frm[:, :], cst[src])
        eps = dve.do(lambda e: e.memset(small[:, 0:1], EPS))
        one = dve.do(lambda e: e.memset(small[:, 1:2], 1.0))
        zz = dve.do(lambda e: e.memset(PC[:, 0:2, :], 0.0))
        zx = [load(pool, t["xs"][128 * u:128 * u + 128, :].rearrange("p (a n) -> p a n", a=2),
                   PC[:, 0:2, :], zz) for u in range(NUNIT)]

        VG_MIX, VG_MLP, VG_FIN, V_PS, VG1, VG2, V_C, V_BF = 0, 8, 16, 24, 28, 36, 44, 52

        def rstd(xtoks, out, *free):
            b = bank()
            for k in range(8):
                s = a_act(TMP[:, k % 2, :], X[:, k, :], ACT.Square, xtoks[k], tmp_free[k % 2])
                tok = mm(b.ap[:, :], onesf[:, :], TMP[:, k % 2, :], k == 0, k == 7, s, cst["onesf"],
                         *(b.free if k == 0 else ()), last=True)
                tmp_free[k % 2] = [tok]
            r = a_act(out, b.ap[:, :], ACT.Sqrt, tok, eps, *free, bias=small[:, 0:1], scale=1.0 / D)
            b.free = [r]
            return dve.do(lambda e: e.reciprocal(out, out), r)

        RST = RT[:, 0:512]
        rst_free = [[]]

        def normed(xtoks, gcol, scol, h_free):
            r = rstd(xtoks, RST, *rst_free[0])
            toks = []
            for k in range(8):
                j = 2 + k % 2
                w = stt(TMP[:, j, :], X[:, k, :], gcol(k), RST, ALU.mult, ALU.mult, r, xtoks[k],
                        cst["vecs"], tmp_free[j])
                if scol is not None:
                    w = ts(dve, TMP[:, j, :], TMP[:, j, :], scol(k), ALU.add, w)
                hi, lo = split_to(RH, k, TMP[:, j, :], act, pool if k % 2 else dve, h_free, w)
                tmp_free[j] = [hi, lo]
                toks.append([hi, lo])
            rst_free[0] = [w]
            return toks

        H = normed([xt[k // 2] for k in range(8)], lambda k: vecs[:, VG_MIX + k:VG_MIX + k + 1], None, [])
        hx = (RH, 0, H)

        Kz = M[:, :, :].rearrange("p (b g r) n -> p b g r n", b=2, g=2)
        kzero = [dve.do(lambda e, i=i: e.memset(M[:, 4 * i:4 * i + 4, :], 0.0)) for i in range(2)]
        scz = dve.do(lambda e: e.memset(PB[:, 1, :], 0.0))
        scz2 = dve.do(lambda e: e.memset(TB[:, 1, 0:1024], 0.0))

        def rope(m, outs):
            def first(b, tok, scale):
                j = m % 2
                e1 = a_act(TMP[:, j, :], b.ap[:, :], ACT.Copy, tok, tmp_free[j], scale=scale)
                b.free = [e1]

                def second():
                    b2 = bank()
                    r = mm(b2.ap[:, :], rotT[:, :], TMP[:, j, :], True, True, e1, cst["rotT"], b2.free,
                           last=True)
                    c = tt(pool, TMP[:, 2 + j, :], TMP[:, j, :], TAB[:, 0, :], ALU.mult, e1,
                           cst["tab"], tmp_free[2 + j])
                    s_ = tt(dve, TMP[:, j, :], b2.ap[:, :], TAB[:, 1, :], ALU.mult, r, c, cst["tab"])
                    b2.free = [s_]
                    toks = []
                    for (lo_, hi_), dst, fr in outs:
                        toks.append(tt(dve, dst, TMP[lo_:hi_, j, :], TMP[lo_:hi_, 2 + j, :], ALU.add,
                                       s_, c, fr))
                    tmp_free[j] = [toks[-1]]
                    tmp_free[2 + j] = [toks[-1]]
                    return toks
                return second
            return first

        pend = [None]

        def flush():
            if pend[0] is not None:
                f, pend[0] = pend[0], None
                f()

        xread = H[7]
        qtok = {}
        ktok = {}
        vtok = {}
        cmpt = {}
        F2 = PB[:, 0, 0:1024].rearrange("p (g n) -> p g n", g=2)
        Fpk, Fpv = PB[:, 1, 0:992], TB[:, 0, 0:992]

        def fin_qkv(u, b, tok):
            flush()
            if u < 8:
                sec = rope(u, [((0, 128), X[:, u, :], xread)])(b, tok, 0.125)

                def g():
                    qtok[u] = sec()[0]
                pend[0] = g
            elif u < 10:
                br = u - 8
                outs = []
                for g_ in range(2):
                    for p_ in range(2):
                        outs.append(((64 * g_, 64 * g_ + 64), Kz[64 * p_:64 * p_ + 64, br, g_, p_, :], kzero))
                sec = rope(u, outs)(b, tok, 1.0)

                def g():
                    tk = sec()
                    for g_ in range(2):
                        for p_ in range(2):
                            ktok[(br, g_, p_)] = tk[2 * g_ + p_]
                pend[0] = g
            elif u < 12:
                src = b.ap
                kv = u - 10
                fre = cmpt.get("f2free", [])
                cs = []
                for g_ in range(2):
                    cs.append(copy(dve, F2[0:64, g_, :], src[64 * g_:64 * g_ + 64, :], tok, fre))
                    cs.append(copy(dve, F2[64:128, g_, 0:511], src[64 * g_:64 * g_ + 64, 1:512], tok, fre))
                b.free = [cs[-1]]
                Fp = (Fpk, Fpv)[kv]
                for lp in range(16):
                    o = Fp[:, lp * 62:lp * 62 + 62].rearrange("p (g n) -> p g n", g=2)
                    i_ = F2[:, :, 2 * lp:2 * lp + 481:16]
                    last = ts(dve, o, i_, PE2[:, kv * 16 + lp:kv * 16 + lp + 1], ALU.add, cs, cst["pe2"], scz)
                cmpt["f2free"] = [last]
                cmpt[kv] = last
            elif u < 14:
                br = u - 12
                j = u % 2
                e1 = copy(act, TMP[:, j, :], b.ap[:, :], tok, tmp_free[j])
                b.free = [e1]

                def g():
                    b2 = bank()
                    for i in range(4):
                        tk = tr(b2.ap[:, 128 * i:128 * i + 128], TMP[:, j, 128 * i:128 * i + 128], e1,
                                cst["identf"], *(b2.free if i == 0 else ()), last=(i == 3))
                    tmp_free[j] = [tk]
                    vtok[br] = copy(dve, VV[:, br, :], b2.ap[:, :], tk)
                    b2.free = [vtok[br]]
                pend[0] = g
            else:
                j = u % 2
                e1 = a_act(TMP[0:48, j, :], b.ap[0:48, :], ACT.Sigmoid, tok, tmp_free[j])
                b.free = [e1]

                def g():
                    b2 = bank()
                    for i in range(4):
                        tk = tr(b2.ap[:, 48 * i:48 * i + 48], TMP[0:48, j, 128 * i:128 * i + 128], e1,
                                cst["identf"], *(b2.free if i == 0 else ()), last=(i == 3))
                    tmp_free[j] = [tk]
                    cmpt["gate"] = copy(dve, GTS[:, :], b2.ap[:, 0:192], tk)
                    b2.free = [cmpt["gate"]]
                pend[0] = g

        GTS = sb("GTS", [128, 192])
        PE2 = sb("PE2", [128, 32])
        MCB = sb("MCB", [128, 128])
        CW2 = sb("CW2", [128, 2, 192])
        CTB = sb("CTB", [128, 124])
        KCZ = sb("KCZ", [128, 4, 32])
        VBK = sb("VBK", [128, 4, 128])
        cst["pe2"] = load(act, PE2[:, :], t["pe2"])
        cst["mcb"] = load(act, MCB[:, :], t["mcb"])
        cst["cw2"] = load(act, CW2[:, :, :], t["cw2"])
        cst["ctb"] = load(act, CTB[:, :], t["ctb"])
        kcz0 = dve.do(lambda e: e.memset(KCZ[:, :, :], 0.0))
        vbk0 = dve.do(lambda e: e.memset(VBK[:, :, :], 0.0))
        for u in range(15):
            dense("w_qkv", u, hx, 8, fin_qkv)
        flush()

        HID = TB[:, 1, 0:256]
        HT = TB[:, 1, 256:512].rearrange("p (c n) -> p c n", c=2)
        kct = []
        vct = []
        prev = []
        for kv in range(2):
            b = bank()
            Fp = (Fpk, Fpv)[kv]
            for c in range(4):
                n = get("w_c", kv * 4 + c)
                for q in range(4):
                    lp = 4 * c + q
                    tok = mm(b.ap[0:62, 0:256], Fp[:, lp * 62:lp * 62 + 62],
                             RAW[:, n % NRAW, q * 256:q * 256 + 256], lp == 0, lp == 15,
                             cmpt[kv], landed[n], *(b.free if lp == 0 else ()), last=(q == 3))
                used(n, tok)
            g1 = a_act(HID[0:62, :], b.ap[0:62, 0:256], ACT.Gelu_apprx_tanh, tok, scz2, prev)
            b.free = [g1]
            b = bank()
            for c in range(2):
                tok = tr(b.ap[:, 128 * c:128 * c + 62], HID[0:62, 128 * c:128 * c + 128], g1, b.free,
                         last=(c == 1))
            c1 = copy(dve, HT[:, :, 0:62], b.ap[:, 0:256].rearrange("p (c n) -> p c n", c=2)[:, :, 0:62],
                      tok, prev, scz2)
            b.free = [c1]
            b = bank()
            if kv == 0:
                for c in range(2):
                    tok = mm(b.ap[:, 0:62], CW2[:, c, 0:128], HT[:, c, 0:62], c == 0, c == 1, c1,
                             cst["cw2"], *(b.free if c == 0 else ()), last=(c == 1))
                prev = [tok]
                T0, T1 = TB[:, 1, 512:574], TB[:, 1, 576:638]
                e1 = copy(dve, T0, b.ap[:, 0:62], tok, scz2)
                b.free = [e1]
                b = bank()
                tok = mm(b.ap[:, 0:62], rotT[:, :], T0, True, True, e1, b.free, last=True)
                e2 = tt(dve, T1, b.ap[:, 0:62], CTB[:, 62:124], ALU.mult, tok, cst["ctb"], scz2)
                b.free = [e2]
                e3 = tt(dve, T0, T0, CTB[:, 0:62], ALU.mult, tok, e1)
                for g_ in range(2):
                    for p_ in range(2):
                        r0 = 64 * p_
                        kct.append(tt(dve, KCZ[r0:r0 + 64, 2 * g_ + p_, 0:31], T0[r0:r0 + 64, 31 * g_:31 * g_ + 31],
                                      T1[r0:r0 + 64, 31 * g_:31 * g_ + 31], ALU.add, e2, e3, kcz0))
            else:
                for g_ in range(2):
                    for c in range(2):
                        tok = mm(b.ap[0:31, 64 * g_:64 * g_ + 64], HT[:, c, 31 * g_:31 * g_ + 31],
                                 CW2[:, c, 128:192], c == 0, c == 1, c1, cst["cw2"],
                                 *(b.free if c == 0 and g_ == 0 else ()), last=(c == 1))
                for g_ in range(2):
                    for a in range(2):
                        for z in range(2):
                            r0 = 64 * a + 32 * z
                            vct.append(copy(dve, VBK[r0:r0 + 31, 2 * g_ + a, 64 * z:64 * z + 64],
                                            b.ap[0:31, 64 * g_:64 * g_ + 64], tok, vbk0))
                b.free = [vct[-1]]

        SCQ = [PB[:, 0, 0:512], PB[:, 0, 512:1024]]
        SCW = [PB[:, 1, 0:512], PB[:, 1, 512:1024]]
        SB_ = TB[:, 0, 0:64]
        pbw = [cmpt["f2free"], cmpt[0], cmpt[1], [pe.do(lambda e: e.matmul(banks[7].ap[0:32, 0:32], identb[:, 0:32], identb[:, 0:32], start=True, stop=True), cst["identb"], banks[7].free)]]
        gts = GTS[:, :].rearrange("p (i h b) -> p i h b", i=4, b=3)
        mcb = MCB[:, :].rearrange("p (i n) -> p i n", i=4)
        pct = []
        sf = [[], []]
        for Q in range(4):
            g_ = Q // 2
            b = bank()
            for a in range(2):
                for p_ in range(2):
                    j = 2 * a + p_
                    tok = mm(b.ap[32 * j:32 * j + 32, :], KCZ[:, 2 * g_ + p_, :], X[:, 2 * Q + a, :], True, True,
                             kct, qtok[2 * Q + a], b.free, last=(j == 3))
            A, W = SCQ[Q % 2], SCW[Q % 2]
            fr = sf[Q % 2]
            e1 = copy(act, A, b.ap[:, :], tok, pbw, fr)
            b.free = [e1]
            b = bank()
            for i in range(4):
                tok = tr(b.ap[:, 128 * i:128 * i + 128], A[:, 128 * i:128 * i + 128], e1, b.free, last=(i == 3))
            W4 = W.rearrange("p (i h n) -> p i h n", i=4, h=4)
            B4 = b.ap[:, :].rearrange("p (i h n) -> p i h n", i=4, h=4)
            for i in range(4):
                e2 = tt(dve, W4[:, i], B4[:, i], mcb[:, i, :].unsqueeze(1).broadcast_to([128, 4, 32]), ALU.add, tok,
                        cst["mcb"], pbw, fr)
            b.free = [e2]
            W3 = W.rearrange("p (x n) -> p x n", n=32)
            SM, SR = SB_[:, 0:16], SB_[:, 16:32]
            e3 = dve.do(lambda e, W3=W3: e.reduce_max(SM, W3, AX), e2)
            e4 = ts(dve, SM, SM, -1e29, ALU.max, e3)
            e5 = tt(dve, W3, W3, SM.unsqueeze(2).broadcast_to([128, 16, 32]), ALU.subtract, e4)
            e6 = a_act(W, W, ACT.Exp, e5)
            e7 = dve.do(lambda e, W3=W3: e.reduce_sum(SR, W3, AX), e6)
            e8 = ts(dve, SR, SR, 1e-30, ALU.max, e7)
            e9 = dve.do(lambda e: e.reciprocal(SR, SR), e8)
            e10 = tt(dve, SR.rearrange("p (i h) -> p i h", i=4), SR.rearrange("p (i h) -> p i h", i=4),
                     gts[:, :, 4 * Q:4 * Q + 4, 0], ALU.mult, e9, cmpt["gate"])
            e11 = tt(dve, W3, W3, SR.unsqueeze(2).broadcast_to([128, 16, 32]), ALU.mult, e10)
            b = bank()
            for i in range(4):
                tok = tr(b.ap[:, 128 * i:128 * i + 128], W[:, 128 * i:128 * i + 128], e11, b.free, last=(i == 3))
            c1 = copy(act, PC[:, Q, :], b.ap[:, :], tok, zx, cst["maskb"], cst["maskt"])
            b.free = [c1]
            sf[Q % 2] = [tok]
            pct.append(c1)
        cmpdone = sf[0] + sf[1] + [e11]

        SBK = [0, 1, 2, 3]
        TBK = [4, 5]
        OBK = [6, 7]
        stat = sb("stat", [128, 3, 2, 4])

        def attention(N, qtile, keys, kneed, score_add, weight, value, obank, ostart, odone, first_need):
            pfree, tfree = [first_need, first_need], [first_need, first_need]
            ptok, ttok = {}, {}
            sfree = [[], []]
            off = [0, 128, 384, 768]
            for n in range(N + 2):
                if n < N:
                    P_ = PB[:, n % 2, :]
                    mxs, sms, rcs = stat[:, 0, n % 2, :], stat[:, 1, n % 2, :], stat[:, 2, n % 2, :]
                    ex = []
                    adder = score_add(n) if score_add else None
                    for i in range(4):
                        b = banks[SBK[i]]
                        w = 128 * (i + 1)
                        mm(b.ap[:, 0:w], qtile(n, i), keys(n)[:, 0:w], True, False, kneed(n), b.free)
                        tok = mm(b.ap[:, w - 128:w], identb[:, :], maskb[:, :], False, True, cst["identb"],
                                 cst["maskb"], last=True)
                        pd = P_[:, off[i]:off[i] + w]
                        if adder is None:
                            m_ = dve.do(lambda e, b=b, w=w, o=mxs[:, i:i + 1]: e.tensor_reduce(
                                o, b.ap[:, 0:w], AX, ALU.max, negate=True), tok, sfree[n % 2])
                            x_ = act.do(lambda e, b=b, w=w, pd=pd, mx=mxs[:, i:i + 1], sm=sms[:, i:i + 1]:
                                        e.activation(pd, b.ap[:, 0:w], ACT.Exp, bias=mx, accum_out=sm),
                                        m_, tok, pfree[n % 2], sfree[n % 2])
                            b.free = [x_]
                        else:
                            ad, atok = adder[:2]
                            a_ = tt(dve, pd, b.ap[:, 0:w], ad[:, 0:w], ALU.add, tok, atok, pfree[n % 2])
                            b.free = [a_]
                            m_ = dve.do(lambda e, pd=pd, o=mxs[:, i:i + 1]: e.tensor_reduce(
                                o, pd, AX, ALU.max, negate=True), a_, sfree[n % 2])
                            x_ = act.do(lambda e, pd=pd, mx=mxs[:, i:i + 1], sm=sms[:, i:i + 1]:
                                        e.activation(pd, pd, ACT.Exp, bias=mx, accum_out=sm), m_, sfree[n % 2])
                            if i == 3:
                                adder[2](a_)
                        ex.append(x_)
                    r_ = dve.do(lambda e, o=rcs, i_=sms: e.reciprocal(o, i_), ex, sfree[n % 2])
                    if weight is not None:
                        wt, wtok = weight(n)
                        r_ = tt(dve, rcs, rcs, wt, ALU.mult, r_, wtok)
                    pt = []
                    for i in range(4):
                        w = 128 * (i + 1)
                        pd = P_[:, off[i]:off[i] + w]
                        pt.append(ts(dve, pd, pd, rcs[:, i:i + 1], ALU.mult, ex[i], r_))
                    ptok[n] = pt
                    sfree[n % 2] = [pt[-1]]
                if 1 <= n <= N:
                    m = n - 1
                    P_, T_ = PB[:, m % 2, :], TB[:, m % 2, :]
                    tks = []
                    for j in range(4):
                        b = banks[TBK[j % 2]]
                        for i in range(j, 4):
                            tok = tr(b.ap[:, 128 * (i - j):128 * (i - j) + 128],
                                     P_[:, off[i] + 128 * j:off[i] + 128 * j + 128], ptok[m][i], b.free,
                                     last=(i == 3))
                        c = (0, 512, 896, 1152)[j]
                        w = 512 - 128 * j
                        tks.append(copy(act, T_[:, c:c + w], b.ap[:, 0:w], tok, tfree[m % 2]))
                        b.free = [tks[-1]]
                    pfree[m % 2] = [tok]
                    ttok[m] = tks
                if n >= 2:
                    m = n - 2
                    T_ = TB[:, m % 2, :]
                    b, r0 = obank(m)
                    st_ = ostart(m, b)
                    for j in range(4):
                        c = (0, 512, 896, 1152)[j]
                        w = 512 - 128 * j
                        va, vt = value(m, j)
                        tok = mm(b.ap[r0:r0 + 64, 128 * j:512], va, T_[:, c:c + w], st_ and j == 0, False,
                                 ttok[m][j], vt, *(b.free if j == 0 else ()), last=(j == 3), shared=True)
                    tfree[m % 2] = [tok]
                    odone(m, b, tok)
            return pfree + tfree

        RAT = {}

        def nsa_start(m, b):
            if m % 4 == 0:
                pr = m // 4
                mm(b.ap[:, :], VBK[:, 2 * (pr // 4) + pr % 2, :], PC[:, pr // 2, :], True, False, vct,
                   pct[pr // 2], b.free, shared=True)
            return False

        def nsa_done(m, b, tok):
            if m % 4 == 3:
                RAT[m // 4] = list(split_to(RA, m // 4, b.ap[:, :], act, dve, [], tok))
                b.free = RAT[m // 4]

        ring[0] = 0
        adone = attention(
            32, lambda n, i: X[:, n // 4, 128 * i:128 * i + 128],
            lambda n: Kz[:, n % 2, n // 16, (n // 2) % 2, :],
            lambda n: [qtok[n // 4], ktok[(n % 2, n // 16, (n // 2) % 2)]], None,
            lambda n: (gts[:, :, n // 2, 1 + n % 2], cmpt["gate"]),
            lambda m, j: (VV[:, m % 2, 128 * j + 64 * (m // 16):128 * j + 64 * (m // 16) + 64], vtok[m % 2]),
            lambda m: (banks[OBK[(m // 4) % 2]], 64 * ((m // 2) % 2)), nsa_start, nsa_done, cmpdone)
        xt = [load(act, X[:, 2 * i:2 * i + 2, :], t["xT"][:, 2 * i:2 * i + 2, :], adone) for i in range(4)]
        xt = [xt[k // 2] for k in range(8)]
        if stop == "nsa":
            return finish_program(nc, ctx, locals())

        gb_bank = {}
        mtok = {}
        sg_free = [[], [], [], []]

        def gate_fin(store):
            def f(m, b, tok):
                j = m % 4
                g1 = a_act(TMP[:, j, :], b.ap[:, :], ACT.Sigmoid, tok, tmp_free[j], sg_free[j])
                b.free = [g1]
                store[m] = g1
            return f

        gt = {}

        def merge_fin(first, base_tok):
            def f(m, b, tok):
                j = m % 4
                if first:
                    o = tt(dve, M[:, m, :], TMP[:, j, :], b.ap[:, :], ALU.mult, tok, gt[m], base_tok)
                    mtok[m] = o
                else:
                    o1 = tt(dve, TMP[:, j, :], TMP[:, j, :], b.ap[:, :], ALU.mult, tok, gt[m])
                    o = tt(pool, M[:, m, :], M[:, m, :], TMP[:, j, :], ALU.add, o1, mtok[m])
                    mtok[m] = o
                    b.free = [o1]
                    tmp_free[j] = [o]
                    return
                b.free = [o]
                tmp_free[j] = [o]
            return f

        oa = (RA, 0, [RAT[k] for k in range(8)])
        for m in range(8):
            dense("w_gb", m, hx, 8, gate_fin(gt))
            if m % 2 == 1:
                dense("w_nsa", m - 1, oa, 8, merge_fin(True, adone))
                dense("w_nsa", m, oa, 8, merge_fin(True, adone))
        ra_free = [(pe.sem, pe.n)]

        UU = PB[:, 0, 0:512]
        UA = PB[:, 0, 512:1024]
        UB = PB[:, 1, 0:512]
        UC = PB[:, 1, 512:1024]
        WP = TB[:, 0, 0:512]
        ICT = TB[:, 1, 0:64]
        cst["wp"] = load(act, WP, t["w_pool"], adone)
        cst["ict"] = load(act, ICT, t["ict"], adone)
        ptk = {}
        pl = {"free": [], "y": {}}

        def fin_u(u, b, tok):
            flush()
            w = (2, 4, 8, 16)[u]
            e1 = copy(act, UU, b.ap[:, :], tok, adone, pl["free"])
            b.free = [e1]
            src, last = UU, e1
            sh, bufs, k = 1, [UA, UB], 0
            while sh < w:
                dst = bufs[k % 2]
                c_ = copy(dve, dst[:, 0:sh], src[:, 0:sh], last, adone, pl["free"])
                last = [tt(dve, dst[:, sh:], src[:, sh:], src[:, 0:512 - sh], ALU.add, last, c_), c_]
                src, sh, k = dst, sh * 2, k + 1
            m1 = tt(dve, src[:, 0:16], src[:, 0:16], ICT[:, 16 * u:16 * u + 16], ALU.mult, last, cst["ict"])
            m2 = ts(dve, src[:, 16:], src[:, 16:], 1.0 / w, ALU.mult, last)
            d = tt(dve, UC, src, UU, ALU.subtract, m1, m2, pl["free"])

            def g():
                b2 = bank()
                tk = mm(b2.ap[:, :], WP[:, 128 * u:128 * u + 128], UC, True, True, d, cst["wp"], b2.free,
                        last=True)
                y = a_act(UU, b2.ap[:, :], ACT.Copy, tk, d, scale=vecs[:, V_PS + u:V_PS + u + 1])
                b2.free = [y]
                hi, lo = split_to(RA, u, UU, act, dve, ra_free, y)
                pl["free"] = [hi, lo, tk]
                pl["y"][u] = [hi, lo]
            pend[0] = g

        for u in range(4):
            dense("w_u", u, hx, 8, fin_u)
        flush()
        ya = (RA, 0, [pl["y"][k] for k in range(4)])
        for m in range(8):
            dense("w_ga", m, hx, 8, gate_fin(gt))
            if m % 2 == 1:
                dense("w_pp", m // 2, ya, 4, merge_fin(False, None))
        h_free = [(pe.sem, pe.n)]
        H = [list(split_to(RH, k, M[:, k, :], act, pool if k % 2 else dve, h_free, mtok[k])) for k in range(8)]

        def residual(m, b, tok):
            o = tt(dve, X[:, m, :], X[:, m, :], b.ap[:, :], ALU.add, tok, xt[m])
            b.free = [o]
            xt[m] = o

        for m in range(8):
            dense("w_out", m, (RH, 0, H), 8, residual)
        h_free = [(pe.sem, pe.n)]
        H = normed(xt, lambda k: vecs[:, VG_MLP + k:VG_MLP + k + 1], None, h_free)
        hx = (RH, 0, H)
        if stop == "mix":
            return finish_program(nc, ctx, locals())

        CA = small[:, 8:16]
        cs = a_act(CA, vecs[:, V_C:V_C + 8], ACT.Sigmoid, cst["vecs"])
        cs = tt(dve, CA, CA, vecs[:, V_C:V_C + 8], ALU.mult, cs)
        MROW = PC[:, 0:3, :]
        adab = banks[7]
        ad = {"n": 0, "out": []}

        def ada_unit():
            u = ad["n"]
            if u >= 48:
                return
            ad["n"] += 1
            n = get("ada", u)
            J, k, half = u // 16, (u % 16) // 2, u % 2
            for c in range(2):
                cc = 2 * half + c
                tok = mm(adab.ap[32 * cc:32 * cc + 1, :], CA[:, k:k + 1], RAW[:, n % NRAW, 512 * c:512 * c + 512],
                         k == 0, k == 7, cs, landed[n], *(adab.free if k == 0 else ()), last=(c == 1), shared=True)
            used(n, tok)
            if u % 16 == 15:
                cps = []
                for cc in range(4):
                    cps.append(copy(dve, MROW[32 * cc:32 * cc + 1, J, :], adab.ap[32 * cc:32 * cc + 1, :], tok, adone,
                                    pct))
                adab.free = [cps[-1]]
                for cc in range(4):
                    ad["out"].append(load(act, t["mod"][4 * J + cc:4 * J + cc + 1, :], MROW[32 * cc:32 * cc + 1, J, :], cps[cc]))

        RB = list(range(7))
        a_free = [(pe.sem, pe.n)]
        tmpi = [0]
        for f in range(4):
            FT = {}

            def fin1(m, b, tok):
                i_ = tmpi[0] % 2
                tmpi[0] += 1
                r_ = a_act(TMP[:, i_, :], b.ap[:, :], ACT.Relu, tok, tmp_free[i_])
                v_ = tt(dve, TMP[:, 2 + i_, :], TMP[:, i_, :], b.ap[:, :], ALU.mult, r_, tmp_free[2 + i_])
                b.free = [v_]
                tmp_free[i_] = [v_]
                hi, lo = split_to(RA, m % 8, TMP[:, 2 + i_, :], act, pool if i_ else dve, a_free, v_)
                tmp_free[2 + i_] = [hi, lo]
                FT[m % 8] = [hi, lo]
            for m in range(8):
                dense("w_ff1", f * 8 + m, hx, 8, fin1, RB)
                ada_unit()
            fa_ = (RA, 0, [FT[k] for k in range(8)])
            for m in range(8):
                dense("w_ff2", f * 8 + m, fa_, 8, lambda mm_, b, tok: residual(mm_ % 8, b, tok), RB)
                if m % 2:
                    ada_unit()
            a_free = [(pe.sem, pe.n)]
        h_free = [(pe.sem, pe.n)]

        md = load(act, TMP[0:48, 0, 0:128], t["mod"].rearrange("a b -> (a b)").rearrange("(m p) -> m p", p=128),
                  ad["out"], tmp_free[0])
        b = bank()
        tok = tr(b.ap[:, 0:48], TMP[0:48, 0, 0:128], md, b.free, last=True)
        tmp_free[0] = [tok]
        ADB = RT[:, 512:560]
        cst["adab"] = load(act, ADB, t["adab"])
        md = tt(dve, modt[:, :], b.ap[:, 0:48], ADB, ALU.add, tok, cst["adab"])
        b.free = [md]
        g1s = stt(gsc[:, 0:8], modt[:, 8:16], small[:, 1:2], vecs[:, VG1:VG1 + 8], ALU.add, ALU.mult, md, one)
        g2s = stt(gsc[:, 8:16], modt[:, 32:40], small[:, 1:2], vecs[:, VG2:VG2 + 8], ALU.add, ALU.mult, md, one)

        r = rstd(xt, RST, *rst_free[0])
        for k in range(8):
            xt[k] = stt(X[:, k, :], X[:, k, :], vecs[:, VG_FIN + k:VG_FIN + k + 1], RST, ALU.mult, ALU.mult, r, xt[k])
        rst_free[0] = [xt[7]]
        if stop == "b1":
            return finish_program(nc, ctx, locals())
        dve.need(g1s, md)
        H = normed(xt, lambda k: gsc[:, k:k + 1], lambda k: modt[:, k:k + 1], h_free)
        hx = (RH, 0, H)
        kz2 = [dve.do(lambda e, i=i: e.memset(M[:, 4 * i:4 * i + 4, :], 0.0), h_free) for i in range(2)]

        QA = PC
        VA = [VV[:, 0, :], VV[:, 1, :], TAB[:, 0, :], TAB[:, 1, :]]
        pcfree = ad["out"]
        q2, k2, v2 = {}, {}, {}

        def fin_q(m, b, tok):
            q2[m] = a_act(QA[:, m, :], b.ap[:, :], ACT.Copy, tok, pcfree, scale=0.125)
            b.free = [q2[m]]

        def fin_z(kz_tok, scale, store):
            def f(m, b, tok):
                a1 = a_act(M[0:64, 2 * m, :], b.ap[0:64, :], ACT.Copy, tok, kz_tok, scale=scale)
                a2 = a_act(M[64:128, 2 * m + 1, :], b.ap[64:128, :], ACT.Copy, tok, kz_tok, scale=scale)
                b.free = [a2]
                store[2 * m], store[2 * m + 1] = a1, a2
            return f

        def fin_v(i, b, tok):
            v2[i] = copy(dve, VA[i], b.ap[:, :], tok, vfree)
            b.free = [v2[i]]

        vfree = [h_free]
        for u in range(4):
            dense("w2_qa", u, hx, 8, fin_q)
        FR = TMP
        nf = {}

        def fin_fa(u, b, tok):
            y = a_act(FR[0:8, 0, :], b.ap[0:8, :], ACT.Identity, tok, tmp_free[0], cst["vecs"],
                      bias=vecs[0:8, V_BF:V_BF + 1])
            b.free = [y]
            ab = a_act(FR[0:8, 1, :], FR[0:8, 0, :], ACT.Abs, y, tmp_free[1])
            ex = a_act(FR[0:8, 1, :], FR[0:8, 1, :], ACT.Exp, ab, scale=-1.0)
            ln = a_act(FR[0:8, 1, :], FR[0:8, 1, :], ACT.Ln, ex, one, bias=small[0:8, 1:2])
            nm = ts(dve, FR[0:8, 0, :], FR[0:8, 0, :], -1.0, ALU.mult, ab, s2=0.0, op1=ALU.max)
            sm_ = tt(dve, FR[0:8, 2, :], FR[0:8, 0, :], FR[0:8, 1, :], ALU.add, nm, ln, tmp_free[2])
            z_ = dve.do(lambda e: e.memset(FR[0:8, 0, :], 0.0), sm_)
            sc = dve.do(lambda e: e.tensor_tensor_scan(FR[0:8, 3, :], FR[0:8, 2, :], FR[0:8, 0, :], 0.0,
                                                       ALU.add, ALU.add), sm_, z_, tmp_free[3])
            nf["d"] = load(act, t["nf"], FR[0:8, 3, :], sc)
            for i in range(4):
                tmp_free[i] = [sc, nf["d"]]
        dense("w2_fa", 0, hx, 8, fin_fa)
        for u in range(4):
            dense("w2_ka", u, hx, 8, fin_z(kz2, 1.0, k2))
        dense_rows("w2_va", 4, hx, fin_v, [0, 1, 2, 3])

        FB = [TMP[:, 0, :], TMP[:, 1, :]]
        fbl = {}
        fbfree = {0: [], 1: []}

        def fb_load(n):
            fbl[n] = load(sp, FB[n % 2], t["nf"][n:n + 1, :].broadcast_to([128, 512]), nf["d"], tmp_free[n % 2],
                          fbfree[n % 2])

        fb_load(0)

        def fox_add(n):
            def done(tok):
                fbfree[n % 2] = [tok]
            if n + 1 < 8:
                fb_load(n + 1)
            return FB[n % 2], fbl[n], done

        def fox_done(m, b, tok):
            if m % 2 == 1:
                RAT[m // 2] = list(split_to(RA, m // 2, b.ap[:, :], act, dve, a_free, tok))
                b.free = RAT[m // 2]

        adone2 = attention(
            8, lambda n, i: QA[:, n // 2, 128 * i:128 * i + 128],
            lambda n: M[:, n, :], lambda n: [q2[n // 2], k2[n]], fox_add, None,
            lambda m, j: (VA[j][:, 64 * m:64 * m + 64], v2[j]),
            lambda m: (banks[OBK[(m // 2) % 2]], 64 * (m % 2)), lambda m, b: True, fox_done, [h_free])
        for i in range(2):
            tmp_free[i] = [tmp_free[i], fbfree[i]]
        if stop == "fox":
            return finish_program(nc, ctx, locals())

        pcfree = adone2
        vfree = adone2
        KB = PC
        kb2, qz2 = {}, {}

        def fin_kb(m, b, tok):
            kb2[m] = a_act(KB[:, m, :], b.ap[:, :], ACT.Copy, tok, adone2)
            b.free = [kb2[m]]
        for u in range(4):
            dense("w2_qb", u, hx, 8, fin_z(adone2, 0.125, qz2))
        for u in range(4):
            dense("w2_kb", u, hx, 8, fin_kb)
        dense_rows("w2_vb", 4, hx, fin_v, [0, 1, 2, 3])

        sets = [[0, 1, 2], [3, 4, 5]]
        place = [(0, 0), (1, 0), (2, 0), (1, 384)]
        zsp, zst = {}, {}
        spf, taf = [adone2, adone2], [adone2, adone2]
        segs = [(0, 0, 512), (1, 512, 512), (2, 1024, 256)]
        for n in range(9):
            if n < 8:
                h, pr = n, n // 2
                bs = [banks[i] for i in sets[n % 2]]
                SPt, TAt = PB[:, n % 2, :], TB[:, n % 2, :]
                for j in (0, 1, 3, 2):
                    bi, o = place[j]
                    w = 512 - 128 * j
                    tok = mm(bs[bi].ap[:, o:o + w], KB[:, pr, 128 * j:128 * j + 128], M[:, h, 128 * j:512],
                             o == 0, False, kb2[pr], qz2[h], *(bs[bi].free if o == 0 else ()), last=True,
                             shared=True)
                ab = []
                for bi, o, w in segs:
                    ab.append(a_act(TAt[:, o:o + w], bs[bi].ap[:, 0:w], ACT.Abs, tok, taf[n % 2]))
                ex = a_act(TAt, TAt, ACT.Exp, ab, scale=-1.0)
                ln = a_act(TAt, TAt, ACT.Ln, ex, one, bias=small[:, 1:2])
                sps = []
                for bi, o, w in segs:
                    sps.append(stt(SPt[:, o:o + w], bs[bi].ap[:, 0:w], 0.0, TAt[:, o:o + w], ALU.max, ALU.add,
                                   ln, tok, spf[n % 2]))
                mk = []
                for j in range(4):
                    o = PACK[j]
                    mk.append(tt(pool, SPt[:, o:o + 128], SPt[:, o:o + 128], sltm[:, :], ALU.mult, sps,
                                 cst["sltm"]))
                zsp[n], zst[n] = (sps, mk), bs
            if n >= 1:
                m = n - 1
                bs = zst[m]
                SPt, TAt = PB[:, m % 2, :], TB[:, m % 2, :]
                sps, mk = zsp[m]
                for j in range(4):
                    bi, o = place[j]
                    w = 512 - 128 * j
                    mm(bs[bi].ap[:, o:o + w], ntri[:, :], SPt[:, PACK[j]:PACK[j] + w], False, False, mk, sps,
                       cst["ntri"], cst["nones"], shared=True)
                    for jj in range(j + 1, 4):
                        w2 = 512 - 128 * jj
                        mm(bs[bi].ap[:, o + 128 * (jj - j):o + w], nones[:, :], SPt[:, PACK[jj]:PACK[jj] + w2],
                           False, False, shared=True)
                    tok = mm(bs[bi].ap[:, o:o + 128], identb[:, :], maskt[:, :], False, True, cst["maskt"],
                             last=True, shared=True)
                spf[m % 2] = [tok]
                av = []
                for bi, o, w in segs:
                    av.append(a_act(TAt[:, o:o + w], bs[bi].ap[:, 0:w], ACT.Exp, tok))
                    bs[bi].free = [av[-1]]
                b = banks[OBK[(m // 2) % 2]]
                r0 = 64 * (m % 2)
                for j in range(4):
                    tok = mm(b.ap[r0:r0 + 64, 128 * j:512], VA[j][:, 64 * m:64 * m + 64],
                             TAt[:, PACK[j]:PACK[j] + 512 - 128 * j], j == 0, False, av, v2[j],
                             *(b.free if j == 0 else ()), last=(j == 3), shared=True)
                taf[m % 2] = [tok]
                if m % 2 == 1:
                    k = 4 + m // 2
                    RAT[k] = list(split_to(RA, k, b.ap[:, :], act, dve, a_free, tok))
                    b.free = RAT[k]
        sdone = spf + taf + [(act.sem, act.n), (dve.sem, dve.n)]
        if stop == "sb":
            return finish_program(nc, ctx, locals())

        fo, so = (RA, 0, [RAT[k] for k in range(4)]), (RA, 4, [RAT[4 + k] for k in range(4)])
        for m in range(0, 8, 2):
            dense("w2_ga", m, hx, 8, gate_fin(gt))
            dense("w2_ga", m + 1, hx, 8, gate_fin(gt))
            dense("w2_fox", m // 2, fo, 4, merge_fin(True, sdone))
            dense("w2_gb", m, hx, 8, gate_fin(gt))
            dense("w2_gb", m + 1, hx, 8, gate_fin(gt))
            dense("w2_sb", m // 2, so, 4, merge_fin(False, None))
        h_free = [(pe.sem, pe.n)]
        H = [list(split_to(RH, k, M[:, k, :], act, pool if k % 2 else dve, h_free, mtok[k])) for k in range(8)]

        def residual2(m, b, tok):
            o = stt(X[:, m, :], b.ap[:, :], modt[:, 16 + m:17 + m], X[:, m, :], ALU.mult, ALU.add, tok, xt[m], md)
            b.free = [o]
            xt[m] = o
        for m in range(8):
            dense("w2_out", m, (RH, 0, H), 8, residual2)
        if stop == "mix2":
            return finish_program(nc, ctx, locals())

        r = rstd(xt, RST, *rst_free[0])
        ht = []
        for k in range(8):
            w = stt(M[:, k, :], X[:, k, :], gsc[:, 8 + k:9 + k], RST, ALU.mult, ALU.mult, r, xt[k], g2s, H[k])
            ht.append(ts(dve, M[:, k, :], M[:, k, :], modt[:, 24 + k:25 + k], ALU.add, w, md))
        RW = TAB[:, 0, 0:160]
        cst["rw"] = load(act, RW, t["rw"], sdone)
        b = bank()
        for k in range(8):
            tok = mm(b.ap[0:20, :], RW[:, 20 * k:20 * k + 20], M[:, k, :], k == 0, k == 7, ht[k], cst["rw"], b.free,
                     last=(k == 7))
        LT = TMP[0:20, 0, :]
        l1 = a_act(LT, b.ap[0:20, :], ACT.Identity, tok, tmp_free[0], bias=vecs[0:20, V_BF + 1:V_BF + 2])
        b.free = [l1]
        b = bank()
        for i in range(4):
            tok = tr(b.ap[:, 20 * i:20 * i + 20], TMP[0:20, 0, 128 * i:128 * i + 128], l1, b.free, last=(i == 3))
        XT_ = [VV, TAB]
        pos_rows = []
        vt_free = {0: [sdone], 1: [sdone, cst["rw"], tok]}
        HT4 = {}

        def rows_of(i):
            bb = [banks[2 * (i % 2) + 4 * 0], banks[2 * (i % 2) + 1]]
            dst = (PB, TB)[i // 2][:, i % 2, 0:1024]
            cps = []
            for hf in range(2):
                for k in range(4):
                    tk = tr(bb[hf].ap[:, 128 * k:128 * k + 128], M[:, 4 * hf + k, 128 * i:128 * i + 128],
                            ht[4 * hf + k], bb[hf].free, last=(k == 3))
                c = copy(act if hf else dve, dst[:, 512 * hf:512 * hf + 512], bb[hf].ap[:, :], tk, sdone)
                bb[hf].free = [c]
                cps.append(c)
            return dst, cps
        LG = RT[:, 560:640]
        LG3 = LG.rearrange("p (i n) -> p i n", n=20)
        c0 = copy(dve, LG, b.ap[:, 0:80], tok)
        b.free = [c0]
        hrows = [rows_of(i) for i in range(4)]

        R_ = TMP[:, 1:4, :].rearrange("p a n -> p (a n)")
        ro = [0]

        def reg(n):
            a = R_[:, ro[0]:ro[0] + n]
            ro[0] += n
            return a
        w0 = [tmp_free[1], tmp_free[2], tmp_free[3]]
        dve.need(w0)
        last = [c0]

        def v(fn):
            last[0] = dve.do(fn, last[0])
            return last[0]

        def vtt(o, a, b_, op):
            return v(lambda e: e.tensor_tensor(o, a, b_, op))

        W4_ = RW4 = VV[:, 0, 0:64]
        cst["rk"] = load(act, VV[:, 0, 0:64], t["rk"], sdone)
        dve.need(cst["rk"])
        RK4 = VV[:, 0, 0:16].rearrange("p (i n) -> p i n", n=4)
        E128 = VV[:, 0, 16:32]
        JJ = VV[:, 0, 32:39]

        def b3(a, n):
            return a.unsqueeze(2).broadcast_to([128, 4, n])

        def first_max(src, n):
            mx, oh, m2 = reg(4), reg(16), reg(4)
            oh3 = oh.rearrange("p (i n) -> p i n", n=4)
            v(lambda e: e.reduce_max(mx, src, AX))
            vtt(oh3, src, b3(mx, 4), ALU.is_equal)
            vtt(oh3, oh3, RK4, ALU.mult)
            v(lambda e: e.reduce_max(m2, oh3, AX))
            vtt(oh3, oh3, b3(m2, 4), ALU.is_equal)
            return mx, oh3
        G3, E3 = LG3[:, :, 0:4], LG3[:, :, 4:20]
        gm, gh = first_max(G3, 4)
        gx = reg(16).rearrange("p (i n) -> p i n", n=4)
        gs = reg(4)
        vtt(gx, G3, b3(gm, 4), ALU.subtract)
        last[0] = a_act(gx, gx, ACT.Exp, last[0])
        v(lambda e: e.reduce_sum(gs, gx, AX))
        v(lambda e: e.reciprocal(gs, gs))
        em = reg(64)
        es = reg(16).rearrange("p (i n) -> p i n", n=4)
        for i in range(4):
            e4 = em[:, 16 * i:16 * i + 16].rearrange("p (g e) -> p g e", g=4)
            vtt(e4, E3[:, i, :].rearrange("p (g e) -> p g e", g=4), gh[:, i, :].unsqueeze(2).broadcast_to([128, 4, 4]),
                ALU.mult)
            v(lambda e, o=es[:, i, :], e4=e4: e.reduce_sum(o, e4.rearrange("p g e -> p e g"), AX))
        m1, o1 = first_max(es, 4)
        e2_ = reg(16).rearrange("p (i n) -> p i n", n=4)
        v(lambda e: e.scalar_tensor_tensor(e2_, o1, NEG, es, ALU.mult, ALU.add))
        m2, o2 = first_max(e2_, 4)
        ex = reg(16).rearrange("p (i n) -> p i n", n=4)
        vtt(ex, es, b3(m1, 4), ALU.subtract)
        last[0] = a_act(ex, ex, ACT.Exp, last[0])
        zs = reg(4)
        v(lambda e: e.reduce_sum(zs, ex, AX))
        v(lambda e: e.reciprocal(zs, zs))
        vtt(ex, ex, b3(zs, 4), ALU.mult)
        pk = reg(8).rearrange("p (k i) -> p k i", k=2)
        px = reg(16).rearrange("p (i n) -> p i n", n=4)
        for kk, oo in enumerate((o1, o2)):
            vtt(px, ex, oo, ALU.mult)
            v(lambda e, o=pk[:, kk, :]: e.reduce_sum(o, px, AX))
        ps_ = reg(4)
        vtt(ps_, pk[:, 0, :], pk[:, 1, :], ALU.add)
        v(lambda e: e.reciprocal(ps_, ps_))
        vtt(ps_, ps_, gs, ALU.mult)
        WK = RT[:, 640:648].rearrange("p (k i) -> p k i", k=2)
        for kk in range(2):
            vtt(WK[:, kk, :], pk[:, kk, :], ps_, ALU.mult)
        wk_tok = last[0]
        OE = [reg(64), reg(64)]
        for kk, oo in enumerate((o1, o2)):
            for i in range(4):
                d4 = OE[kk][:, 16 * i:16 * i + 16].rearrange("p (g e) -> p g e", g=4)
                vtt(d4, gh[:, i, :].unsqueeze(2).broadcast_to([128, 4, 4]),
                    oo[:, i, :].unsqueeze(1).broadcast_to([128, 4, 4]), ALU.mult)
        MB = sb("MB", [128, 80], BF16)
        vtt(MB[:, 0:64], OE[0], OE[1], ALU.add)
        b = bank(list(range(4, 8)))
        mbt = last[0]
        for i in range(4):
            for ii in range(i + 1):
                mm(b.ap[:, 16 * i:16 * i + 16], trib[:, :] if ii == i else onesb[:, :],
                   MB[:, 16 * ii:16 * ii + 16], ii == 0 and i == 0, False, mbt, cst["trib"], cst["onesb"], b.free,
                   shared=True)
        for ii in range(4):
            tok = mm(b.ap[:, 64:80], onesb[:, :], MB[:, 16 * ii:16 * ii + 16], False, ii == 3, last=(ii == 3),
                     shared=True)
        rank = reg(80)
        last[0] = copy(dve, rank, b.ap[:, 0:80], tok)
        b.free = [last[0]]
        NE = rank[:, 64:80]
        xe, xa, xi = reg(16), reg(16), reg(16)
        v(lambda e: e.tensor_scalar(xe, NE, 128.5, None, ALU.is_gt))
        for lim in (256.5, 384.5):
            v(lambda e, lim=lim: e.scalar_tensor_tensor(xe, NE, lim, xe, ALU.is_gt, ALU.add))
        v(lambda e: e.memset(xa, 0.0))
        v(lambda e: e.tensor_tensor_scan(xi, xe, xa, 0.0, ALU.add, ALU.add))
        EXI = sb("EXI", [1, 8], I32)
        ej, cj = reg(8), reg(16)
        for j in range(7):
            v(lambda e, j=j: e.tensor_scalar(cj[0:1, :], xi[0:1, :], j + 0.5, None, ALU.is_lt))
            v(lambda e, j=j: e.reduce_sum(ej[0:1, j:j + 1], cj[0:1, :], AX))
        v(lambda e: e.tensor_scalar(ej[0:1, 0:7], ej[0:1, 0:7], 15.0, None, ALU.min))
        late["tok"] = v(lambda e: e.tensor_copy(EXI[0:1, 0:7], ej[0:1, 0:7]))
        base = reg(16)
        vtt(base, xi, xe, ALU.subtract)
        v(lambda e: e.tensor_scalar(base, base, 128.0, 1920.0, ALU.mult, ALU.add))
        vtt(base, base, E128, ALU.subtract)
        vl = reg(64)
        POSF = reg(8)
        for i in range(4):
            ri, vi = rank[:, 16 * i:16 * i + 16], vl[:, 16 * i:16 * i + 16]
            v(lambda e, ri=ri, vi=vi: e.scalar_tensor_tensor(vi, ri, 127.5, base, ALU.is_gt, ALU.mult))
            vtt(vi, vi, ri, ALU.add)
            vtt(vi, vi, E128, ALU.add)
        for kk in range(2):
            vtt(OE[kk], OE[kk], vl, ALU.mult)
            v(lambda e, kk=kk: e.reduce_sum(POSF[:, 4 * kk:4 * kk + 4], OE[kk].rearrange("p (i n) -> p i n", n=16), AX))
        POS = sb("POS", [128, 8], U32)
        pos_t = v(lambda e: e.tensor_copy(POS[:, :], POSF))
        sct = []
        for i in range(4):
            for kk in range(2):
                counter[0] += 1
                s = sem(f"d{counter[0]}")
                c = 4 * kk + i
                sct.append(pool.dma(lambda e, c=c, i=i: e.indirect_dma_start(
                    t["xs"], bass.IndirectOffsetOnAxis(ap=POS[:, c:c + 1], axis=0), hrows[i][0], None),
                    s, 16, pos_t, hrows[i][1], zx))
        G2B, GFB = TB[:, 0, 0:1024], TB[:, 1, 0:1024]
        if stop == "route":
            return finish_program(nc, ctx, locals())

        lo_engine[0] = lambda n: pool if n % 3 == 2 else dve
        xin = [PB[:, 0, 0:1024], PB[:, 1, 0:1024]]
        yout = [TB[:, 0, 0:1024], TB[:, 1, 0:1024]]
        xin_f, yout_f = [sct, sct], [sct, sct]
        XH = [RH[:, :, 0:2, :], RH[:, :, 2:4, :]]
        AH = [RH[:, :, 4, :], RH[:, :, 5, :]]
        hfree = [(pe.sem, pe.n)]
        xh_f, ah_f = [hfree, hfree], [hfree, hfree]
        GU = [PC[:, 0, :], PC[:, 1, :]]
        gu_f = [sdone, sdone]
        xl, xht, aht, yst = {}, {}, {}, []

        def load_x(u):
            xl[u] = load(act, xin[u % 2], t["xs"][128 * u:128 * u + 128, :], sct, xin_f[u % 2])

        def prep(u):
            tk = []
            for hf in range(2):
                b = banks[hf]
                for k in range(4):
                    c = (4 * hf + k) * 128
                    tok = tr(b.ap[:, 128 * k:128 * k + 128], xin[u % 2][:, c:c + 128], xl[u], b.free, last=(k == 3))
                d = XH[u % 2]
                hi = copy(act, d[:, 0, hf, :], b.ap[:, :], tok, xh_f[u % 2])
                lo = tt(dve, d[:, 1, hf, :], b.ap[:, :], hiF(d[:, 0, hf, :]), ALU.subtract, hi, xh_f[u % 2])
                b.free = [lo]
                tk.append([hi, lo])
            xin_f[u % 2] = [tok]
            xht[u] = tk

        def up(u, name, b):
            d = XH[u % 2]
            for c in range(4):
                n = get(name, (u, c))
                s, lo_t, hi_t = parts[n]
                for kk in range(2):
                    k = 2 * c + kk
                    xh, xlo = (d[:, x, k // 4, 128 * (k % 4):128 * (k % 4) + 128] for x in (0, 1))
                    wh, wl = (RS[:, s, x, 512 * kk:512 * kk + 512] for x in (0, 1))
                    mm(b.ap[:, :], xh, wh, k == 0, False, hi_t, xht[u][k // 4], *(b.free if k == 0 else ()))
                    mm(b.ap[:, :], xlo, wh, False, False)
                    tok = mm(b.ap[:, :], xh, wl, False, k == 7, lo_t, last=(kk == 1))
                used(n, tok)
            return tok

        def down(u):
            bb = [banks[5], banks[6]]
            d = AH[u % 2]
            for c in range(4):
                n = get("w_down", (u, c))
                s, lo_t, hi_t = parts[n]
                for hf in range(2):
                    b = bb[hf]
                    xh, xlo = (d[:, x, 128 * c:128 * c + 128] for x in (0, 1))
                    wh, wl = (RS[:, s, x, 512 * hf:512 * hf + 512] for x in (0, 1))
                    mm(b.ap[:, :], xh, wh, c == 0, False, hi_t, aht[u], *(b.free if c == 0 else ()))
                    mm(b.ap[:, :], xlo, wh, False, False)
                    tok = mm(b.ap[:, :], xh, wl, False, c == 3, lo_t, last=True)
                    if c == 3:
                        cp = copy(act if hf else dve, yout[u % 2][:, 512 * hf:512 * hf + 512], b.ap[:, :], tok,
                                  yout_f[u % 2])
                        b.free = [cp]
                        cps.append(cp)
                used(n, tok)
            ah_f[u % 2] = [tok]
            yst.append(load(act, t["ys"][128 * u:128 * u + 128, :], yout[u % 2], cps[-2:]))
            yout_f[u % 2] = [yst[-1]]

        cps = []
        load_x(0)
        load_x(1)
        prep(0)
        for u in range(NUNIT):
            tg = up(u, "w_gate", banks[2])
            G_ = GU[u % 2]
            s1 = a_act(G_, banks[2].ap[:, :], ACT.Silu, tg, gu_f[u % 2])
            banks[2].free = [s1]
            if u + 1 < NUNIT:
                prep(u + 1)
            tu = up(u, "w_up", banks[3])
            xh_f[u % 2] = [tu]
            s2 = tt(dve, G_, G_, banks[3].ap[:, :], ALU.mult, s1, tu)
            banks[3].free = [s2]
            if u + 2 < NUNIT:
                load_x(u + 2)
            if u:
                down(u - 1)
            b = banks[4]
            for k in range(4):
                tok = tr(b.ap[:, 128 * k:128 * k + 128], G_[:, 128 * k:128 * k + 128], s2, b.free, last=(k == 3))
            gu_f[u % 2] = [tok]
            hi = copy(act, AH[u % 2][:, 0, :], b.ap[:, :], tok, ah_f[u % 2])
            lo = tt(dve, AH[u % 2][:, 1, :], b.ap[:, :], hiF(AH[u % 2][:, 0, :]), ALU.subtract, hi, ah_f[u % 2])
            b.free = [lo]
            aht[u] = [hi, lo]
        down(NUNIT - 1)

        g2r = load(act, M[:, 0:2, :], t["mod"][10:12, :].rearrange("a b -> (a b)").rearrange("(o a b) -> o a b", o=1, a=2)
                   .broadcast_to([128, 2, 512]), ht, [h[1] for h in hrows])
        g2b = load(act, M[:, 2:4, :], t["g2b"].rearrange("(o a b) -> o a b", o=1, a=2).broadcast_to([128, 2, 512]), ht)
        gfb = load(act, M[:, 4:6, :], t["final_g"].rearrange("(o a b) -> o a b", o=1, a=2).broadcast_to([128, 2, 512]), ht)
        g2 = tt(dve, M[:, 0:2, :], M[:, 0:2, :], M[:, 2:4, :], ALU.add, g2r, g2b)
        G2 = M[:, 0:2, :].rearrange("p a b -> p (a b)")
        GF = M[:, 4:6, :].rearrange("p a b -> p (a b)")
        outs = []
        ybuf = [[PC[:, 0:2, :], PC[:, 2:4, :]], [TMP[:, 0:2, :], TMP[:, 2:4, :]]]
        zb = [VV, TAB]
        yall = [yst, gu_f, [(act.sem, act.n), (dve.sem, dve.n), (pe.sem, pe.n)]]
        yf = [yall, yall]
        for i in range(4):
            ya_ = []
            bufs = [x.rearrange("p a b -> p (a b)") for x in ybuf[i % 2]]
            for kk in range(2):
                counter[0] += 1
                s = sem(f"d{counter[0]}")
                c = 4 * kk + i
                ya_.append(pool.dma(lambda e, c=c, d=bufs[kk]: e.indirect_dma_start(
                    d, None, t["ys"], bass.IndirectOffsetOnAxis(ap=POS[:, c:c + 1], axis=0)), s, 16, yf[i % 2]))
            bb = [banks[2 * (i % 2)], banks[2 * (i % 2) + 1]]
            for hf in range(2):
                for k in range(4):
                    tk = tr(bb[hf].ap[:, 128 * k:128 * k + 128], X[:, 4 * hf + k, 128 * i:128 * i + 128],
                            xt[4 * hf + k], bb[hf].free, last=(k == 3))
            A_, B_ = bufs
            y1 = ts(dve, A_, A_, WK[:, 0, i:i + 1], ALU.mult, ya_[0])
            y2 = stt(A_, B_, WK[:, 1, i:i + 1], A_, ALU.mult, ALU.add, y1, ya_[1])
            y3 = tt(dve, A_, A_, G2, ALU.mult, y2, g2)
            y4 = []
            for hf in range(2):
                y4.append(tt(dve, A_[:, 512 * hf:512 * hf + 512], A_[:, 512 * hf:512 * hf + 512], bb[hf].ap[:, :],
                             ALU.add, y3, tk))
                bb[hf].free = [y4[-1]]
            ss = stat[:, 0, i % 2, 0:1]
            q1 = a_act(B_, A_, ACT.Square, y4, accum_out=ss)
            q2_ = a_act(ss, ss, ACT.Sqrt, q1, bias=small[:, 0:1], scale=1.0 / D)
            q3 = dve.do(lambda e, ss=ss: e.reciprocal(ss, ss), q2_)
            q4 = stt(B_, A_, ss, GF, ALU.mult, ALU.mult, q3, gfb)
            o_ = load(act, t["out"][0, 128 * i:128 * i + 128, :], B_, q4)
            outs.append(o_)
            yf[i % 2] = [o_]
        sp.need(outs, yst, every)
        return finish_program(nc, ctx, locals())


def finish_program(nc, ctx, env):
    sp, pe, act, dve, pool = (env[n] for n in ("sp", "pe", "act", "dve", "pool"))
    if env["stop"] is not None:
        for q in (pe, act, dve, pool):
            sp.need((q.sem, q.n))
        sp.need(env["every"])
        sp.need([(x, 16 * ((env["st"]["load"] - i + 4) // 5)) for i, x in enumerate(env["raw_sem"])])
        if "sct" in env:
            sp.need(env["sct"])
        fin = ctx.enter_context(nc.semaphore("s_fin"))
        o = env["t"]["out"][0, 0:128, 0:128]
        sp.dma(lambda e: e.dma_start(o, env["identf"][:, :]), fin, 16)
        sp.need((fin, 16))
    block = ctx.enter_context(nc.Block())
    for q, name in ((sp, "sync"), (pe, "tensor"), (act, "scalar"), (dve, "vector"), (pool, "gpsimd")):
        def body(eng, q=q):
            for kind, a, b in q.items:
                if kind == "wait":
                    eng.wait_ge(a, b)
                elif kind == "call":
                    a(eng)
                else:
                    ins = a(eng)
                    if b is not None:
                        ins.then_inc(b[0], b[1])
        {"sync": block.sync, "tensor": block.tensor, "scalar": block.scalar, "vector": block.vector,
         "gpsimd": block.gpsimd}[name](body)


def tiles(w, pad=0):
    w = np.asarray(w)
    if pad:
        w = np.concatenate([w, np.zeros((w.shape[0], pad), w.dtype)], axis=1)
    K, N = w.shape[0] // 128, w.shape[1] // 128
    per = 8 // K
    a = w.reshape(K, 128, N // per, per, 128).transpose(2, 1, 3, 0, 4)
    return np.ascontiguousarray(a).reshape(N // per, 128, 1024)


def rows(w):
    w = np.asarray(w)
    K = w.shape[0] // 256
    return np.ascontiguousarray(w.reshape(K, 2, 128, 512).transpose(0, 2, 1, 3)).reshape(K, 128, 1024)


def cols(v, n):
    return np.asarray(v).reshape(n, 128).T


def constants():
    f = np.float32
    c = {}
    c["identf"] = np.eye(128, dtype=f)
    r = np.zeros((128, 128), f)
    for b in range(2):
        for d in range(64):
            if d < 32:
                r[64 * b + d + 32, 64 * b + d] = -1
            else:
                r[64 * b + d - 32, 64 * b + d] = 1
    c["rotT"] = r
    c["onesf"] = np.ones((128, 128), f)
    i, j = np.arange(128)[:, None], np.arange(128)[None, :]
    c["ntri"] = -(i >= j).astype(f)
    c["nones"] = -np.ones((128, 128), f)
    c["sltm"] = (i < j).astype(f)
    c["maskb"] = np.where(j > i, NEG, 0.0).astype(f)
    c["maskt"] = np.where(i >= j, NEG, 0.0).astype(f)
    inv = np.power(f(10000.0), -np.arange(0, 64, 2, dtype=f) / f(64)).astype(f)

    def table(pos):
        ang = (pos.astype(f)[:, None] * inv[None, :]).astype(f)
        ang = np.concatenate([ang, ang], axis=-1)
        return np.cos(ang).T.astype(f), np.sin(ang).T.astype(f)
    co, si = table(np.arange(S))
    c["tab"] = np.stack([np.concatenate([co, co]), np.concatenate([si, si])], axis=1)
    co, si = table(np.arange(CMP) * 16 + 31)
    c["ctb"] = np.concatenate([np.tile(co, (2, 2)), np.tile(si, (2, 2))], axis=1)
    tt_ = np.arange(S).reshape(4, 128).T[:, :, None]
    n = np.arange(32)[None, None, :]
    c["mcb"] = np.where((16 * n + 31 > tt_) | (n == 31), NEG, 0.0).astype(f).reshape(128, 128)
    c["ict"] = np.tile(np.concatenate([1.0 / np.minimum(np.arange(16) + 1, w) for w in (2, 4, 8, 16)]).astype(f), (128, 1))
    rk = np.zeros((128, 64), f)
    rk[:, 0:16] = np.tile(np.array([4, 3, 2, 1], f), 4)
    rk[:, 16:32] = 128 * np.arange(16)
    c["rk"] = rk
    return c


def layout(i):
    a = {}
    a["xT"] = np.ascontiguousarray(np.asarray(i["x"])[0].T.reshape(8, 128, S).transpose(1, 0, 2))
    w = np.asarray(i["w_in"])[0]
    u, q, kc, vc, ks, vs, kw, vw, g, gm = np.split(w, np.cumsum([512, 1024, 128, 128, 128, 128, 128, 128, 48]), axis=1)
    a["w_qkv"] = tiles(np.concatenate([q, ks, kw, kc, vc, vs, vw, g], axis=1), pad=80)
    ck = [np.asarray(i[n])[0].reshape(4, 4, 128, 256).transpose(0, 2, 1, 3).reshape(4, 128, 1024)
          for n in ("w_ck1", "w_cv1")]
    a["w_c"] = np.concatenate(ck)
    c2 = np.asarray(i["w_ck2"])[0].reshape(2, 128, 64).transpose(1, 0, 2)
    v2 = np.asarray(i["w_cv2"])[0].reshape(2, 128, 64).transpose(1, 0, 2)
    a["cw2"] = np.concatenate([c2, c2, v2], axis=2)
    a["pe2"] = np.concatenate([np.asarray(i[n])[0].reshape(16, 128).T for n in ("pe_k", "pe_v")], axis=1)
    a["w_ga"], a["w_gb"] = tiles(gm[:, :1024]), tiles(gm[:, 1024:])
    a["w_nsa"] = tiles(i["w_proj_nsa"][0])
    a["w_u"] = tiles(u)
    a["w_pool"] = np.ascontiguousarray(np.asarray(i["w_pool"])[0].transpose(1, 0, 2).reshape(128, 512))
    a["w_pp"] = tiles(i["w_proj_pool"][0])
    a["w_out"] = tiles(i["w_out"][0])
    a["w_ff1"] = tiles(i["w_ff1"][0])
    f2 = np.asarray(i["w_ff2"])[0]
    a["w_ff2"] = np.concatenate([tiles(f2[1024 * f:1024 * f + 1024]) for f in range(4)])
    aw = np.asarray(i["ada_w_2"])[0].reshape(8, 128, 3, 2, 1024).transpose(2, 0, 3, 1, 4)
    a["ada"] = np.ascontiguousarray(aw).reshape(48, 128, 1024)
    a["adab"] = cols(i["ada_b_2"][0], 48)
    a["g2b"] = np.asarray(i["ada_b_2"])[0, 5120:6144]
    w = np.asarray(i["w_in_2"])[0]
    sp_ = np.split(w, [512, 1024, 1536, 1544, 2056, 2568, 3080, 4104], axis=1)
    for n, x in zip(("qa", "ka", "va", "fa", "qb", "kb", "vb", "ga", "gb"), sp_):
        a["w2_" + n] = rows(x) if n in ("va", "vb") else tiles(x, pad=120 if n == "fa" else 0)
    a["w2_fox"], a["w2_sb"] = tiles(i["w_branch_fox_2"][0]), tiles(i["w_branch_sb_2"][0])
    a["w2_out"] = tiles(i["w_out_2"][0])
    vec = np.zeros((128, 64), np.float32)
    vec[:, 0:8], vec[:, 8:16] = cols(i["norm_mix"][0], 8), cols(i["norm_mlp"][0], 8)
    vec[:, 16:24], vec[:, 24:28] = cols(i["norm_final"], 8), cols(i["pool_scale"][0], 4)
    vec[:, 28:36], vec[:, 36:44] = cols(i["norm1_g_2"][0], 8), cols(i["norm2_g_2"][0], 8)
    vec[:, 44:52] = cols(i["c_2"][0], 8)
    vec[0:8, 52] = np.asarray(i["b_forget_2"])[0]
    vec[0:4, 53], vec[4:20, 53] = np.asarray(i["router_group_b_2"])[0], np.asarray(i["router_expert_b_2"])[0]
    a["vecs"] = vec
    rw = np.concatenate([np.asarray(i["router_group_w_2"])[0], np.asarray(i["router_expert_w_2"])[0]], axis=1)
    a["rw"] = rw.reshape(8, 128, 20).transpose(1, 0, 2).reshape(128, 160)
    for n, k in (("w_gate", "expert_w_gate_2"), ("w_up", "expert_w_up_2")):
        x = np.asarray(i[k])[0].reshape(16, 4, 2, 128, 512).transpose(0, 1, 3, 2, 4)
        a[n] = np.ascontiguousarray(x).reshape(16, 4, 128, 1024)
    a["w_down"] = np.asarray(i["expert_w_down_2"])[0].reshape(16, 4, 128, 1024)
    a["final_g"] = np.asarray(i["final_g_2"])
    a.update(constants())
    return {k: np.ascontiguousarray(v) for k, v in a.items()}


def build(nc, arrays, stop=None):
    t = {}
    for name, a in arrays.items():
        t[name] = nc.dram_tensor(f"in_{name}", a.shape, mybir.dt.from_np(a.dtype), kind="ExternalInput").ap()
    t["out"] = nc.dram_tensor("out_0", (1, S, D), F32, kind="ExternalOutput").ap()
    t["xs"] = nc.dram_tensor("xs", (NUNIT * 128, D), F32, kind="Internal").ap()
    t["ys"] = nc.dram_tensor("ys", (NUNIT * 128, D), F32, kind="Internal").ap()
    t["mod"] = nc.dram_tensor("mod", (12, 512), F32, kind="Internal").ap()
    t["nf"] = nc.dram_tensor("nf", (8, 512), F32, kind="Internal").ap()
    program(nc, t, stop)


def kernel(**inputs):
    import concourse.bacc as bacc
    from concourse.bass_utils import run_bass_kernel_spmd

    nc = bacc.Bacc("TRN2", target_bir_lowering=False, num_devices=1)
    arrays = layout(inputs)
    build(nc, arrays)
    r = run_bass_kernel_spmd(nc, [{f"in_{k}": v for k, v in arrays.items()}], core_ids=[0])
    return r.results[0]["out_0"]
```

```python
from contextlib import ExitStack

import numpy as np

import concourse.bass as bass
from concourse import mybir

F32 = mybir.dt.float32
F32R = mybir.dt.float32r
BF16 = mybir.dt.bfloat16
I32 = mybir.dt.int32
U32 = mybir.dt.uint32
ALU = mybir.AluOpType
ACT = mybir.ActivationFunctionType
AX = mybir.AxisListType.X

S = 512
D = 1024
NEG = -1e30
EPS = 1e-6
NRAW = 5
NSPL = 4
NUNIT = 23
CMP = 31
PACK = (0, 512, 1024, 896)


class Queue:

    def __init__(self, sem):
        self.sem, self.n, self.items, self.seen = sem, 0, [], {}

    def need(self, *tokens):
        for t in tokens:
            if t is None:
                continue
            if isinstance(t, list):
                self.need(*t)
                continue
            sem, value = t
            if self.seen.get(id(sem), 0) < value:
                self.seen[id(sem)] = value
                self.items.append(("wait", sem, value))

    def do(self, fn, *tokens):
        self.need(*tokens)
        self.n += 1
        self.items.append(("op", fn, (self.sem, 1)))
        return (self.sem, self.n)

    def quiet(self, fn, *tokens):
        self.need(*tokens)
        self.items.append(("op", fn, None))

    def dma(self, fn, sem, value, *tokens):
        self.need(*tokens)
        self.items.append(("op", fn, (sem, 16)))
        return (sem, value)

    def branch(self, count, *tokens):
        self.need((self.sem, self.n), *tokens)
        self.items.append(("if", count, self.n))
        self.before = dict(self.seen)

    def join(self):
        self.need((self.sem, self.n))
        self.items.append(("join", None, self.n))
        self.seen = self.before

    def bump(self):
        self.n += 1
        self.items.append(("op", lambda e: e.sem_inc(self.sem, 1), None))
        return (self.sem, self.n)

    def emit(self, eng):
        at = 0
        while at < len(self.items):
            kind, a, b = self.items[at]
            if kind == "if":
                end = next(i for i in range(at, len(self.items)) if self.items[i][0] == "join")
                steps = self.items[end][2] - b
                with eng.If(eng.value_load(a, min_val=0, max_val=7) > 0):
                    for x in self.items[at + 1:end]:
                        self.one(eng, x)
                with eng.Else():
                    if steps:
                        eng.sem_inc(self.sem, steps)
                    else:
                        eng.nop()
                at = end
            else:
                self.one(eng, self.items[at])
            at += 1

    def one(self, eng, item):
        kind, a, b = item
        if kind == "wait":
            eng.wait_ge(a, b)
        elif kind == "call":
            a(eng)
        else:
            ins = a(eng)
            if b is not None:
                ins.then_inc(b[0], b[1])


class Bank:

    def __init__(self, ap):
        self.ap, self.free = ap, []


def program(nc, t, stop=None):
    ctx = ExitStack()
    with ctx:
        def sb(name, shape, dt=F32):
            return ctx.enter_context(nc.sbuf_tensor(name, shape, dt))

        def sem(name):
            return ctx.enter_context(nc.semaphore(name))

        RS = sb("RS", [128, NSPL, 2, 1024], F32R)
        RH = sb("RH", [128, 2, 8, S], F32R)
        RA = sb("RA", [128, 2, 8, S], F32R)
        RAW = sb("RAW", [128, NRAW, 1024])
        X = sb("X", [128, 8, S])
        M = sb("M", [128, 8, S])
        PB = sb("PB", [128, 2, 1280])
        TB = sb("TB", [128, 3, 1280])
        PC = sb("PC", [128, 4, S])
        TAB = sb("TAB", [128, 2, S])
        VV = sb("VV", [128, 2, S])
        TMP = sb("TMP", [128, 4, S])
        identf = sb("identf", [128, 128])
        rotT = sb("rotT", [128, 128])
        onesf = sb("onesf", [128, 128])
        ntri = sb("ntri", [128, 128])
        nones = sb("nones", [128, 128])
        sltm = sb("sltm", [128, 128])
        identb = sb("identb", [128, 128], BF16)
        maskb = sb("maskb", [128, 128], BF16)
        maskt = sb("maskt", [128, 128], BF16)
        trib = sb("trib", [128, 128], BF16)
        onesb = sb("onesb", [128, 128], BF16)
        vecs = sb("vecs", [128, 64])
        modt = sb("modt", [128, 48])
        gsc = sb("gsc", [128, 32])
        small = sb("small", [128, 64])
        RT = sb("RT", [128, 704])
        banks = [Bank(ctx.enter_context(nc.psum_tensor(f"ps{i}", [128, 512], F32))) for i in range(8)]

        pe, act, dve, pool, sp = (Queue(sem("s_" + n)) for n in ("pe", "act", "dve", "pool", "sp"))

        def hiF(ap):
            return ap.bitcast(F32)

        counter = [0]
        every = []

        def load(q, dst, src, *tokens):
            counter[0] += 1
            s = sem(f"d{counter[0]}")
            every.append((s, 16))
            return q.dma(lambda e: e.dma_start(dst, src), s, 16, *tokens)

        slots = {}

        def load_slot(q, slot, dst, src, *tokens):
            if slot not in slots:
                slots[slot] = [sem("d_" + slot), 0]
            c = slots[slot]
            c[1] += 16
            return q.dma(lambda e: e.dma_start(dst, src), c[0], c[1], *tokens)

        def a_act(out, in_, func, *tokens, **kw):
            return act.do(lambda e: e.activation(out, in_, func, **kw), *tokens)

        def tt(q, out, a, b, op, *tokens):
            return q.do(lambda e: e.tensor_tensor(out, a, b, op), *tokens)

        def ts(q, out, a, s1, op0, *tokens, s2=None, op1=None):
            if op1 is None:
                return q.do(lambda e: e.tensor_scalar(out, a, s1, None, op0), *tokens)
            return q.do(lambda e: e.tensor_scalar(out, a, s1, s2, op0, op1), *tokens)

        def stt(out, a, s, b, op0, op1, *tokens):
            return dve.do(lambda e: e.scalar_tensor_tensor(out, a, s, b, op0, op1), *tokens)

        def copy(q, out, in_, *tokens):
            if q is act:
                return a_act(out, in_, ACT.Copy, *tokens)
            return q.do(lambda e: e.tensor_copy(out, in_), *tokens)

        def mm(out, lhsT, rhs, start, stop, *tokens, last=False, shared=False):
            fn = lambda e: e.matmul(out, lhsT, rhs, start=start, stop=stop, skip_group_check=shared)
            return pe.do(fn, *tokens) if last else pe.quiet(fn, *tokens)

        def tr(out, in_, *tokens, last=False, ident=None):
            n = in_.shape[0]
            idn = identf[0:n, 0:n]
            fn = lambda e: e.transpose(out, in_, idn)
            return pe.do(fn, *tokens) if last else pe.quiet(fn, *tokens)

        plan = []

        def add(name, kind):
            for u in range(t[name].shape[0]):
                plan.append((name, u, t[name][u], kind))

        def add1(name, u, kind="split"):
            plan.append((name, u, t[name][u], kind))

        add("w_qkv", "split")
        add("w_c", "raw")
        for m in range(8):
            add1("w_gb", m)
            if m % 2 == 1:
                add1("w_nsa", m - 1)
                add1("w_nsa", m)
        add("w_u", "split")
        for m in range(8):
            add1("w_ga", m)
            if m % 2 == 1:
                add1("w_pp", m // 2)
        add("w_out", "split")
        ada = iter(range(48))
        for f in range(4):
            for m in range(8):
                add1("w_ff1", f * 8 + m)
                for u in [x for _, x in zip(range(1), ada)]:
                    add1("ada", u, "raw")
            for m in range(8):
                add1("w_ff2", f * 8 + m)
                if m % 2:
                    for u in [x for _, x in zip(range(1), ada)]:
                        add1("ada", u, "raw")
        for n in ("w2_qa", "w2_fa", "w2_ka", "w2_va", "w2_qb", "w2_kb", "w2_vb"):
            add(n, "split")
        for m in range(0, 8, 2):
            add1("w2_ga", m)
            add1("w2_ga", m + 1)
            add1("w2_fox", m // 2)
            add1("w2_gb", m)
            add1("w2_gb", m + 1)
            add1("w2_sb", m // 2)
        add("w2_out", "split")
        extra_reg = {}
        for u0, u1 in ((0, 16), (16, NUNIT)):
            for u in range(u0, u1):
                for n in ("w_gate", "w_up"):
                    for c in range(4):
                        plan.append((n, (u, c), None, "split"))
                if u > u0:
                    for c in range(4):
                        plan.append(("w_down", (u - 1, c), None, "split"))
            for c in range(4):
                plan.append(("w_down", (u1 - 1, c), None, "split"))
            if u0 == 0:
                always = len(plan)

        raw_sem = [sem(f"raw{i}") for i in range(NRAW)]
        raw_free = [[] for _ in range(NRAW)]
        spl_free = [[] for _ in range(NSPL)]
        st = {"load": 0, "split": 0, "nsplit": 0, "get": 0}
        landed, parts = {}, {}
        lo_engine = [lambda n: pool]
        late = {}

        def stream_load(n):
            name, u, src, kind = plan[n]
            r = n % NRAW
            dst = RAW[:, r, :]
            need = list(raw_free[r])
            if src is None:
                uu, c = u
                if uu < 16:
                    src = t[name][uu, c]
                else:
                    if uu not in late:
                        late[uu] = True
                        need.append(late["tok"])
                        j = uu - 16

                        def ld(e, j=j):
                            extra_reg[j] = e.value_load(EXI[0:1, j:j + 1], min_val=0, max_val=15)
                        sp.need(late["tok"])
                        sp.items.append(("call", ld, None))

                    def fn(e, j=uu - 16, name=name, c=c):
                        w = t[name][bass.ds(extra_reg[j], 1), c, :, :].rearrange("a p n -> (a p) n")
                        return e.dma_start(dst, w)
                    landed[n] = sp.dma(fn, raw_sem[r], 16 * (n // NRAW + 1), need)
                    return
            landed[n] = sp.dma(lambda e: e.dma_start(dst, src), raw_sem[r], 16 * (n // NRAW + 1), need)

        def stream_split(n):
            if plan[n][3] == "raw":
                return
            k = st["nsplit"]
            st["nsplit"] += 1
            s, r = k % NSPL, n % NRAW
            hi = a_act(RS[:, s, 0, :], RAW[:, r, :], ACT.Copy, landed[n], spl_free[s])
            q = lo_engine[0](k)
            lo = tt(q, RS[:, s, 1, :], RAW[:, r, :], hiF(RS[:, s, 0, :]), ALU.subtract,
                    landed[n], hi, spl_free[s])
            raw_free[r] = [hi, lo]
            parts[n] = (s, lo, hi)

        def get(name, u):
            n = st["get"]
            assert plan[n][:2] == (name, u), (plan[n][:2], name, u)
            end = always if n < always else len(plan)
            while st["load"] <= min(n + NRAW - 1, end - 1):
                stream_load(st["load"])
                st["load"] += 1
                while st["split"] < min(st["load"], n + NSPL):
                    stream_split(st["split"])
                    st["split"] += 1
            while st["split"] <= min(n + NSPL - 1, end - 1):
                stream_split(st["split"])
                st["split"] += 1
            st["get"] += 1
            return n

        def used(n, tok):
            if plan[n][3] == "raw":
                raw_free[n % NRAW] = [tok]
            else:
                spl_free[parts[n][0]] = [tok]

        ring = [0]

        def bank(pool_=None):
            b = (pool_ or range(8))
            ring[0] += 1
            return banks[b[ring[0] % len(b)]]

        def dense(name, u, acts, K, finish, which=range(8)):
            R, k0, toks = acts
            n = get(name, u)
            s, lo_t, hi_t = parts[n]
            for m in range(8 // K):
                b = bank(which)
                for k in range(K):
                    c = (m * K + k) * 128
                    wh, wl = RS[:, s, 0, c:c + 128], RS[:, s, 1, c:c + 128]
                    xh, xl = R[:, 0, k0 + k, :], R[:, 1, k0 + k, :]
                    mm(b.ap[:, :], wh, xh, k == 0, False, hi_t, toks[k], *(b.free if k == 0 else ()))
                    mm(b.ap[:, :], wh, xl, False, False)
                    tok = mm(b.ap[:, :], wl, xh, False, k == K - 1, lo_t, last=(k == K - 1))
                if m == 8 // K - 1:
                    used(n, tok)
                finish((8 // K) * u + m, b, tok)

        def dense_rows(name, units, acts, finish, which):
            R, k0, toks = acts
            for u in range(units):
                n = get(name, u)
                s, lo_t, hi_t = parts[n]
                for kk in range(2):
                    k = 2 * u + kk
                    wh, wl = (RS[:, s, x, kk * 512:kk * 512 + 512] for x in (0, 1))
                    for i in range(4):
                        b = banks[which[i]]
                        xh, xl = (R[:, x, k0 + k, 128 * i:128 * i + 128] for x in (0, 1))
                        mm(b.ap[:, :], xh, wh, k == 0, False, hi_t, toks[k], *(b.free if k == 0 else ()))
                        mm(b.ap[:, :], xl, wh, False, False)
                        tok = mm(b.ap[:, :], xh, wl, False, k == 7, lo_t, last=True)
                        if k == 7:
                            finish(i, b, tok)
                used(n, tok)

        def split_to(R, k, src, hi_q, lo_q, free, *tokens):
            hi = copy(hi_q, R[:, 0, k, :], src, free, *tokens)
            lo = tt(lo_q, R[:, 1, k, :], src, hiF(R[:, 0, k, :]), ALU.subtract, hi, free, *tokens)
            return hi, lo

        tmp_free = [[] for _ in range(4)]
        cst = {}
        xt = [load(sp, X[:, 2 * i:2 * i + 2, :], t["xT"][:, 2 * i:2 * i + 2, :]) for i in range(4)]
        cst["onesf"] = load(sp, onesf[:, :], t["onesf"])
        cst["vecs"] = load(sp, vecs[:, :], t["vecs"])
        for name, dst in (("identf", identf), ("rotT", rotT)):
            cst[name] = load(sp, dst[:, :], t[name])
        cst["tab"] = load(sp, TAB[:, :, :], t["tab"])
        for name, dst in (("ntri", ntri), ("nones", nones), ("sltm", sltm), ("maskb", PC[:, 2, 0:128]),
                          ("maskt", PC[:, 2, 128:256])):
            cst[name] = load(sp, dst[:, :], t[name])
        for name, dst, src in (("identb", identb, "identf"), ("maskb", maskb, "maskb"), ("maskt", maskt, "maskt"),
                               ("trib", trib, "sltm"), ("onesb", onesb, "onesf")):
            frm = {"identf": identf, "sltm": sltm, "onesf": onesf, "maskb": PC[:, 2, 0:128],
                   "maskt": PC[:, 2, 128:256]}[src]
            cst[name] = copy(pool, dst[:, :], frm[:, :], cst[src])
        eps = dve.do(lambda e: e.memset(small[:, 0:1], EPS))
        one = dve.do(lambda e: e.memset(small[:, 1:2], 1.0))

        VG_MIX, VG_MLP, VG_FIN, V_PS, VG1, VG2, V_C, V_BF = 0, 8, 16, 24, 28, 36, 44, 52

        def rstd(xtoks, out, *free):
            b = bank()
            for k in range(8):
                s = a_act(TMP[:, k % 2, :], X[:, k, :], ACT.Square, xtoks[k], tmp_free[k % 2])
                tok = mm(b.ap[:, :], onesf[:, :], TMP[:, k % 2, :], k == 0, k == 7, s, cst["onesf"],
                         *(b.free if k == 0 else ()), last=True)
                tmp_free[k % 2] = [tok]
            r = a_act(out, b.ap[:, :], ACT.Sqrt, tok, eps, *free, bias=small[:, 0:1], scale=1.0 / D)
            b.free = [r]
            return dve.do(lambda e: e.reciprocal(out, out), r)

        RST = RT[:, 0:512]
        rst_free = [[]]
        sq = {}

        def square_in(k, xtok):
            if k == 0:
                sq["acc"] = a_act(RST, X[:, 0, :], ACT.Square, xtok, rst_free[0])
                return
            j = k % 2
            s = a_act(TMP[:, j, :], X[:, k, :], ACT.Square, xtok, tmp_free[j])
            sq["acc"] = tt(pool if k < 7 else dve, RST, RST, TMP[:, j, :], ALU.add, s, sq["acc"])
            tmp_free[j] = [sq["acc"]]

        SQ2, RST2 = PB[:, 0, 0:512], PB[:, 0, 512:1024]

        def square_in2(k, xtok, *free):
            g = vecs[:, VG_FIN + k:VG_FIN + k + 1]
            if k == 0:
                sq["acc2"] = a_act(SQ2, X[:, 0, :], ACT.Square, xtok, cst["vecs"], *free, scale=g)
                return
            j = k % 2
            s = a_act(TMP[:, j, :], X[:, k, :], ACT.Square, xtok, tmp_free[j], scale=g)
            sq["acc2"] = tt(dve, SQ2, SQ2, TMP[:, j, :], ALU.add, s, sq["acc2"])
            tmp_free[j] = [sq["acc2"]]

        def rstd_twice():
            b, b2 = bank(), bank()
            t1 = mm(b.ap[:, :], onesf[:, :], RST, True, True, sq["acc"], b.free, last=True)
            t2 = mm(b2.ap[:, :], onesf[:, :], SQ2, True, True, sq["acc2"], b2.free, last=True)
            r = a_act(RST, b.ap[:, :], ACT.Sqrt, t1, eps, bias=small[:, 0:1], scale=1.0 / D)
            b.free = [r]
            r1 = dve.do(lambda e: e.reciprocal(RST, RST), r)
            u = tt(dve, RST2, RST, RST, ALU.mult, r1)
            u = tt(dve, RST2, RST2, b2.ap[:, :], ALU.mult, u, t2)
            b2.free = [u]
            u = a_act(RST2, RST2, ACT.Sqrt, u, eps, bias=small[:, 0:1], scale=1.0 / D)
            return r1, dve.do(lambda e: e.reciprocal(RST2, RST2), u)

        def rstd_summed():
            b = bank()
            tok = mm(b.ap[:, :], onesf[:, :], RST, True, True, sq["acc"], cst["onesf"], b.free, last=True)
            r = a_act(RST, b.ap[:, :], ACT.Sqrt, tok, eps, bias=small[:, 0:1], scale=1.0 / D)
            b.free = [r]
            return dve.do(lambda e: e.reciprocal(RST, RST), r)

        def normed(xtoks, gcol, scol, h_free, r=None, R_=RST):
            r = r or rstd(xtoks, RST, *rst_free[0])
            toks = []
            for k in range(8):
                j = 2 + k % 2
                w = stt(TMP[:, j, :], X[:, k, :], gcol(k), R_, ALU.mult, ALU.mult, r, xtoks[k],
                        cst["vecs"], tmp_free[j])
                if scol is not None:
                    w = ts(dve, TMP[:, j, :], TMP[:, j, :], scol(k), ALU.add, w)
                hi, lo = split_to(RH, k, TMP[:, j, :], act, pool if k % 2 else dve, h_free, w)
                tmp_free[j] = [hi, lo]
                toks.append([hi, lo])
            rst_free[0] = [w]
            return toks

        H = normed([xt[k // 2] for k in range(8)], lambda k: vecs[:, VG_MIX + k:VG_MIX + k + 1], None, [])
        hx = (RH, 0, H)

        Kz = M[:, :, :].rearrange("p (b g r) n -> p b g r n", b=2, g=2)
        kzero = [dve.do(lambda e, i=i: e.memset(M[:, 4 * i:4 * i + 4, :], 0.0)) for i in range(2)]
        scz = dve.do(lambda e: e.memset(PB[:, 1, :], 0.0))
        scz2 = dve.do(lambda e: e.memset(TB[:, 1, 0:1024], 0.0))

        def rope(m, outs):
            def first(b, tok, scale):
                j = m % 2
                e1 = a_act(TMP[:, j, :], b.ap[:, :], ACT.Copy, tok, tmp_free[j], scale=scale)
                b.free = [e1]

                def second():
                    b2 = bank()
                    r = mm(b2.ap[:, :], rotT[:, :], TMP[:, j, :], True, True, e1, cst["rotT"], b2.free,
                           last=True)
                    c = tt(pool, TMP[:, 2 + j, :], TMP[:, j, :], TAB[:, 0, :], ALU.mult, e1,
                           cst["tab"], tmp_free[2 + j])
                    s_ = tt(dve, TMP[:, j, :], b2.ap[:, :], TAB[:, 1, :], ALU.mult, r, c, cst["tab"])
                    b2.free = [s_]
                    toks = []
                    for (lo_, hi_), dst, fr in outs:
                        toks.append(tt(dve, dst, TMP[lo_:hi_, j, :], TMP[lo_:hi_, 2 + j, :], ALU.add,
                                       s_, c, fr))
                    tmp_free[j] = [toks[-1]]
                    tmp_free[2 + j] = [toks[-1]]
                    return toks
                return second
            return first

        pend = [None]

        def flush():
            if pend[0] is not None:
                f, pend[0] = pend[0], None
                f()

        xread = H[7]
        qtok = {}
        ktok = {}
        vtok = {}
        cmpt = {}
        F2 = PB[:, 0, 0:1024].rearrange("p (g n) -> p g n", g=2)
        Fpk, Fpv = PB[:, 1, 0:992], TB[:, 0, 0:992]

        def fin_qkv(u, b, tok):
            flush()
            if u < 8:
                sec = rope(u, [((0, 128), X[:, u, :], xread)])(b, tok, 0.125)

                def g():
                    qtok[u] = sec()[0]
                pend[0] = g
            elif u < 10:
                br = u - 8
                outs = []
                for g_ in range(2):
                    for p_ in range(2):
                        outs.append(((64 * g_, 64 * g_ + 64), Kz[64 * p_:64 * p_ + 64, br, g_, p_, :], kzero))
                sec = rope(u, outs)(b, tok, 1.0)

                def g():
                    tk = sec()
                    for g_ in range(2):
                        for p_ in range(2):
                            ktok[(br, g_, p_)] = tk[2 * g_ + p_]
                pend[0] = g
            elif u < 12:
                src = b.ap
                kv = u - 10
                fre = cmpt.get("f2free", [])
                cs = []
                for g_ in range(2):
                    cs.append(copy(dve, F2[0:64, g_, :], src[64 * g_:64 * g_ + 64, :], tok, fre))
                    cs.append(copy(dve, F2[64:128, g_, 0:511], src[64 * g_:64 * g_ + 64, 1:512], tok, fre))
                b.free = [cs[-1]]
                Fp = (Fpk, Fpv)[kv]
                for lp in range(16):
                    o = Fp[:, lp * 62:lp * 62 + 62].rearrange("p (g n) -> p g n", g=2)
                    i_ = F2[:, :, 2 * lp:2 * lp + 481:16]
                    last = ts(dve, o, i_, PE2[:, kv * 16 + lp:kv * 16 + lp + 1], ALU.add, cs, cst["pe2"], scz)
                cmpt["f2free"] = [last]
                cmpt[kv] = last
            elif u < 14:
                br = u - 12
                j = u % 2
                e1 = copy(act, TMP[:, j, :], b.ap[:, :], tok, tmp_free[j])
                b.free = [e1]

                def g():
                    b2 = bank()
                    for i in range(4):
                        tk = tr(b2.ap[:, 128 * i:128 * i + 128], TMP[:, j, 128 * i:128 * i + 128], e1,
                                cst["identf"], *(b2.free if i == 0 else ()), last=(i == 3))
                    tmp_free[j] = [tk]
                    vtok[br] = copy(dve, VV[:, br, :], b2.ap[:, :], tk)
                    b2.free = [vtok[br]]
                pend[0] = g
            else:
                j = u % 2
                e1 = a_act(TMP[0:48, j, :], b.ap[0:48, :], ACT.Sigmoid, tok, tmp_free[j])
                b.free = [e1]

                def g():
                    b2 = bank()
                    for i in range(4):
                        tk = tr(b2.ap[:, 48 * i:48 * i + 48], TMP[0:48, j, 128 * i:128 * i + 128], e1,
                                cst["identf"], *(b2.free if i == 0 else ()), last=(i == 3))
                    tmp_free[j] = [tk]
                    cmpt["gate"] = copy(dve, GTS[:, :], b2.ap[:, 0:192], tk)
                    b2.free = [cmpt["gate"]]
                pend[0] = g

        GTS = RT[:, 512:704]
        PE2 = sb("PE2", [128, 32])
        CW2 = TB[:, 2, 0:384].rearrange("p (c n) -> p c n", c=2)
        CTB = TB[:, 2, 384:508]
        MCB = TB[:, 2, 508:636]
        KCZ = sb("KCZ", [128, 4, 32])
        VBK = sb("VBK", [128, 4, 128])
        cst["pe2"] = load(sp, PE2[:, :], t["pe2"])
        cst["mcb"] = load(sp, MCB[:, :], t["mcb"])
        cst["cw2"] = load(sp, CW2[:, :, :], t["cw2"])
        cst["ctb"] = load(sp, CTB[:, :], t["ctb"])
        kcz0 = dve.do(lambda e: e.memset(KCZ[:, :, :], 0.0))
        vbk0 = dve.do(lambda e: e.memset(VBK[:, :, :], 0.0))
        for u in range(15):
            dense("w_qkv", u, hx, 8, fin_qkv)
        flush()

        HID = TB[:, 1, 0:256]
        HT = TB[:, 1, 256:512].rearrange("p (c n) -> p c n", c=2)
        kct = []
        vct = []
        prev = []
        for kv in range(2):
            b = bank()
            Fp = (Fpk, Fpv)[kv]
            for c in range(4):
                n = get("w_c", kv * 4 + c)
                for q in range(4):
                    lp = 4 * c + q
                    tok = mm(b.ap[0:62, 0:256], Fp[:, lp * 62:lp * 62 + 62],
                             RAW[:, n % NRAW, q * 256:q * 256 + 256], lp == 0, lp == 15,
                             cmpt[kv], landed[n], *(b.free if lp == 0 else ()), last=(q == 3))
                used(n, tok)
            g1 = a_act(HID[0:62, :], b.ap[0:62, 0:256], ACT.Gelu_apprx_tanh, tok, scz2, prev)
            b.free = [g1]
            b = bank()
            for c in range(2):
                tok = tr(b.ap[:, 128 * c:128 * c + 62], HID[0:62, 128 * c:128 * c + 128], g1, b.free,
                         last=(c == 1))
            c1 = copy(dve, HT[:, :, 0:62], b.ap[:, 0:256].rearrange("p (c n) -> p c n", c=2)[:, :, 0:62],
                      tok, prev, scz2)
            b.free = [c1]
            b = bank()
            if kv == 0:
                for c in range(2):
                    tok = mm(b.ap[:, 0:62], CW2[:, c, 0:128], HT[:, c, 0:62], c == 0, c == 1, c1,
                             cst["cw2"], *(b.free if c == 0 else ()), last=(c == 1))
                prev = [tok]
                T0, T1 = TB[:, 1, 512:574], TB[:, 1, 576:638]
                e1 = copy(dve, T0, b.ap[:, 0:62], tok, scz2)
                b.free = [e1]
                b = bank()
                tok = mm(b.ap[:, 0:62], rotT[:, :], T0, True, True, e1, b.free, last=True)
                e2 = tt(dve, T1, b.ap[:, 0:62], CTB[:, 62:124], ALU.mult, tok, cst["ctb"], scz2)
                b.free = [e2]
                e3 = tt(dve, T0, T0, CTB[:, 0:62], ALU.mult, tok, e1)
                for g_ in range(2):
                    for p_ in range(2):
                        r0 = 64 * p_
                        kct.append(tt(dve, KCZ[r0:r0 + 64, 2 * g_ + p_, 0:31], T0[r0:r0 + 64, 31 * g_:31 * g_ + 31],
                                      T1[r0:r0 + 64, 31 * g_:31 * g_ + 31], ALU.add, e2, e3, kcz0))
            else:
                for g_ in range(2):
                    for c in range(2):
                        tok = mm(b.ap[0:31, 64 * g_:64 * g_ + 64], HT[:, c, 31 * g_:31 * g_ + 31],
                                 CW2[:, c, 128:192], c == 0, c == 1, c1, cst["cw2"],
                                 *(b.free if c == 0 and g_ == 0 else ()), last=(c == 1))
                for g_ in range(2):
                    for a in range(2):
                        for z in range(2):
                            r0 = 64 * a + 32 * z
                            vct.append(copy(dve, VBK[r0:r0 + 31, 2 * g_ + a, 64 * z:64 * z + 64],
                                            b.ap[0:31, 64 * g_:64 * g_ + 64], tok, vbk0))
                b.free = [vct[-1]]

        SCQ = [PB[:, 0, 0:512], PB[:, 0, 512:1024]]
        SCW = [PB[:, 1, 0:512], PB[:, 1, 512:1024]]
        SB_ = TB[:, 0, 0:64]
        pbw = [cmpt["f2free"], cmpt[0], cmpt[1], [pe.do(lambda e: e.matmul(banks[7].ap[0:32, 0:32], identb[:, 0:32], identb[:, 0:32], start=True, stop=True), cst["identb"], banks[7].free)]]
        gts = GTS[:, :].rearrange("p (i h b) -> p i h b", i=4, b=3)
        mcb = MCB[:, :].rearrange("p (i n) -> p i n", i=4)
        pct = []
        sf = [[], []]
        for Q in range(4):
            g_ = Q // 2
            b = bank()
            for a in range(2):
                for p_ in range(2):
                    j = 2 * a + p_
                    tok = mm(b.ap[32 * j:32 * j + 32, :], KCZ[:, 2 * g_ + p_, :], X[:, 2 * Q + a, :], True, True,
                             kct, qtok[2 * Q + a], b.free, last=(j == 3))
            A, W = SCQ[Q % 2], SCW[Q % 2]
            fr = sf[Q % 2]
            e1 = copy(act, A, b.ap[:, :], tok, pbw, fr)
            b.free = [e1]
            b = bank()
            for i in range(4):
                tok = tr(b.ap[:, 128 * i:128 * i + 128], A[:, 128 * i:128 * i + 128], e1, b.free, last=(i == 3))
            W4 = W.rearrange("p (i h n) -> p i h n", i=4, h=4)
            B4 = b.ap[:, :].rearrange("p (i h n) -> p i h n", i=4, h=4)
            for i in range(4):
                e2 = tt(dve, W4[:, i], B4[:, i], mcb[:, i, :].unsqueeze(1).broadcast_to([128, 4, 32]), ALU.add, tok,
                        cst["mcb"], pbw, fr)
            b.free = [e2]
            W3 = W.rearrange("p (x n) -> p x n", n=32)
            SM, SR = SB_[:, 0:16], SB_[:, 16:32]
            e3 = dve.do(lambda e, W3=W3: e.reduce_max(SM, W3, AX), e2)
            e4 = ts(dve, SM, SM, -1e29, ALU.max, e3)
            e5 = tt(dve, W3, W3, SM.unsqueeze(2).broadcast_to([128, 16, 32]), ALU.subtract, e4)
            e6 = a_act(W, W, ACT.Exp, e5)
            e7 = dve.do(lambda e, W3=W3: e.reduce_sum(SR, W3, AX), e6)
            e8 = ts(dve, SR, SR, 1e-30, ALU.max, e7)
            e9 = dve.do(lambda e: e.reciprocal(SR, SR), e8)
            e10 = tt(dve, SR.rearrange("p (i h) -> p i h", i=4), SR.rearrange("p (i h) -> p i h", i=4),
                     gts[:, :, 4 * Q:4 * Q + 4, 0], ALU.mult, e9, cmpt["gate"])
            e11 = tt(dve, W3, W3, SR.unsqueeze(2).broadcast_to([128, 16, 32]), ALU.mult, e10)
            b = bank()
            for i in range(4):
                tok = tr(b.ap[:, 128 * i:128 * i + 128], W[:, 128 * i:128 * i + 128], e11, b.free, last=(i == 3))
            c1 = copy(act, PC[:, Q, :], b.ap[:, :], tok, cst["maskb"], cst["maskt"])
            b.free = [c1]
            sf[Q % 2] = [tok]
            pct.append(c1)
        cmpdone = sf[0] + sf[1] + [e11]

        SBK = [0, 1, 2, 3]
        TPL = ((4, 0), (5, 0), (6, 0), (5, 384))
        stat = sb("stat", [128, 3, 2, 4])

        def attention(N, qtile, keys, kneed, score_add, weight, value, obank, ostart, odone, first_need):
            pfree, tfree = [first_need] * 2, [first_need] * 3
            ptok, ttok = {}, {}
            sfree = [[], []]
            off = [0, 128, 384, 768]
            toff = PACK

            def meet_values(m, js):
                for j in js:
                    c, w = toff[j], 512 - 128 * j
                    for q in (m, m + 1):
                        b, r0 = obank(q)
                        st_ = ostart(q, b) if j == 0 else False
                        va, vt = value(q, j)
                        tok = mm(b.ap[r0:r0 + 64, 128 * j:512], va, TB[:, q % 3, c:c + w], st_, False,
                                 ttok[q][j], vt, *(b.free if j == 0 else ()), last=True, shared=True)
                if js[-1] == 3:
                    tfree[m % 3] = tfree[(m + 1) % 3] = [tok]
                    odone(m + 1, b, tok)

            for n in range(N + 3):
                if n % 2 == 0 and n >= 4:
                    meet_values(n - 4, (2, 3))
                tks = {}
                if n < N:
                    P_ = PB[:, n % 2, :]
                    mxs, sms, rcs = stat[:, 0, n % 2, :], stat[:, 1, n % 2, :], stat[:, 2, n % 2, :]
                    adder = score_add(n) if score_add else None
                    ex = [None] * 4
                for i in (3, 2, 1, 0):
                    if n < N:
                        b = banks[SBK[i]]
                        w = 128 * (i + 1)
                        mm(b.ap[:, 0:w], qtile(n, i), keys(n)[:, 0:w], True, False, kneed(n), b.free)
                        tok = mm(b.ap[:, w - 128:w], identb[:, :], maskb[:, :], False, True, cst["identb"],
                                 cst["maskb"], last=True)
                        pd = P_[:, off[i]:off[i] + w]
                        if adder is None:
                            m_ = dve.do(lambda e, b=b, w=w, o=mxs[:, i:i + 1]: e.tensor_reduce(
                                o, b.ap[:, 0:w], AX, ALU.max, negate=True), tok, sfree[n % 2])
                            x_ = act.do(lambda e, b=b, w=w, pd=pd, mx=mxs[:, i:i + 1], sm=sms[:, i:i + 1]:
                                        e.activation(pd, b.ap[:, 0:w], ACT.Exp, bias=mx, accum_out=sm),
                                        m_, tok, pfree[n % 2], sfree[n % 2])
                            b.free = [x_]
                        else:
                            ad, atok = adder[:2]
                            a_ = dve.do(lambda e, b=b, w=w, pd=pd, o=mxs[:, i:i + 1], ad=ad:
                                        e.tensor_tensor_reduce(out=pd, in0=b.ap[:, 0:w], in1=ad[:, 0:w],
                                                               scale=-1.0, scalar=3e38, op0=ALU.add, op1=ALU.min,
                                                               accum_out=o),
                                        tok, atok, pfree[n % 2], sfree[n % 2])
                            b.free = [a_]
                            x_ = act.do(lambda e, pd=pd, mx=mxs[:, i:i + 1], sm=sms[:, i:i + 1]:
                                        e.activation(pd, pd, ACT.Exp, bias=mx, scale=-1.0, accum_out=sm), a_,
                                        sfree[n % 2])
                            if i == 0:
                                adder[2](a_)
                        ex[i] = x_
                    if n % 2 == 1 and n >= 3 and i >= 2:
                        meet_values(n - 3, (3 - i,))
                if 1 <= n <= N:
                    m = n - 1
                    for j in (0, 1, 3, 2):
                        bi, o = TPL[j]
                        for ii in range(j, 4):
                            tok = tr(banks[bi].ap[:, o + 128 * (ii - j):o + 128 * (ii - j) + 128],
                                     PB[:, m % 2, off[ii] + 128 * j:off[ii] + 128 * j + 128], ptok[m][ii],
                                     banks[bi].free if o == 0 else None, last=(ii == 3))
                        if j == 1:
                            continue
                        c, w = {0: (0, 512), 3: (512, 512), 2: (1024, 256)}[j]
                        tk = copy(act, TB[:, m % 3, c:c + w], banks[bi].ap[:, 0:w], tok, tfree[m % 3])
                        banks[bi].free = [tk]
                        tks[j] = tk
                        if j == 3:
                            tks[1] = tk
                    pfree[m % 2] = [tok]
                    ttok[m] = tks
                if n < N:
                    r_ = dve.do(lambda e, o=rcs, i_=sms: e.reciprocal(o, i_), ex, sfree[n % 2])
                    if weight is not None:
                        wt, wtok = weight(n)
                        r_ = tt(dve, rcs, rcs, wt, ALU.mult, r_, wtok)
                    pt = []
                    for i in range(4):
                        w = 128 * (i + 1)
                        pd = P_[:, off[i]:off[i] + w]
                        pt.append(ts(dve, pd, pd, rcs[:, i:i + 1], ALU.mult, ex[i], r_))
                    ptok[n] = pt
                    sfree[n % 2] = [pt[-1]]
            return pfree + tfree

        RAT = {}

        def nsa_start(m, b):
            if m % 4 == 0:
                pr = m // 4
                mm(b.ap[:, :], VBK[:, 2 * (pr // 4) + pr % 2, :], PC[:, pr // 2, :], True, False, vct,
                   pct[pr // 2], b.free, shared=True)
            return False

        def nsa_done(m, b, tok):
            if m % 4 == 3:
                RAT[m // 4] = list(split_to(RA, m // 4, b.ap[:, :], act, dve, [], tok))
                b.free = RAT[m // 4]

        ring[0] = 0
        adone = attention(
            32, lambda n, i: X[:, n // 4, 128 * i:128 * i + 128],
            lambda n: Kz[:, (n // 2) % 2, n // 16, n % 2, :],
            lambda n: [qtok[n // 4], ktok[((n // 2) % 2, n // 16, n % 2)]], None,
            lambda n: (gts[:, :, 2 * (n // 4) + n % 2, 1 + (n // 2) % 2], cmpt["gate"]),
            lambda m, j: (VV[:, (m // 2) % 2, 128 * j + 64 * (m // 16):128 * j + 64 * (m // 16) + 64],
                          vtok[(m // 2) % 2]),
            lambda m: (banks[7], 64 * (m % 2)), nsa_start, nsa_done, cmpdone)
        xt = [load(act, X[:, 2 * i:2 * i + 2, :], t["xT"][:, 2 * i:2 * i + 2, :], adone) for i in range(4)]
        xt = [xt[k // 2] for k in range(8)]
        if stop == "nsa":
            return finish_program(nc, ctx, locals())

        gb_bank = {}
        mtok = {}
        sg_free = [[], [], [], []]

        def gate_fin(store):
            def f(m, b, tok):
                j = m % 4
                g1 = a_act(TMP[:, j, :], b.ap[:, :], ACT.Sigmoid, tok, tmp_free[j], sg_free[j])
                b.free = [g1]
                store[m] = g1
            return f

        gt = {}

        def merge_fin(first, base_tok):
            def f(m, b, tok):
                j = m % 4
                if first:
                    o = tt(dve, M[:, m, :], TMP[:, j, :], b.ap[:, :], ALU.mult, tok, gt[m], base_tok)
                    mtok[m] = o
                else:
                    o1 = tt(dve, TMP[:, j, :], TMP[:, j, :], b.ap[:, :], ALU.mult, tok, gt[m])
                    o = tt(pool, M[:, m, :], M[:, m, :], TMP[:, j, :], ALU.add, o1, mtok[m])
                    mtok[m] = o
                    b.free = [o1]
                    tmp_free[j] = [o]
                    return
                b.free = [o]
                tmp_free[j] = [o]
            return f

        oa = (RA, 0, [RAT[k] for k in range(8)])
        for m in range(8):
            dense("w_gb", m, hx, 8, gate_fin(gt))
            if m % 2 == 1:
                dense("w_nsa", m - 1, oa, 8, merge_fin(True, adone))
                dense("w_nsa", m, oa, 8, merge_fin(True, adone))
        ra_free = [(pe.sem, pe.n)]

        UU = PB[:, 0, 0:512]
        UA = PB[:, 0, 512:1024]
        UB = PB[:, 1, 0:512]
        UC = PB[:, 1, 512:1024]
        WP = TB[:, 0, 0:512]
        ICT = TB[:, 1, 0:64]
        cst["wp"] = load(act, WP, t["w_pool"], adone)
        cst["ict"] = load(act, ICT, t["ict"], adone)
        ptk = {}
        pl = {"free": [], "y": {}}

        def fin_u(u, b, tok):
            flush()
            w = (2, 4, 8, 16)[u]
            e1 = copy(act, UU, b.ap[:, :], tok, adone, pl["free"])
            b.free = [e1]
            src, last = UU, e1
            sh, bufs, k = 1, [UA, UB], 0
            while sh < w:
                dst = bufs[k % 2]
                c_ = copy(dve, dst[:, 0:sh], src[:, 0:sh], last, adone, pl["free"])
                last = [tt(dve, dst[:, sh:], src[:, sh:], src[:, 0:512 - sh], ALU.add, last, c_), c_]
                src, sh, k = dst, sh * 2, k + 1
            m1 = tt(dve, src[:, 0:16], src[:, 0:16], ICT[:, 16 * u:16 * u + 16], ALU.mult, last, cst["ict"])
            m2 = ts(dve, src[:, 16:], src[:, 16:], 1.0 / w, ALU.mult, last)
            d = tt(dve, UC, src, UU, ALU.subtract, m1, m2, pl["free"])

            def g():
                b2 = bank()
                tk = mm(b2.ap[:, :], WP[:, 128 * u:128 * u + 128], UC, True, True, d, cst["wp"], b2.free,
                        last=True)
                y = a_act(UU, b2.ap[:, :], ACT.Copy, tk, d, scale=vecs[:, V_PS + u:V_PS + u + 1])
                b2.free = [y]
                hi, lo = split_to(RA, u, UU, act, dve, ra_free, y)
                pl["free"] = [hi, lo, tk]
                pl["y"][u] = [hi, lo]
            pend[0] = g

        for u in range(4):
            dense("w_u", u, hx, 8, fin_u)
        flush()
        ya = (RA, 0, [pl["y"][k] for k in range(4)])
        for m in range(8):
            dense("w_ga", m, hx, 8, gate_fin(gt))
            if m % 2 == 1:
                dense("w_pp", m // 2, ya, 4, merge_fin(False, None))
        h_free = [(pe.sem, pe.n)]
        H = [list(split_to(RH, k, M[:, k, :], act, pool if k % 2 else dve, h_free, mtok[k])) for k in range(8)]

        def residual(m, b, tok):
            o = tt(dve, X[:, m, :], X[:, m, :], b.ap[:, :], ALU.add, tok, xt[m])
            b.free = [o]
            xt[m] = o
            if lastx[0]:
                square_in(m, o)
            if lastx[0] == 2:
                square_in2(m, o, ra_free)

        lastx = [True]
        for m in range(8):
            dense("w_out", m, (RH, 0, H), 8, residual)
        lastx[0] = False
        h_free = [(pe.sem, pe.n)]
        H = normed(xt, lambda k: vecs[:, VG_MLP + k:VG_MLP + k + 1], None, h_free, rstd_summed())
        hx = (RH, 0, H)
        if stop == "mix":
            return finish_program(nc, ctx, locals())

        CA = small[:, 8:16]
        cs = a_act(CA, vecs[:, V_C:V_C + 8], ACT.Sigmoid, cst["vecs"])
        cs = tt(dve, CA, CA, vecs[:, V_C:V_C + 8], ALU.mult, cs)
        MROW = PC[:, 0:3, :]
        adab = banks[7]
        ad = {"n": 0, "out": []}

        def ada_unit():
            u = ad["n"]
            if u >= 48:
                return
            ad["n"] += 1
            n = get("ada", u)
            J, k, half = u // 16, (u % 16) // 2, u % 2
            for c in range(2):
                cc = 2 * half + c
                tok = mm(adab.ap[32 * cc:32 * cc + 1, :], CA[:, k:k + 1], RAW[:, n % NRAW, 512 * c:512 * c + 512],
                         k == 0, k == 7, cs, landed[n], *(adab.free if k == 0 else ()), last=(c == 1), shared=True)
            used(n, tok)
            if u % 16 == 15:
                cps = []
                for cc in range(4):
                    cps.append(copy(dve, MROW[32 * cc:32 * cc + 1, J, :], adab.ap[32 * cc:32 * cc + 1, :], tok, adone,
                                    pct))
                adab.free = [cps[-1]]
                for cc in range(4):
                    ad["out"].append(load(act, t["mod"][4 * J + cc:4 * J + cc + 1, :], MROW[32 * cc:32 * cc + 1, J, :], cps[cc]))

        zz = dve.do(lambda e: e.memset(TB[:, 2, 0:1024], 0.0), adone)
        zx = []
        zsem = sem("zsem")
        RB = list(range(7))
        a_free = [(pe.sem, pe.n)]
        tmpi = [0]
        for f in range(4):
            FT = {}

            def fin1(m, b, tok):
                i_ = tmpi[0] % 2
                tmpi[0] += 1
                r_ = a_act(TMP[:, i_, :], b.ap[:, :], ACT.Relu, tok, tmp_free[i_])
                v_ = tt(dve, TMP[:, 2 + i_, :], TMP[:, i_, :], b.ap[:, :], ALU.mult, r_, tmp_free[2 + i_])
                b.free = [v_]
                tmp_free[i_] = [v_]
                hi, lo = split_to(RA, m % 8, TMP[:, 2 + i_, :], act, pool if i_ else dve, a_free, v_)
                tmp_free[2 + i_] = [hi, lo]
                FT[m % 8] = [hi, lo]
            for m in range(8):
                dense("w_ff1", f * 8 + m, hx, 8, fin1, RB)
                ada_unit()
                if len(zx) < 2 * NUNIT - 16:
                    u = len(zx)
                    dst, u = (t["xs"], u) if u < NUNIT else (t["ys"], u - NUNIT + 16)
                    src = TB[:, 2, 0:1024]
                    zx.append(sp.dma(lambda e, d=dst[128 * u:128 * u + 128, :]: e.dma_start(d, src), zsem,
                                     16 * (2 * NUNIT - 16), zz))
            fa_ = (RA, 0, [FT[k] for k in range(8)])
            lastx[0] = 2 if f == 3 else 0
            for m in range(8):
                dense("w_ff2", f * 8 + m, fa_, 8, lambda mm_, b, tok: residual(mm_ % 8, b, tok), RB)
                if m % 2:
                    ada_unit()
            a_free = [(pe.sem, pe.n)]
        h_free = [(pe.sem, pe.n)]

        md = load(act, TMP[0:48, 0, 0:128], t["mod"].rearrange("a b -> (a b)").rearrange("(m p) -> m p", p=128),
                  ad["out"], tmp_free[0])
        b = bank()
        tok = tr(b.ap[:, 0:48], TMP[0:48, 0, 0:128], md, b.free, last=True)
        tmp_free[0] = [tok]
        ADB = RT[:, 512:560]
        cst["adab"] = load(act, ADB, t["adab"], adone)
        md = tt(dve, modt[:, :], b.ap[:, 0:48], ADB, ALU.add, tok, cst["adab"])
        b.free = [md]
        g1s = stt(gsc[:, 0:8], modt[:, 8:16], small[:, 1:2], vecs[:, VG1:VG1 + 8], ALU.add, ALU.mult, md, one)
        g2s = stt(gsc[:, 8:16], modt[:, 32:40], small[:, 1:2], vecs[:, VG2:VG2 + 8], ALU.add, ALU.mult, md, one)

        r, r2 = rstd_twice()
        for k in range(8):
            xt[k] = stt(X[:, k, :], X[:, k, :], vecs[:, VG_FIN + k:VG_FIN + k + 1], RST, ALU.mult, ALU.mult, r, xt[k])
        rst_free[0] = [xt[7]]
        if stop == "b1":
            return finish_program(nc, ctx, locals())
        dve.need(g1s, md)
        H = normed(xt, lambda k: gsc[:, k:k + 1], lambda k: modt[:, k:k + 1], h_free, r2, RST2)
        hx = (RH, 0, H)
        kz2 = [dve.do(lambda e, i=i: e.memset(M[:, 4 * i:4 * i + 4, :], 0.0), h_free) for i in range(2)]

        QA = PC
        VA = [VV[:, 0, :], VV[:, 1, :], TAB[:, 0, :], TAB[:, 1, :]]
        pcfree = ad["out"]
        q2, k2, v2 = {}, {}, {}

        def fin_q(m, b, tok):
            q2[m] = a_act(QA[:, m, :], b.ap[:, :], ACT.Copy, tok, pcfree, scale=0.125)
            b.free = [q2[m]]

        def fin_z(kz_tok, scale, store):
            def f(m, b, tok):
                a1 = a_act(M[0:64, 2 * m, :], b.ap[0:64, :], ACT.Copy, tok, kz_tok, scale=scale)
                a2 = a_act(M[64:128, 2 * m + 1, :], b.ap[64:128, :], ACT.Copy, tok, kz_tok, scale=scale)
                b.free = [a2]
                store[2 * m], store[2 * m + 1] = a1, a2
            return f

        def fin_v(i, b, tok):
            v2[i] = copy(dve, VA[i], b.ap[:, :], tok, vfree)
            b.free = [v2[i]]

        vfree = [h_free]
        for u in range(4):
            dense("w2_qa", u, hx, 8, fin_q)
        FR = TMP
        nf = {}

        def fin_fa(u, b, tok):
            y = a_act(FR[0:8, 0, :], b.ap[0:8, :], ACT.Identity, tok, tmp_free[0], cst["vecs"],
                      bias=vecs[0:8, V_BF:V_BF + 1])
            b.free = [y]
            ab = a_act(FR[0:8, 1, :], FR[0:8, 0, :], ACT.Abs, y, tmp_free[1])
            ex = a_act(FR[0:8, 1, :], FR[0:8, 1, :], ACT.Exp, ab, scale=-1.0)
            ln = a_act(FR[0:8, 1, :], FR[0:8, 1, :], ACT.Ln, ex, one, bias=small[0:8, 1:2])
            nm = ts(dve, FR[0:8, 0, :], FR[0:8, 0, :], -1.0, ALU.mult, ab, s2=0.0, op1=ALU.max)
            sm_ = tt(dve, FR[0:8, 2, :], FR[0:8, 0, :], FR[0:8, 1, :], ALU.add, nm, ln, tmp_free[2])
            z_ = dve.do(lambda e: e.memset(FR[0:8, 0, :], 0.0), sm_)
            sc = dve.do(lambda e: e.tensor_tensor_scan(FR[0:8, 3, :], FR[0:8, 2, :], FR[0:8, 0, :], 0.0,
                                                       ALU.add, ALU.add), sm_, z_, tmp_free[3])
            nf["d"] = load(act, t["nf"], FR[0:8, 3, :], sc)
            for i in range(4):
                tmp_free[i] = [sc, nf["d"]]
        dense("w2_fa", 0, hx, 8, fin_fa)
        for u in range(4):
            dense("w2_ka", u, hx, 8, fin_z(kz2, 1.0, k2))
        dense_rows("w2_va", 4, hx, fin_v, [0, 1, 2, 3])

        FB = [TMP[:, 0, :], TMP[:, 1, :]]
        fbl = {}
        fbfree = {0: [], 1: []}

        def fb_load(n):
            fbl[n] = load(sp, FB[n % 2], t["nf"][n:n + 1, :].broadcast_to([128, 512]), nf["d"], tmp_free[n % 2],
                          fbfree[n % 2])

        fb_load(0)

        def fox_add(n):
            def done(tok):
                fbfree[n % 2] = [tok]
            if n + 1 < 8:
                fb_load(n + 1)
            return FB[n % 2], fbl[n], done

        def fox_done(m, b, tok):
            if m % 2 == 1:
                RAT[m // 2] = list(split_to(RA, m // 2, b.ap[:, :], act, dve, a_free, tok))
                b.free = RAT[m // 2]

        adone2 = attention(
            8, lambda n, i: QA[:, n // 2, 128 * i:128 * i + 128],
            lambda n: M[:, n, :], lambda n: [q2[n // 2], k2[n]], fox_add, None,
            lambda m, j: (VA[j][:, 64 * m:64 * m + 64], v2[j]),
            lambda m: (banks[7], 64 * (m % 2)), lambda m, b: True, fox_done, [h_free])
        for i in range(2):
            tmp_free[i] = [tmp_free[i], fbfree[i]]
        if stop == "fox":
            return finish_program(nc, ctx, locals())

        pcfree = adone2
        vfree = adone2
        KB = PC
        kb2, qz2 = {}, {}

        def fin_kb(m, b, tok):
            kb2[m] = a_act(KB[:, m, :], b.ap[:, :], ACT.Copy, tok, adone2)
            b.free = [kb2[m]]
        for u in range(4):
            dense("w2_qb", u, hx, 8, fin_z(adone2, 0.125, qz2))
        for u in range(4):
            dense("w2_kb", u, hx, 8, fin_kb)
        dense_rows("w2_vb", 4, hx, fin_v, [0, 1, 2, 3])

        sets = [[0, 1, 2], [3, 4, 5]]
        place = [(0, 0), (1, 0), (2, 0), (1, 384)]
        zsp, zst = {}, {}
        spf, taf = [adone2] * 2, [adone2] * 3
        segs = [(0, 0, 512), (1, 512, 512), (2, 1024, 256)]
        ABT = TMP[:, :, :].rearrange("p a n -> p (a n)")[:, 0:1280]
        abf = [tmp_free[0], tmp_free[1], tmp_free[2]]
        avt = {}
        for n in range(10):
            if n < 8:
                h, pr = n, n // 2
                bs = [banks[i] for i in sets[n % 2]]
                SPt = PB[:, n % 2, :]
                for j in (0, 1, 3, 2):
                    bi, o = place[j]
                    w = 512 - 128 * j
                    tok = mm(bs[bi].ap[:, o:o + w], KB[:, pr, 128 * j:128 * j + 128], M[:, h, 128 * j:512],
                             o == 0, False, kb2[pr], qz2[h], *(bs[bi].free if o == 0 else ()), last=True,
                             shared=True)
                ab = []
                for bi, o, w in segs:
                    ab.append(a_act(ABT[:, o:o + w], bs[bi].ap[:, 0:w], ACT.Abs, tok, abf))
                ex = a_act(ABT, ABT, ACT.Exp, ab, scale=-1.0)
                ln = a_act(ABT, ABT, ACT.Ln, ex, one, bias=small[:, 1:2])
                sps = []
                for bi, o, w in segs:
                    sps.append(stt(SPt[:, o:o + w], bs[bi].ap[:, 0:w], 0.0, ABT[:, o:o + w], ALU.max, ALU.add,
                                   ln, tok, spf[n % 2]))
                abf = [sps[-1]]
                mk = []
                for j in range(4):
                    o = PACK[j]
                    mk.append(tt(pool, SPt[:, o:o + 128], SPt[:, o:o + 128], sltm[:, :], ALU.mult, sps,
                                 cst["sltm"]))
                zsp[n], zst[n] = (sps, mk), bs
            if 1 <= n <= 8:
                m = n - 1
                bs = zst[m]
                SPt, TAt = PB[:, m % 2, :], TB[:, m % 3, :]
                sps, mk = zsp[m]
                av = []
                for j in (0, 1, 3, 2):
                    bi, o = place[j]
                    w = 512 - 128 * j
                    mm(bs[bi].ap[:, o:o + w], ntri[:, :], SPt[:, PACK[j]:PACK[j] + w], False, False, mk, sps,
                       cst["ntri"], cst["nones"], shared=True)
                    for jj in range(j + 1, 4):
                        w2 = 512 - 128 * jj
                        mm(bs[bi].ap[:, o + 128 * (jj - j):o + w], nones[:, :], SPt[:, PACK[jj]:PACK[jj] + w2],
                           False, False, shared=True)
                    tok = mm(bs[bi].ap[:, o:o + 128], identb[:, :], maskt[:, :], False, True, cst["maskt"],
                             last=True, shared=True)
                    if j == 1:
                        continue
                    bi, o, w = segs[bi]
                    av.append(a_act(TAt[:, o:o + w], bs[bi].ap[:, 0:w], ACT.Exp, tok, taf[m % 3]))
                    bs[bi].free = [av[-1]]
                spf[m % 2] = [tok]
                avt[m] = av
            if n >= 3 and n % 2 == 1:
                b = banks[6 + (n // 2) % 2]
                for j in range(4):
                    for m in (n - 3, n - 2):
                        r0 = 64 * (m % 2)
                        tok = mm(b.ap[r0:r0 + 64, 128 * j:512], VA[j][:, 64 * m:64 * m + 64],
                                 TB[:, m % 3, PACK[j]:PACK[j] + 512 - 128 * j], j == 0, False, avt[m], v2[j],
                                 *(b.free if j == 0 else ()), last=True, shared=True)
                taf[(n - 3) % 3] = taf[(n - 2) % 3] = [tok]
                k = 4 + (n - 3) // 2
                RAT[k] = list(split_to(RA, k, b.ap[:, :], act, dve, a_free, tok))
                b.free = RAT[k]
        for i in range(3):
            tmp_free[i] = abf
        sdone = spf + taf + [(act.sem, act.n), (dve.sem, dve.n)]
        if stop == "sb":
            return finish_program(nc, ctx, locals())

        fo, so = (RA, 0, [RAT[k] for k in range(4)]), (RA, 4, [RAT[4 + k] for k in range(4)])
        for m in range(0, 8, 2):
            dense("w2_ga", m, hx, 8, gate_fin(gt))
            dense("w2_ga", m + 1, hx, 8, gate_fin(gt))
            dense("w2_fox", m // 2, fo, 4, merge_fin(True, sdone))
            dense("w2_gb", m, hx, 8, gate_fin(gt))
            dense("w2_gb", m + 1, hx, 8, gate_fin(gt))
            dense("w2_sb", m // 2, so, 4, merge_fin(False, None))
        h_free = [(pe.sem, pe.n)]
        H = [list(split_to(RH, k, M[:, k, :], act, pool if k % 2 else dve, h_free, mtok[k])) for k in range(8)]

        def residual2(m, b, tok):
            o = stt(X[:, m, :], b.ap[:, :], modt[:, 16 + m:17 + m], X[:, m, :], ALU.mult, ALU.add, tok, xt[m], md)
            b.free = [o]
            xt[m] = o
            square_in(m, o)
        for m in range(8):
            dense("w2_out", m, (RH, 0, H), 8, residual2)
        if stop == "mix2":
            return finish_program(nc, ctx, locals())

        r = rstd_summed()
        ht = []
        for k in range(8):
            w = stt(M[:, k, :], X[:, k, :], gsc[:, 8 + k:9 + k], RST, ALU.mult, ALU.mult, r, xt[k], g2s, H[k])
            ht.append(ts(dve, M[:, k, :], M[:, k, :], modt[:, 24 + k:25 + k], ALU.add, w, md))
        RW = TAB[:, 0, 0:160]
        cst["rw"] = load(act, RW, t["rw"], sdone)
        b = bank()
        for k in range(8):
            tok = mm(b.ap[0:20, :], RW[:, 20 * k:20 * k + 20], M[:, k, :], k == 0, k == 7, ht[k], cst["rw"], b.free,
                     last=(k == 7))
        LT = TMP[0:20, 0, :]
        l1 = a_act(LT, b.ap[0:20, :], ACT.Identity, tok, tmp_free[0], bias=vecs[0:20, V_BF + 1:V_BF + 2])
        b.free = [l1]
        b = bank()
        for i in range(4):
            tok = tr(b.ap[:, 20 * i:20 * i + 20], TMP[0:20, 0, 128 * i:128 * i + 128], l1, b.free, last=(i == 3))
        XT_ = [VV, TAB]
        pos_rows = []
        vt_free = {0: [sdone], 1: [sdone, cst["rw"], tok]}
        HT4 = {}

        def rows_of(i):
            bb = [banks[2 * (i % 2) + 4 * 0], banks[2 * (i % 2) + 1]]
            dst = (PB, TB)[i // 2][:, i % 2, 0:1024]
            cps = []
            for hf in range(2):
                for k in range(4):
                    tk = tr(bb[hf].ap[:, 128 * k:128 * k + 128], M[:, 4 * hf + k, 128 * i:128 * i + 128],
                            ht[4 * hf + k], bb[hf].free, last=(k == 3))
                c = copy(act if hf else dve, dst[:, 512 * hf:512 * hf + 512], bb[hf].ap[:, :], tk, sdone)
                bb[hf].free = [c]
                cps.append(c)
            return dst, cps
        LG = RT[:, 560:640]
        LG3 = LG.rearrange("p (i n) -> p i n", n=20)
        c0 = copy(dve, LG, b.ap[:, 0:80], tok)
        b.free = [c0]
        hrows = [rows_of(i) for i in range(4)]

        R_ = TMP[:, 1:4, :].rearrange("p a n -> p (a n)")
        ro = [0]

        def reg(n):
            a = R_[:, ro[0]:ro[0] + n]
            ro[0] += n
            return a
        w0 = [tmp_free[1], tmp_free[2], tmp_free[3]]
        dve.need(w0)
        last = [c0]

        def v(fn):
            last[0] = dve.do(fn, last[0])
            return last[0]

        def vtt(o, a, b_, op):
            return v(lambda e: e.tensor_tensor(o, a, b_, op))

        W4_ = RW4 = VV[:, 0, 0:64]
        cst["rk"] = load(act, VV[:, 0, 0:64], t["rk"], sdone)
        dve.need(cst["rk"])
        RK4 = VV[:, 0, 0:16].rearrange("p (i n) -> p i n", n=4)
        E128 = VV[:, 0, 16:32]
        JJ = VV[:, 0, 32:39]

        def b3(a, n):
            return a.unsqueeze(2).broadcast_to([128, 4, n])

        def first_max(src, n):
            mx, oh, m2 = reg(4), reg(16), reg(4)
            oh3 = oh.rearrange("p (i n) -> p i n", n=4)
            v(lambda e: e.reduce_max(mx, src, AX))
            vtt(oh3, src, b3(mx, 4), ALU.is_equal)
            vtt(oh3, oh3, RK4, ALU.mult)
            v(lambda e: e.reduce_max(m2, oh3, AX))
            vtt(oh3, oh3, b3(m2, 4), ALU.is_equal)
            return mx, oh3
        G3, E3 = LG3[:, :, 0:4], LG3[:, :, 4:20]
        gm, gh = first_max(G3, 4)
        gx = reg(16).rearrange("p (i n) -> p i n", n=4)
        gs = reg(4)
        vtt(gx, G3, b3(gm, 4), ALU.subtract)
        last[0] = a_act(gx, gx, ACT.Exp, last[0])
        v(lambda e: e.reduce_sum(gs, gx, AX))
        v(lambda e: e.reciprocal(gs, gs))
        em = reg(64)
        es = reg(16).rearrange("p (i n) -> p i n", n=4)
        em4 = em.rearrange("p (i g e) -> p i g e", i=4, g=4)
        E4 = E3.rearrange("p i (g e) -> p i g e", g=4)
        vtt(em4, E4, gh.unsqueeze(3).broadcast_to([128, 4, 4, 4]), ALU.mult)
        v(lambda e: e.reduce_sum(es, em4.rearrange("p i g e -> p i e g"), AX))
        m1, o1 = first_max(es, 4)
        e2_ = reg(16).rearrange("p (i n) -> p i n", n=4)
        v(lambda e: e.scalar_tensor_tensor(e2_, o1, NEG, es, ALU.mult, ALU.add))
        m2, o2 = first_max(e2_, 4)
        ex = reg(16).rearrange("p (i n) -> p i n", n=4)
        vtt(ex, es, b3(m1, 4), ALU.subtract)
        last[0] = a_act(ex, ex, ACT.Exp, last[0])
        zs = reg(4)
        v(lambda e: e.reduce_sum(zs, ex, AX))
        v(lambda e: e.reciprocal(zs, zs))
        vtt(ex, ex, b3(zs, 4), ALU.mult)
        pk = reg(8).rearrange("p (k i) -> p k i", k=2)
        px = reg(16).rearrange("p (i n) -> p i n", n=4)
        for kk, oo in enumerate((o1, o2)):
            vtt(px, ex, oo, ALU.mult)
            v(lambda e, o=pk[:, kk, :]: e.reduce_sum(o, px, AX))
        ps_ = reg(4)
        vtt(ps_, pk[:, 0, :], pk[:, 1, :], ALU.add)
        v(lambda e: e.reciprocal(ps_, ps_))
        vtt(ps_, ps_, gs, ALU.mult)
        WK = RT[:, 640:648].rearrange("p (k i) -> p k i", k=2)
        for kk in range(2):
            vtt(WK[:, kk, :], pk[:, kk, :], ps_, ALU.mult)
        wk_tok = last[0]
        OE = [reg(64), reg(64)]
        for kk, oo in enumerate((o1, o2)):
            vtt(OE[kk].rearrange("p (i g e) -> p i g e", i=4, g=4), gh.unsqueeze(3).broadcast_to([128, 4, 4, 4]),
                oo.unsqueeze(2).broadcast_to([128, 4, 4, 4]), ALU.mult)
        MB = sb("MB", [128, 80], BF16)
        vtt(MB[:, 0:64], OE[0], OE[1], ALU.add)
        b = bank(list(range(4, 8)))
        mbt = last[0]
        for i in range(4):
            for ii in range(i + 1):
                mm(b.ap[:, 16 * i:16 * i + 16], trib[:, :] if ii == i else onesb[:, :],
                   MB[:, 16 * ii:16 * ii + 16], ii == 0 and i == 0, False, mbt, cst["trib"], cst["onesb"], b.free,
                   shared=True)
        for ii in range(4):
            tok = mm(b.ap[:, 64:80], onesb[:, :], MB[:, 16 * ii:16 * ii + 16], False, ii == 3, last=(ii == 3),
                     shared=True)
        rank = reg(80)
        last[0] = copy(dve, rank, b.ap[:, 0:80], tok)
        b.free = [last[0]]
        NE = rank[:, 64:80]
        xe, xa, xi = reg(16), reg(16), reg(16)
        v(lambda e: e.tensor_scalar(xe, NE, 128.5, None, ALU.is_gt))
        for lim in (256.5, 384.5):
            v(lambda e, lim=lim: e.scalar_tensor_tensor(xe, NE, lim, xe, ALU.is_gt, ALU.add))
        v(lambda e: e.memset(xa, 0.0))
        v(lambda e: e.tensor_tensor_scan(xi, xe, xa, 0.0, ALU.add, ALU.add))
        base = reg(16)
        vtt(base, xi, xe, ALU.subtract)
        v(lambda e: e.tensor_scalar(base, base, 128.0, 1920.0, ALU.mult, ALU.add))
        vtt(base, base, E128, ALU.subtract)
        vl = reg(64)
        POSF = reg(8)
        R3, V3 = rank[:, 0:64].rearrange("p (i e) -> p i e", i=4), vl.rearrange("p (i e) -> p i e", i=4)
        v(lambda e: e.scalar_tensor_tensor(V3, R3, 127.5, base.unsqueeze(1).broadcast_to([128, 4, 16]),
                                           ALU.is_gt, ALU.mult))
        vtt(V3, V3, R3, ALU.add)
        vtt(V3, V3, E128.unsqueeze(1).broadcast_to([128, 4, 16]), ALU.add)
        for kk in range(2):
            vtt(OE[kk], OE[kk], vl, ALU.mult)
            v(lambda e, kk=kk: e.reduce_sum(POSF[:, 4 * kk:4 * kk + 4], OE[kk].rearrange("p (i n) -> p i n", n=16), AX))
        POS = sb("POS", [128, 8], U32)
        pos_t = v(lambda e: e.tensor_copy(POS[:, :], POSF))
        EXI = sb("EXI", [1, 8], I32)
        ej, cj = reg(8), reg(112).rearrange("p (j e) -> p j e", j=7)
        v(lambda e: e.tensor_tensor(cj[0:1], xi[0:1, :].unsqueeze(1).broadcast_to([1, 7, 16]),
                                    JJ[0:1, :].unsqueeze(2).broadcast_to([1, 7, 16]), ALU.is_lt))
        v(lambda e: e.reduce_sum(ej[0:1, 0:7], cj[0:1], AX))
        v(lambda e: e.tensor_scalar(ej[0:1, 0:7], ej[0:1, 0:7], 15.0, None, ALU.min))
        v(lambda e: e.tensor_copy(ej[0:1, 7:8], xi[0:1, 15:16]))
        late["tok"] = v(lambda e: e.tensor_copy(EXI[0:1, 0:8], ej[0:1, 0:8]))
        sct = []
        for i in range(4):
            for kk in range(2):
                counter[0] += 1
                s = sem(f"d{counter[0]}")
                c = 4 * kk + i
                sct.append(pool.dma(lambda e, c=c, i=i: e.indirect_dma_start(
                    t["xs"], bass.IndirectOffsetOnAxis(ap=POS[:, c:c + 1], axis=0), hrows[i][0], None),
                    s, 16, pos_t, hrows[i][1], zx))
        G2B, GFB = TB[:, 0, 0:1024], TB[:, 1, 0:1024]
        if stop == "route":
            return finish_program(nc, ctx, locals())

        lo_engine[0] = lambda n: pool if n % 3 == 2 else dve
        xin = [PB[:, 0, 0:1024], PB[:, 1, 0:1024]]
        yout = [TB[:, 0, 0:1024], TB[:, 1, 0:1024]]
        xin_f, yout_f = [sct, sct], [sct, sct]
        XH = [RH[:, :, 0:2, :], RH[:, :, 2:4, :]]
        AH = [RH[:, :, 4, :], RH[:, :, 5, :]]
        hfree = [(pe.sem, pe.n)]
        xh_f, ah_f = [hfree, hfree], [hfree, hfree]
        GU = [PC[:, 0, :], PC[:, 1, :]]
        gu_f = [sdone, sdone]
        xl, xht, aht, yst = {}, {}, {}, []

        def load_x(u):
            xl[u] = load_slot(act, f"x{u % 2}{u // 16}", xin[u % 2], t["xs"][128 * u:128 * u + 128, :], sct, xin_f[u % 2])

        def prep(u):
            tk = []
            for hf in range(2):
                b = banks[hf]
                for k in range(4):
                    c = (4 * hf + k) * 128
                    tok = tr(b.ap[:, 128 * k:128 * k + 128], xin[u % 2][:, c:c + 128], xl[u], b.free, last=(k == 3))
                d = XH[u % 2]
                hi = copy(act, d[:, 0, hf, :], b.ap[:, :], tok, xh_f[u % 2])
                lo = tt(dve, d[:, 1, hf, :], b.ap[:, :], hiF(d[:, 0, hf, :]), ALU.subtract, hi, xh_f[u % 2])
                b.free = [lo]
                tk.append([hi, lo])
            xin_f[u % 2] = [tok]
            xht[u] = tk

        def up(u, name, b):
            d = XH[u % 2]
            for c in range(4):
                n = get(name, (u, c))
                s, lo_t, hi_t = parts[n]
                for kk in range(2):
                    k = 2 * c + kk
                    xh, xlo = (d[:, x, k // 4, 128 * (k % 4):128 * (k % 4) + 128] for x in (0, 1))
                    wh, wl = (RS[:, s, x, 512 * kk:512 * kk + 512] for x in (0, 1))
                    mm(b.ap[:, :], xh, wh, k == 0, False, hi_t, xht[u][k // 4], *(b.free if k == 0 else ()))
                    mm(b.ap[:, :], xlo, wh, False, False)
                    tok = mm(b.ap[:, :], xh, wl, False, k == 7, lo_t, last=(kk == 1))
                used(n, tok)
            return tok

        def down(u):
            bb = [banks[5], banks[6]]
            d = AH[u % 2]
            for c in range(4):
                n = get("w_down", (u, c))
                s, lo_t, hi_t = parts[n]
                for hf in range(2):
                    b = bb[hf]
                    xh, xlo = (d[:, x, 128 * c:128 * c + 128] for x in (0, 1))
                    wh, wl = (RS[:, s, x, 512 * hf:512 * hf + 512] for x in (0, 1))
                    mm(b.ap[:, :], xh, wh, c == 0, False, hi_t, aht[u], *(b.free if c == 0 else ()))
                    mm(b.ap[:, :], xlo, wh, False, False)
                    tok = mm(b.ap[:, :], xh, wl, False, c == 3, lo_t, last=True)
                    if c == 3:
                        cp = copy(act if hf else dve, yout[u % 2][:, 512 * hf:512 * hf + 512], b.ap[:, :], tok,
                                  yout_f[u % 2])
                        b.free = [cp]
                        cps.append(cp)
                used(n, tok)
            ah_f[u % 2] = [tok]
            yst.append(load_slot(act, f"y{u % 2}{u // 16}", t["ys"][128 * u:128 * u + 128, :], yout[u % 2], cps[-2:], zx))
            yout_f[u % 2] = [yst[-1]]

        cps = []

        def experts(u0, u1):
            load_x(u0)
            load_x(u0 + 1)
            prep(u0)
            for u in range(u0, u1):
                tg = up(u, "w_gate", banks[2])
                G_ = GU[u % 2]
                s1 = a_act(G_, banks[2].ap[:, :], ACT.Silu, tg, gu_f[u % 2])
                banks[2].free = [s1]
                if u + 1 < u1:
                    prep(u + 1)
                tu = up(u, "w_up", banks[3])
                xh_f[u % 2] = [tu]
                s2 = tt(dve, G_, G_, banks[3].ap[:, :], ALU.mult, s1, tu)
                banks[3].free = [s2]
                if u + 2 < u1:
                    load_x(u + 2)
                if u > u0:
                    down(u - 1)
                b = banks[4]
                for k in range(4):
                    tok = tr(b.ap[:, 128 * k:128 * k + 128], G_[:, 128 * k:128 * k + 128], s2, b.free, last=(k == 3))
                gu_f[u % 2] = [tok]
                hi = copy(act, AH[u % 2][:, 0, :], b.ap[:, :], tok, ah_f[u % 2])
                lo = tt(dve, AH[u % 2][:, 1, :], b.ap[:, :], hiF(AH[u % 2][:, 0, :]), ALU.subtract, hi, ah_f[u % 2])
                b.free = [lo]
                aht[u] = [hi, lo]
            down(u1 - 1)

        experts(0, 16)
        base_st = list(yst)
        queues = (pe, act, dve, pool, sp)
        for q in queues:
            q.branch(EXI[0:1, 7:8], late["tok"])
        yst.clear()
        experts(16, NUNIT)
        sp.need([tuple(slots[k]) for k in ("x01", "x11", "y01", "y11")], [(x, 16 * ((len(plan) - i + NRAW - 1) // NRAW)) for i, x in enumerate(raw_sem)])
        for q in queues:
            q.join()
        yst = [sp.bump(), base_st]
        yout_f = [yst, yst]

        g2r = load(act, M[:, 0:2, :], t["mod"][10:12, :].rearrange("a b -> (a b)").rearrange("(o a b) -> o a b", o=1, a=2)
                   .broadcast_to([128, 2, 512]), ht, [h[1] for h in hrows])
        g2b = load(act, M[:, 2:4, :], t["g2b"].rearrange("(o a b) -> o a b", o=1, a=2).broadcast_to([128, 2, 512]), ht)
        gfb = load(act, M[:, 4:6, :], t["final_g"].rearrange("(o a b) -> o a b", o=1, a=2).broadcast_to([128, 2, 512]), ht)
        g2 = tt(dve, M[:, 0:2, :], M[:, 0:2, :], M[:, 2:4, :], ALU.add, g2r, g2b)
        G2 = M[:, 0:2, :].rearrange("p a b -> p (a b)")
        GF = M[:, 4:6, :].rearrange("p a b -> p (a b)")
        outs = []
        bufs = [[PC[:, 0:2, :], PC[:, 2:4, :]], [TMP[:, 0:2, :], TMP[:, 2:4, :]]]
        bufs = [[x.rearrange("p a b -> p (a b)") for x in p_] for p_ in bufs]
        bufs += [[PB[:, 0, 0:1024], PB[:, 1, 0:1024]], [TB[:, 0, 0:1024], TB[:, 1, 0:1024]]]
        yall = [yst, gu_f, xin_f, yout_f, [(act.sem, act.n), (dve.sem, dve.n), (pe.sem, pe.n)]]
        gat = {}
        for i in range(4):
            for kk in range(2):
                counter[0] += 1
                s = sem(f"d{counter[0]}")
                c = 4 * kk + i
                gat[i, kk] = pool.dma(lambda e, c=c, d=bufs[i][kk]: e.indirect_dma_start(
                    d, None, t["ys"], bass.IndirectOffsetOnAxis(ap=POS[:, c:c + 1], axis=0)), s, 16, yall)
        fin = {}
        for i in range(5):
            if i < 4:
                A_, B_ = bufs[i]
                bb = [banks[2 * (i % 4)], banks[2 * (i % 4) + 1]]
                for hf in range(2):
                    for k in range(4):
                        tk = tr(bb[hf].ap[:, 128 * k:128 * k + 128], X[:, 4 * hf + k, 128 * i:128 * i + 128],
                                xt[4 * hf + k], bb[hf].free, last=(k == 3))
                y1 = a_act(A_, A_, ACT.Copy, gat[i, 0], wk_tok, scale=WK[:, 0, i:i + 1])
                y2 = stt(A_, B_, WK[:, 1, i:i + 1], A_, ALU.mult, ALU.add, y1, gat[i, 1])
                y3 = tt(pool if i > 1 else dve, A_, A_, G2, ALU.mult, y2, g2)
                y4 = []
                for hf in range(2):
                    y4.append(tt(dve, A_[:, 512 * hf:512 * hf + 512], A_[:, 512 * hf:512 * hf + 512],
                                 bb[hf].ap[:, :], ALU.add, y3, tk))
                ss = small[:, 16 + i:17 + i]
                q1 = a_act(B_, A_, ACT.Square, y4, accum_out=ss)
                fin[i] = a_act(ss, ss, ACT.Sqrt, q1, bias=small[:, 0:1], scale=1.0 / D)
            if i >= 1:
                A_, B_ = bufs[i - 1]
                ss = small[:, 15 + i:16 + i]
                q3 = dve.do(lambda e, ss=ss: e.reciprocal(ss, ss), fin[i - 1])
                q4 = stt(B_, A_, ss, GF, ALU.mult, ALU.mult, q3, gfb)
                outs.append(load(sp, t["out"][0, 128 * (i - 1):128 * i, :], B_, q4))
        sp.need(outs, yst, every, [(x, 16 * ((always - i + NRAW - 1) // NRAW)) for i, x in enumerate(raw_sem)])
        return finish_program(nc, ctx, locals())


def finish_program(nc, ctx, env):
    sp, pe, act, dve, pool = (env[n] for n in ("sp", "pe", "act", "dve", "pool"))
    if env["stop"] is not None:
        for q in (pe, act, dve, pool):
            sp.need((q.sem, q.n))
        sp.need(env["every"])
        sp.need([(x, 16 * ((env["st"]["load"] - i + 4) // 5)) for i, x in enumerate(env["raw_sem"])])
        if "sct" in env:
            sp.need(env["sct"])
        fin = ctx.enter_context(nc.semaphore("s_fin"))
        o = env["t"]["out"][0, 0:128, 0:128]
        sp.dma(lambda e: e.dma_start(o, env["identf"][:, :]), fin, 16)
        sp.need((fin, 16))
    block = ctx.enter_context(nc.Block())
    for q, name in ((sp, "sync"), (pe, "tensor"), (act, "scalar"), (dve, "vector"), (pool, "gpsimd")):
        def body(eng, q=q):
            q.emit(eng)
        {"sync": block.sync, "tensor": block.tensor, "scalar": block.scalar, "vector": block.vector,
         "gpsimd": block.gpsimd}[name](body)


def tiles(w, pad=0):
    w = np.asarray(w)
    if pad:
        w = np.concatenate([w, np.zeros((w.shape[0], pad), w.dtype)], axis=1)
    K, N = w.shape[0] // 128, w.shape[1] // 128
    per = 8 // K
    a = w.reshape(K, 128, N // per, per, 128).transpose(2, 1, 3, 0, 4)
    return np.ascontiguousarray(a).reshape(N // per, 128, 1024)


def rows(w):
    w = np.asarray(w)
    K = w.shape[0] // 256
    return np.ascontiguousarray(w.reshape(K, 2, 128, 512).transpose(0, 2, 1, 3)).reshape(K, 128, 1024)


def cols(v, n):
    return np.asarray(v).reshape(n, 128).T


def constants():
    f = np.float32
    c = {}
    c["identf"] = np.eye(128, dtype=f)
    r = np.zeros((128, 128), f)
    for b in range(2):
        for d in range(64):
            if d < 32:
                r[64 * b + d + 32, 64 * b + d] = -1
            else:
                r[64 * b + d - 32, 64 * b + d] = 1
    c["rotT"] = r
    c["onesf"] = np.ones((128, 128), f)
    i, j = np.arange(128)[:, None], np.arange(128)[None, :]
    c["ntri"] = -(i >= j).astype(f)
    c["nones"] = -np.ones((128, 128), f)
    c["sltm"] = (i < j).astype(f)
    c["maskb"] = np.where(j > i, NEG, 0.0).astype(f)
    c["maskt"] = np.where(i >= j, NEG, 0.0).astype(f)
    inv = np.power(f(10000.0), -np.arange(0, 64, 2, dtype=f) / f(64)).astype(f)

    def table(pos):
        ang = (pos.astype(f)[:, None] * inv[None, :]).astype(f)
        ang = np.concatenate([ang, ang], axis=-1)
        return np.cos(ang).T.astype(f), np.sin(ang).T.astype(f)
    co, si = table(np.arange(S))
    c["tab"] = np.stack([np.concatenate([co, co]), np.concatenate([si, si])], axis=1)
    co, si = table(np.arange(CMP) * 16 + 31)
    c["ctb"] = np.concatenate([np.tile(co, (2, 2)), np.tile(si, (2, 2))], axis=1)
    tt_ = np.arange(S).reshape(4, 128).T[:, :, None]
    n = np.arange(32)[None, None, :]
    c["mcb"] = np.where((16 * n + 31 > tt_) | (n == 31), NEG, 0.0).astype(f).reshape(128, 128)
    c["ict"] = np.tile(np.concatenate([1.0 / np.minimum(np.arange(16) + 1, w) for w in (2, 4, 8, 16)]).astype(f), (128, 1))
    rk = np.zeros((128, 64), f)
    rk[:, 0:16] = np.tile(np.array([4, 3, 2, 1], f), 4)
    rk[:, 16:32] = 128 * np.arange(16)
    rk[:, 32:39] = np.arange(7) + 0.5
    c["rk"] = rk
    return c


def layout(i):
    a = {}
    a["xT"] = np.ascontiguousarray(np.asarray(i["x"])[0].T.reshape(8, 128, S).transpose(1, 0, 2))
    w = np.asarray(i["w_in"])[0]
    u, q, kc, vc, ks, vs, kw, vw, g, gm = np.split(w, np.cumsum([512, 1024, 128, 128, 128, 128, 128, 128, 48]), axis=1)
    a["w_qkv"] = tiles(np.concatenate([q, ks, kw, kc, vc, vs, vw, g], axis=1), pad=80)
    ck = [np.asarray(i[n])[0].reshape(4, 4, 128, 256).transpose(0, 2, 1, 3).reshape(4, 128, 1024)
          for n in ("w_ck1", "w_cv1")]
    a["w_c"] = np.concatenate(ck)
    c2 = np.asarray(i["w_ck2"])[0].reshape(2, 128, 64).transpose(1, 0, 2)
    v2 = np.asarray(i["w_cv2"])[0].reshape(2, 128, 64).transpose(1, 0, 2)
    a["cw2"] = np.concatenate([c2, c2, v2], axis=2)
    a["pe2"] = np.concatenate([np.asarray(i[n])[0].reshape(16, 128).T for n in ("pe_k", "pe_v")], axis=1)
    a["w_ga"], a["w_gb"] = tiles(gm[:, :1024]), tiles(gm[:, 1024:])
    a["w_nsa"] = tiles(i["w_proj_nsa"][0])
    a["w_u"] = tiles(u)
    a["w_pool"] = np.ascontiguousarray(np.asarray(i["w_pool"])[0].transpose(1, 0, 2).reshape(128, 512))
    a["w_pp"] = tiles(i["w_proj_pool"][0])
    a["w_out"] = tiles(i["w_out"][0])
    a["w_ff1"] = tiles(i["w_ff1"][0])
    f2 = np.asarray(i["w_ff2"])[0]
    a["w_ff2"] = np.concatenate([tiles(f2[1024 * f:1024 * f + 1024]) for f in range(4)])
    aw = np.asarray(i["ada_w_2"])[0].reshape(8, 128, 3, 2, 1024).transpose(2, 0, 3, 1, 4)
    a["ada"] = np.ascontiguousarray(aw).reshape(48, 128, 1024)
    a["adab"] = cols(i["ada_b_2"][0], 48)
    a["g2b"] = np.asarray(i["ada_b_2"])[0, 5120:6144]
    w = np.asarray(i["w_in_2"])[0]
    sp_ = np.split(w, [512, 1024, 1536, 1544, 2056, 2568, 3080, 4104], axis=1)
    for n, x in zip(("qa", "ka", "va", "fa", "qb", "kb", "vb", "ga", "gb"), sp_):
        a["w2_" + n] = rows(x) if n in ("va", "vb") else tiles(x, pad=120 if n == "fa" else 0)
    a["w2_fox"], a["w2_sb"] = tiles(i["w_branch_fox_2"][0]), tiles(i["w_branch_sb_2"][0])
    a["w2_out"] = tiles(i["w_out_2"][0])
    vec = np.zeros((128, 64), np.float32)
    vec[:, 0:8], vec[:, 8:16] = cols(i["norm_mix"][0], 8), cols(i["norm_mlp"][0], 8)
    vec[:, 16:24], vec[:, 24:28] = cols(i["norm_final"], 8), cols(i["pool_scale"][0], 4)
    vec[:, 28:36], vec[:, 36:44] = cols(i["norm1_g_2"][0], 8), cols(i["norm2_g_2"][0], 8)
    vec[:, 44:52] = cols(i["c_2"][0], 8)
    vec[0:8, 52] = np.asarray(i["b_forget_2"])[0]
    vec[0:4, 53], vec[4:20, 53] = np.asarray(i["router_group_b_2"])[0], np.asarray(i["router_expert_b_2"])[0]
    a["vecs"] = vec
    rw = np.concatenate([np.asarray(i["router_group_w_2"])[0], np.asarray(i["router_expert_w_2"])[0]], axis=1)
    a["rw"] = rw.reshape(8, 128, 20).transpose(1, 0, 2).reshape(128, 160)
    for n, k in (("w_gate", "expert_w_gate_2"), ("w_up", "expert_w_up_2")):
        x = np.asarray(i[k])[0].reshape(16, 4, 2, 128, 512).transpose(0, 1, 3, 2, 4)
        a[n] = np.ascontiguousarray(x).reshape(16, 4, 128, 1024)
    a["w_down"] = np.asarray(i["expert_w_down_2"])[0].reshape(16, 4, 128, 1024)
    a["final_g"] = np.asarray(i["final_g_2"])
    a.update(constants())
    return {k: np.ascontiguousarray(v) for k, v in a.items()}


def build(nc, arrays, stop=None):
    t = {}
    for name, a in arrays.items():
        t[name] = nc.dram_tensor(f"in_{name}", a.shape, mybir.dt.from_np(a.dtype), kind="ExternalInput").ap()
    t["out"] = nc.dram_tensor("out_0", (1, S, D), F32, kind="ExternalOutput").ap()
    t["xs"] = nc.dram_tensor("xs", (NUNIT * 128, D), F32, kind="Internal").ap()
    t["ys"] = nc.dram_tensor("ys", (NUNIT * 128, D), F32, kind="Internal").ap()
    t["mod"] = nc.dram_tensor("mod", (12, 512), F32, kind="Internal").ap()
    t["nf"] = nc.dram_tensor("nf", (8, 512), F32, kind="Internal").ap()
    program(nc, t, stop)


def kernel(**inputs):
    import concourse.bacc as bacc
    from concourse.bass_utils import run_bass_kernel_spmd

    nc = bacc.Bacc("TRN2", target_bir_lowering=False, num_devices=1)
    arrays = layout(inputs)
    build(nc, arrays)
    r = run_bass_kernel_spmd(nc, [{f"in_{k}": v for k, v in arrays.items()}], core_ids=[0])
    return r.results[0]["out_0"]
```

```python
from contextlib import ExitStack

import numpy as np

import concourse.bass as bass
from concourse import mybir

F32 = mybir.dt.float32
F32R = mybir.dt.float32r
BF16 = mybir.dt.bfloat16
I32 = mybir.dt.int32
U32 = mybir.dt.uint32
ALU = mybir.AluOpType
ACT = mybir.ActivationFunctionType
AX = mybir.AxisListType.X

S = 512
D = 1024
NEG = -1e30
EPS = 1e-6
NRAW = 5
NSPL = 4
NUNIT = 23
CMP = 31
PACK = (0, 512, 1024, 896)


class Queue:

    def __init__(self, sem):
        self.sem, self.n, self.items, self.seen = sem, 0, [], {}

    def need(self, *tokens):
        for t in tokens:
            if t is None:
                continue
            if isinstance(t, list):
                self.need(*t)
                continue
            sem, value = t
            if self.seen.get(id(sem), 0) < value:
                self.seen[id(sem)] = value
                self.items.append(("wait", sem, value))

    def do(self, fn, *tokens):
        self.need(*tokens)
        self.n += 1
        self.items.append(("op", fn, (self.sem, 1)))
        return (self.sem, self.n)

    def quiet(self, fn, *tokens):
        self.need(*tokens)
        self.items.append(("op", fn, None))

    def dma(self, fn, sem, value, *tokens):
        self.need(*tokens)
        self.items.append(("op", fn, (sem, 16)))
        return (sem, value)

    def branch(self, count, *tokens):
        self.need((self.sem, self.n), *tokens)
        self.items.append(("if", count, self.n))
        self.before = dict(self.seen)

    def join(self):
        self.need((self.sem, self.n))
        self.items.append(("join", None, self.n))
        self.seen = self.before

    def bump(self):
        self.n += 1
        self.items.append(("op", lambda e: e.sem_inc(self.sem, 1), None))
        return (self.sem, self.n)

    def emit(self, eng):
        at = 0
        while at < len(self.items):
            kind, a, b = self.items[at]
            if kind == "if":
                end = next(i for i in range(at, len(self.items)) if self.items[i][0] == "join")
                steps = self.items[end][2] - b
                with eng.If(eng.value_load(a, min_val=0, max_val=7) > 0):
                    for x in self.items[at + 1:end]:
                        self.one(eng, x)
                with eng.Else():
                    if steps:
                        eng.sem_inc(self.sem, steps)
                    else:
                        eng.nop()
                at = end
            else:
                self.one(eng, self.items[at])
            at += 1

    def one(self, eng, item):
        kind, a, b = item
        if kind == "wait":
            eng.wait_ge(a, b)
        elif kind == "call":
            a(eng)
        else:
            ins = a(eng)
            if b is not None:
                ins.then_inc(b[0], b[1])


class Bank:

    def __init__(self, ap):
        self.ap, self.free = ap, []


def program(nc, t, stop=None):
    ctx = ExitStack()
    with ctx:
        def sb(name, shape, dt=F32):
            return ctx.enter_context(nc.sbuf_tensor(name, shape, dt))

        def sem(name):
            return ctx.enter_context(nc.semaphore(name))

        RS = sb("RS", [128, NSPL, 2, 1024], F32R)
        RH = sb("RH", [128, 2, 8, S], F32R)
        RAW = sb("RAW", [128, NRAW, 1024])
        X = sb("X", [128, 8, S])
        M = sb("M", [128, 8, S])
        PB = sb("PB", [128, 2, 1280])
        TB = sb("TB", [128, 3, 1280])
        PC = sb("PC", [128, 4, S])
        TAB = sb("TAB", [128, 2, S])
        VV = sb("VV", [128, 2, S])
        TMP = sb("TMP", [128, 4, S])
        identf = sb("identf", [128, 128])
        rotT = sb("rotT", [128, 128])
        onesf = sb("onesf", [128, 128])
        ntri = sb("ntri", [128, 128])
        nones = sb("nones", [128, 128])
        sltm = sb("sltm", [128, 128])
        identb = sb("identb", [128, 128], BF16)
        maskb = sb("maskb", [128, 128], BF16)
        maskt = sb("maskt", [128, 128], BF16)
        trib = sb("trib", [128, 128], BF16)
        onesb = sb("onesb", [128, 128], BF16)
        vecs = sb("vecs", [128, 64])
        modt = sb("modt", [128, 48])
        gsc = sb("gsc", [128, 32])
        small = sb("small", [128, 64])
        RT = sb("RT", [128, 704])
        PE2 = sb("PE2", [128, 32])
        KCZ = sb("KCZ", [128, 4, 32])
        VBK = sb("VBK", [128, 4, 128])
        stat = sb("stat", [128, 3, 2, 4])
        MB = sb("MB", [128, 80], BF16)
        POS = sb("POS", [128, 8], U32)
        EXI = sb("EXI", [1, 8], I32)
        with nc.sbuf_tensor("RA", [128, 2, 8, S], F32R) as RA:
            pass
        RAW2 = sb("RAW2", [128, 8, 1024])
        banks = [Bank(ctx.enter_context(nc.psum_tensor(f"ps{i}", [128, 512], F32))) for i in range(8)]

        pe, act, dve, pool, sp = (Queue(sem("s_" + n)) for n in ("pe", "act", "dve", "pool", "sp"))

        def hiF(ap):
            return ap.bitcast(F32)

        counter = [0]
        every = []

        def load(q, dst, src, *tokens):
            counter[0] += 1
            s = sem(f"d{counter[0]}")
            every.append((s, 16))
            return q.dma(lambda e: e.dma_start(dst, src), s, 16, *tokens)

        slots = {}

        def load_slot(q, slot, dst, src, *tokens):
            if slot not in slots:
                slots[slot] = [sem("d_" + slot), 0]
            c = slots[slot]
            c[1] += 16
            return q.dma(lambda e: e.dma_start(dst, src), c[0], c[1], *tokens)

        def a_act(out, in_, func, *tokens, **kw):
            return act.do(lambda e: e.activation(out, in_, func, **kw), *tokens)

        def tt(q, out, a, b, op, *tokens):
            return q.do(lambda e: e.tensor_tensor(out, a, b, op), *tokens)

        def ts(q, out, a, s1, op0, *tokens, s2=None, op1=None):
            if op1 is None:
                return q.do(lambda e: e.tensor_scalar(out, a, s1, None, op0), *tokens)
            return q.do(lambda e: e.tensor_scalar(out, a, s1, s2, op0, op1), *tokens)

        def stt(out, a, s, b, op0, op1, *tokens):
            return dve.do(lambda e: e.scalar_tensor_tensor(out, a, s, b, op0, op1), *tokens)

        def copy(q, out, in_, *tokens):
            if q is act:
                return a_act(out, in_, ACT.Copy, *tokens)
            return q.do(lambda e: e.tensor_copy(out, in_), *tokens)

        def mm(out, lhsT, rhs, start, stop, *tokens, last=False, shared=False):
            fn = lambda e: e.matmul(out, lhsT, rhs, start=start, stop=stop, skip_group_check=shared)
            return pe.do(fn, *tokens) if last else pe.quiet(fn, *tokens)

        def tr(out, in_, *tokens, last=False, ident=None):
            n = in_.shape[0]
            idn = identf[0:n, 0:n]
            fn = lambda e: e.transpose(out, in_, idn)
            return pe.do(fn, *tokens) if last else pe.quiet(fn, *tokens)

        plan = []

        def add(name, kind):
            for u in range(t[name].shape[0]):
                plan.append((name, u, t[name][u], kind))

        def add1(name, u, kind="split"):
            plan.append((name, u, t[name][u], kind))

        add("w_qkv", "split")
        add("w_c", "raw")
        for m in range(8):
            add1("w_gb", m)
            if m % 2 == 1:
                add1("w_nsa", m - 1)
                add1("w_nsa", m)
        add("w_u", "split")
        for m in range(8):
            add1("w_ga", m)
            if m % 2 == 1:
                add1("w_pp", m // 2)
        add("w_out", "split")
        ada = iter(range(48))
        for f in range(4):
            for m in range(8):
                add1("w_ff1", f * 8 + m)
                for u in [x for _, x in zip(range(1), ada)]:
                    add1("ada", u, "raw")
            for m in range(8):
                add1("w_ff2", f * 8 + m)
                for u in [x for _, x in zip(range(1), ada)]:
                    add1("ada", u, "raw")
        for n in ("w2_qa", "w2_fa", "w2_ka", "w2_va", "w2_qb", "w2_kb", "w2_vb"):
            add(n, "split")
        for m in range(0, 8, 2):
            add1("w2_ga", m)
            add1("w2_ga", m + 1)
            add1("w2_fox", m // 2)
            add1("w2_gb", m)
            add1("w2_gb", m + 1)
            add1("w2_sb", m // 2)
        add("w2_out", "split")
        extra_reg = {}
        for u0, u1 in ((0, 16), (16, NUNIT)):
            for u in range(u0, u1):
                for n in ("w_gate", "w_up"):
                    for c in range(4):
                        plan.append((n, (u, c), None, "split"))
                if u > u0:
                    for c in range(4):
                        plan.append(("w_down", (u - 1, c), None, "split"))
            for c in range(4):
                plan.append(("w_down", (u1 - 1, c), None, "split"))
            if u0 == 0:
                always = len(plan)

        moe0 = next(i for i, x in enumerate(plan) if x[0] == "w_gate")
        NWIDE = NRAW + 12
        flat = lambda a: a.rearrange("p a b -> p (a b)")
        raws = [RAW[:, i, :] for i in range(NRAW)]
        raws += [RAW2[:, i, :] for i in range(8)]
        raws += [flat(M[:, 2 * j:2 * j + 2, :]) for j in range(4)]
        wide = list(range(NRAW, NRAW + 8)) + [(moe0 + i) % NRAW for i in range(NRAW)] + list(range(NRAW + 8, NWIDE))
        raw_sem = [sem(f"raw{i}") for i in range(NWIDE)]
        raw_free = [[] for _ in range(NWIDE)]
        raw_n = [0] * NWIDE

        def raw_slot(n):
            return n % NRAW if n < moe0 else wide[(n - moe0) % NWIDE]

        def ahead(n):
            return n + 4 if n < moe0 - 5 else n + 12 if n < moe0 else n + NWIDE - 1

        spl_free = [[] for _ in range(NSPL)]
        st = {"load": 0, "split": 0, "nsplit": 0, "get": 0}
        landed, parts = {}, {}
        lo_engine = [lambda n: dve if n in (0, 2) else pool]
        late = {}

        def stream_load(n):
            name, u, src, kind = plan[n]
            r = raw_slot(n)
            dst = raws[r]
            need = list(raw_free[r])
            raw_n[r] += 16
            if src is None:
                uu, c = u
                if uu < 16:
                    src = t[name][uu, c]
                else:
                    if uu not in late:
                        late[uu] = True
                        need.append(late["tok"])
                        j = uu - 16

                        def ld(e, j=j):
                            extra_reg[j] = e.value_load(EXI[0:1, j:j + 1], min_val=0, max_val=15)
                        sp.need(late["tok"])
                        sp.items.append(("call", ld, None))

                    def fn(e, j=uu - 16, name=name, c=c):
                        w = t[name][bass.ds(extra_reg[j], 1), c, :, :].rearrange("a p n -> (a p) n")
                        return e.dma_start(dst, w)
                    landed[n] = sp.dma(fn, raw_sem[r], raw_n[r], need)
                    return
            landed[n] = sp.dma(lambda e: e.dma_start(dst, src), raw_sem[r], raw_n[r], need)

        def stream_split(n):
            if plan[n][3] == "raw":
                return
            k = st["nsplit"]
            st["nsplit"] += 1
            s, r = k % NSPL, raw_slot(n)
            hi = a_act(RS[:, s, 0, :], raws[r], ACT.Copy, landed[n], spl_free[s])
            q = lo_engine[0](k)
            lo = tt(q, RS[:, s, 1, :], raws[r], hiF(RS[:, s, 0, :]), ALU.subtract,
                    landed[n], hi, spl_free[s])
            raw_free[r] = [hi, lo]
            parts[n] = (s, lo, hi)

        def get(name, u):
            n = st["get"]
            assert plan[n][:2] == (name, u), (plan[n][:2], name, u)
            end = always if n < always else len(plan)
            while st["load"] <= min(ahead(n), end - 1):
                stream_load(st["load"])
                st["load"] += 1
                while st["split"] < min(st["load"], n + NSPL):
                    stream_split(st["split"])
                    st["split"] += 1
            while st["split"] <= min(n + NSPL - 1, end - 1):
                stream_split(st["split"])
                st["split"] += 1
            st["get"] += 1
            return n

        def used(n, tok):
            if plan[n][3] == "raw":
                raw_free[raw_slot(n)] = [tok]
            else:
                spl_free[parts[n][0]] = [tok]

        ring = [0]

        def bank(pool_=None):
            b = (pool_ or range(8))
            ring[0] += 1
            return banks[b[ring[0] % len(b)]]

        def dense(name, u, acts, K, finish, which=range(8)):
            R, k0, toks = acts
            n = get(name, u)
            s, lo_t, hi_t = parts[n]
            for m in range(8 // K):
                b = bank(which)
                for k in range(K):
                    c = (m * K + k) * 128
                    wh, wl = RS[:, s, 0, c:c + 128], RS[:, s, 1, c:c + 128]
                    xh, xl = R[:, 0, k0 + k, :], R[:, 1, k0 + k, :]
                    mm(b.ap[:, :], wh, xh, k == 0, False, hi_t, toks[k], *(b.free if k == 0 else ()))
                    mm(b.ap[:, :], wh, xl, False, False)
                    tok = mm(b.ap[:, :], wl, xh, False, k == K - 1, lo_t, last=(k == K - 1))
                if m == 8 // K - 1:
                    used(n, tok)
                finish((8 // K) * u + m, b, tok)

        def dense_rows(name, units, acts, finish, which):
            R, k0, toks = acts
            for u in range(units):
                n = get(name, u)
                s, lo_t, hi_t = parts[n]
                for kk in range(2):
                    k = 2 * u + kk
                    wh, wl = (RS[:, s, x, kk * 512:kk * 512 + 512] for x in (0, 1))
                    for i in range(4):
                        b = banks[which[i]]
                        xh, xl = (R[:, x, k0 + k, 128 * i:128 * i + 128] for x in (0, 1))
                        mm(b.ap[:, :], xh, wh, k == 0, False, hi_t, toks[k], *(b.free if k == 0 else ()))
                        mm(b.ap[:, :], xl, wh, False, False)
                        tok = mm(b.ap[:, :], xh, wl, False, k == 7, lo_t, last=True)
                        if k == 7:
                            finish(i, b, tok)
                used(n, tok)

        def split_to(R, k, src, hi_q, lo_q, free, *tokens):
            hi = copy(hi_q, R[:, 0, k, :], src, free, *tokens)
            lo = tt(lo_q, R[:, 1, k, :], src, hiF(R[:, 0, k, :]), ALU.subtract, hi, free, *tokens)
            return hi, lo

        tmp_free = [[] for _ in range(4)]
        cst = {}
        cst["vecs"] = load(act, vecs[:, :], t["vecs"])
        xt = []
        for i in range(4):
            xt.append(load(sp, X[:, 2 * i:2 * i + 2, :], t["xT"][:, 2 * i:2 * i + 2, :]))
            if i < 2:
                stream_load(i)
                st["load"] += 1
        cst["onesf"] = load(sp, onesf[:, :], t["onesf"])
        for name, dst in (("identf", identf), ("rotT", rotT)):
            cst[name] = load(sp, dst[:, :], t[name])
        cst["tab"] = load(sp, TAB[:, :, :], t["tab"])
        for name, dst in (("ntri", ntri), ("nones", nones), ("sltm", sltm), ("maskb", PC[:, 2, 0:128]),
                          ("maskt", PC[:, 2, 128:256])):
            cst[name] = load(sp, dst[:, :], t[name])
        for name, dst, src in (("identb", identb, "identf"), ("maskb", maskb, "maskb"), ("maskt", maskt, "maskt"),
                               ("trib", trib, "sltm"), ("onesb", onesb, "onesf")):
            frm = {"identf": identf, "sltm": sltm, "onesf": onesf, "maskb": PC[:, 2, 0:128],
                   "maskt": PC[:, 2, 128:256]}[src]
            cst[name] = copy(pool, dst[:, :], frm[:, :], cst[src])
        eps = dve.do(lambda e: e.memset(small[:, 0:1], EPS))
        one = dve.do(lambda e: e.memset(small[:, 1:2], 1.0))

        VG_MIX, VG_MLP, VG_FIN, V_PS, VG1, VG2, V_C, V_BF = 0, 8, 16, 24, 28, 36, 44, 52

        RST = RT[:, 0:512]
        rst_free = [[]]
        sq = {}

        def square_in(k, xtok):
            if k == 0:
                sq["acc"] = a_act(RST, X[:, 0, :], ACT.Square, xtok, rst_free[0])
                return
            j = k % 2
            s = a_act(TMP[:, j, :], X[:, k, :], ACT.Square, xtok, tmp_free[j])
            sq["acc"] = tt(pool if k < 7 and not sq.get("fast") else dve, RST, RST, TMP[:, j, :], ALU.add, s, sq["acc"])
            tmp_free[j] = [sq["acc"]]

        SQ2 = PB[:, 0, 0:512]

        def square_in2(k, xtok, *free):
            g = vecs[:, VG_FIN + k:VG_FIN + k + 1]
            if k == 0:
                sq["acc2"] = a_act(SQ2, X[:, 0, :], ACT.Square, xtok, cst["vecs"], *free, scale=g)
                return
            j = k % 2
            s = a_act(TMP[:, j, :], X[:, k, :], ACT.Square, xtok, tmp_free[j], scale=g)
            sq["acc2"] = tt(dve, SQ2, SQ2, TMP[:, j, :], ALU.add, s, sq["acc2"])
            tmp_free[j] = [sq["acc2"]]

        NR = small[:, 32:56]

        def mean_root(col, acc, b, *tokens):
            for i in range(4):
                tok = mm(b.ap[:, i:i + 1], acc[:, 128 * i:128 * i + 128], onesf[:, 0:1], True, True, b.free,
                         cst["onesf"], *tokens, last=(i == 3))
            r = a_act(NR[:, col:col + 4], b.ap[:, 0:4], ACT.Sqrt, tok, eps, bias=small[:, 0:1], scale=1.0 / D)
            b.free = [r]
            return dve.do(lambda e: e.reciprocal(NR[:, col:col + 4], NR[:, col:col + 4]), r)

        def spread(col, j, b, *tokens):
            dg = TMP[:, j, :].rearrange("p (i n) -> p i n", i=4)
            d = tt(dve, dg, identf[:, :].unsqueeze(1).broadcast_to([128, 4, 128]),
                   NR[:, col:col + 4].unsqueeze(2).broadcast_to([128, 4, 128]), ALU.mult, cst["identf"], tmp_free[j],
                   *tokens)
            tok = mm(b.ap[:, :], onesf[:, :], TMP[:, j, :], True, True, d, b.free, last=True)
            tmp_free[j] = [tok]
            return tok

        def rms_row(which=range(8)):
            b, b2 = bank(which), bank(which)
            r = mean_root(0, RST, b, sq["acc"])
            tok = spread(0, 3, b2, r)
            r = copy(act, RST, b2.ap[:, :], tok)
            b2.free = [r]
            return r

        def scaled(R, k, g, *tokens):
            hi = a_act(R[:, 0, k, :], X[:, k, :], ACT.Copy, cst["vecs"], *tokens, scale=g)
            lo = stt(R[:, 1, k, :], X[:, k, :], g, hiF(R[:, 0, k, :]), ALU.mult, ALU.subtract, hi, *tokens)
            return [hi, lo]

        H = [scaled(RH, k, vecs[:, VG_MIX + k:VG_MIX + k + 1], xt[k // 2]) for k in range(8)]
        hx = (RH, 0, H)
        rms1 = {}

        Kz = M[:, :, :].rearrange("p (b g r) n -> p b g r n", b=2, g=2)
        kzero, scz, scz2 = [], [], []

        def start_squares():
            sq["fast"] = True
            for k in range(8):
                square_in(k, xt[k // 2])
            sq["fast"] = False

        def start_rms():
            rms1["r"] = rms_row()
            xread.append(sq["acc"])
            for i in range(2):
                kzero.append(dve.do(lambda e, i=i: e.memset(M[:, 4 * i:4 * i + 4, :], 0.0)))
            scz.append(dve.do(lambda e: e.memset(PB[:, 1, :], 0.0)))
            scz2.append(dve.do(lambda e: e.memset(TB[:, 1, 0:1024], 0.0)))

        xread = list(H[7])

        def rope(m, outs):
            def first(b, tok, scale):
                j = m % 2
                e1 = stt(TMP[:, j, :], b.ap[:, :], scale, RST, ALU.mult, ALU.mult, tok, rms1["r"], tmp_free[j])
                b.free = [e1]

                def second():
                    b2 = bank()
                    r = mm(b2.ap[:, :], rotT[:, :], TMP[:, j, :], True, True, e1, cst["rotT"], b2.free,
                           last=True)
                    c = tt(pool, TMP[:, 2 + j, :], TMP[:, j, :], TAB[:, 0, :], ALU.mult, e1,
                           cst["tab"], tmp_free[2 + j])
                    s_ = tt(dve, TMP[:, j, :], b2.ap[:, :], TAB[:, 1, :], ALU.mult, r, c, cst["tab"])
                    b2.free = [s_]
                    toks = []
                    for (lo_, hi_), dst, fr in outs:
                        toks.append(tt(dve, dst, TMP[lo_:hi_, j, :], TMP[lo_:hi_, 2 + j, :], ALU.add,
                                       s_, c, fr))
                    tmp_free[j] = [toks[-1]]
                    tmp_free[2 + j] = [toks[-1]]
                    return toks
                return second
            return first

        pend = [None]

        def flush():
            if pend[0] is not None:
                f, pend[0] = pend[0], None
                f()

        qtok = {}
        ktok = {}
        vtok = {}
        cmpt = {}
        F2 = PB[:, 0, 0:1024].rearrange("p (g n) -> p g n", g=2)
        Fpk, Fpv = PB[:, 1, 0:992], TB[:, 0, 0:992]

        def fin_qkv(u, b, tok):
            flush()
            if u < 8:
                sec = rope(u, [((0, 128), X[:, u, :], xread)])(b, tok, 0.125)

                def g():
                    qtok[u] = sec()[0]
                pend[0] = g
            elif u < 10:
                br = u - 8
                outs = []
                for g_ in range(2):
                    for p_ in range(2):
                        outs.append(((64 * g_, 64 * g_ + 64), Kz[64 * p_:64 * p_ + 64, br, g_, p_, :], kzero))
                sec = rope(u, outs)(b, tok, 1.0)

                def g():
                    tk = sec()
                    for g_ in range(2):
                        for p_ in range(2):
                            ktok[(br, g_, p_)] = tk[2 * g_ + p_]
                pend[0] = g
            elif u < 12:
                src = b.ap
                kv = u - 10
                fre = cmpt.get("f2free", [])
                cs = []
                for g_ in range(2):
                    gg = slice(64 * g_, 64 * g_ + 64)
                    cs.append(tt(dve, F2[0:64, g_, :], src[gg, :], RST[gg, :], ALU.mult, tok, rms1["r"], fre))
                    cs.append(tt(dve, F2[64:128, g_, 0:511], src[gg, 1:512], RST[gg, 1:512], ALU.mult, tok,
                                 rms1["r"], fre))
                b.free = [cs[-1]]
                Fp = (Fpk, Fpv)[kv]
                for lp in range(16):
                    o = Fp[:, lp * 62:lp * 62 + 62].rearrange("p (g n) -> p g n", g=2)
                    i_ = F2[:, :, 2 * lp:2 * lp + 481:16]
                    last = ts(dve, o, i_, PE2[:, kv * 16 + lp:kv * 16 + lp + 1], ALU.add, cs, cst["pe2"], scz)
                cmpt["f2free"] = [last]
                cmpt[kv] = last
            elif u < 14:
                br = u - 12
                j = u % 2
                e1 = tt(dve, TMP[:, j, :], b.ap[:, :], RST, ALU.mult, tok, rms1["r"], tmp_free[j])
                b.free = [e1]

                def g():
                    b2 = bank()
                    for i in range(4):
                        tk = tr(b2.ap[:, 128 * i:128 * i + 128], TMP[:, j, 128 * i:128 * i + 128], e1,
                                cst["identf"], *(b2.free if i == 0 else ()), last=(i == 3))
                    tmp_free[j] = [tk]
                    vtok[br] = copy(dve, VV[:, br, :], b2.ap[:, :], tk)
                    b2.free = [vtok[br]]
                pend[0] = g
            else:
                j = u % 2
                e0 = tt(dve, TMP[0:48, j, :], b.ap[0:48, :], RST[0:48, :], ALU.mult, tok, rms1["r"], tmp_free[j])
                b.free = [e0]
                e1 = a_act(TMP[0:48, j, :], TMP[0:48, j, :], ACT.Sigmoid, e0)

                def g():
                    b2 = bank()
                    for i in range(4):
                        tk = tr(b2.ap[:, 48 * i:48 * i + 48], TMP[0:48, j, 128 * i:128 * i + 128], e1,
                                cst["identf"], *(b2.free if i == 0 else ()), last=(i == 3))
                    tmp_free[j] = [tk]
                    cmpt["gate"] = copy(dve, GTS[:, :], b2.ap[:, 0:192], tk)
                    b2.free = [cmpt["gate"]]
                pend[0] = g

        GTS = RT[:, 512:704]
        CW2 = TB[:, 2, 0:384].rearrange("p (c n) -> p c n", c=2)
        CTB = TB[:, 2, 384:508]
        MCB = TB[:, 2, 508:636]
        cst["pe2"] = load(sp, PE2[:, :], t["pe2"])
        cst["mcb"] = load(sp, MCB[:, :], t["mcb"])
        cst["cw2"] = load(sp, CW2[:, :, :], t["cw2"])
        cst["ctb"] = load(sp, CTB[:, :], t["ctb"])
        kcz0 = dve.do(lambda e: e.memset(KCZ[:, :, :], 0.0))
        vbk0 = dve.do(lambda e: e.memset(VBK[:, :, :], 0.0))
        lag = []
        for u in range(15):
            dense("w_qkv", u, hx, 8, lambda *a: lag.append(a))
            if u == 0:
                start_squares()
            elif u == 1:
                start_rms()
            else:
                fin_qkv(*lag.pop(0))
        while lag:
            fin_qkv(*lag.pop(0))
        flush()

        HIDS = [TB[:, 1, 0:256], TB[:, 1, 640:896]]
        HT = TB[:, 1, 256:512].rearrange("p (c n) -> p c n", c=2)
        kct = []
        vct = []
        prev, hid = [], []
        for kv in range(2):
            b = bank()
            Fp = (Fpk, Fpv)[kv]
            for c in range(4):
                n = get("w_c", kv * 4 + c)
                for q in range(4):
                    lp = 4 * c + q
                    tok = mm(b.ap[0:62, 0:256], Fp[:, lp * 62:lp * 62 + 62],
                             RAW[:, n % NRAW, q * 256:q * 256 + 256], lp == 0, lp == 15,
                             cmpt[kv], landed[n], *(b.free if lp == 0 else ()), last=(q == 3))
                used(n, tok)
            hid.append(a_act(HIDS[kv][0:62, :], b.ap[0:62, 0:256], ACT.Gelu_apprx_tanh, tok, scz2))
            b.free = [hid[kv]]
        for kv in range(2):
            HID, g1 = HIDS[kv], hid[kv]
            b = bank()
            for c in range(2):
                tok = tr(b.ap[:, 128 * c:128 * c + 62], HID[0:62, 128 * c:128 * c + 128], g1, b.free,
                         last=(c == 1))
            c1 = copy(dve, HT[:, :, 0:62], b.ap[:, 0:256].rearrange("p (c n) -> p c n", c=2)[:, :, 0:62],
                      tok, prev, scz2)
            b.free = [c1]
            b = bank()
            if kv == 0:
                for c in range(2):
                    tok = mm(b.ap[:, 0:62], CW2[:, c, 0:128], HT[:, c, 0:62], c == 0, c == 1, c1,
                             cst["cw2"], *(b.free if c == 0 else ()), last=(c == 1))
                prev = [tok]
                T0, T1 = TB[:, 1, 512:574], TB[:, 1, 576:638]
                e1 = copy(dve, T0, b.ap[:, 0:62], tok, scz2)
                b.free = [e1]
                b = bank()
                tok = mm(b.ap[:, 0:62], rotT[:, :], T0, True, True, e1, b.free, last=True)
                e2 = tt(dve, T1, b.ap[:, 0:62], CTB[:, 62:124], ALU.mult, tok, cst["ctb"], scz2)
                b.free = [e2]
                e3 = tt(dve, T0, T0, CTB[:, 0:62], ALU.mult, tok, e1)
                for g_ in range(2):
                    for p_ in range(2):
                        r0 = 64 * p_
                        kct.append(tt(dve, KCZ[r0:r0 + 64, 2 * g_ + p_, 0:31], T0[r0:r0 + 64, 31 * g_:31 * g_ + 31],
                                      T1[r0:r0 + 64, 31 * g_:31 * g_ + 31], ALU.add, e2, e3, kcz0))
            else:
                for g_ in range(2):
                    for c in range(2):
                        tok = mm(b.ap[0:31, 64 * g_:64 * g_ + 64], HT[:, c, 31 * g_:31 * g_ + 31],
                                 CW2[:, c, 128:192], c == 0, c == 1, c1, cst["cw2"],
                                 *(b.free if c == 0 and g_ == 0 else ()), last=(c == 1))
                for g_ in range(2):
                    for a in range(2):
                        for z in range(2):
                            r0 = 64 * a + 32 * z
                            vct.append(copy(dve, VBK[r0:r0 + 31, 2 * g_ + a, 64 * z:64 * z + 64],
                                            b.ap[0:31, 64 * g_:64 * g_ + 64], tok, vbk0))
                b.free = [vct[-1]]

        SCQ = [PB[:, 0, 0:512], PB[:, 0, 512:1024]]
        SCW = [PB[:, 1, 0:512], PB[:, 1, 512:1024]]
        SB_ = TB[:, 0, 0:64]
        pbw = [cmpt["f2free"], cmpt[0], cmpt[1], [pe.do(lambda e: e.matmul(banks[7].ap[0:32, 0:32], identb[:, 0:32], identb[:, 0:32], start=True, stop=True), cst["identb"], banks[7].free)]]
        gts = GTS[:, :].rearrange("p (i h b) -> p i h b", i=4, b=3)
        mcb = MCB[:, :].rearrange("p (i n) -> p i n", i=4)
        pct = []
        sf = [[], []]
        cw = {}

        def cmp_front(Q):
            g_ = Q // 2
            b = bank()
            for a in range(2):
                for p_ in range(2):
                    j = 2 * a + p_
                    tok = mm(b.ap[32 * j:32 * j + 32, :], KCZ[:, 2 * g_ + p_, :], X[:, 2 * Q + a, :], True, True,
                             kct, qtok[2 * Q + a], b.free, last=(j == 3))
            A, W = SCQ[Q % 2], SCW[Q % 2]
            fr = sf[Q % 2]
            e1 = copy(act, A, b.ap[:, :], tok, pbw, fr)
            b.free = [e1]
            b = bank()
            for i in range(4):
                tok = tr(b.ap[:, 128 * i:128 * i + 128], A[:, 128 * i:128 * i + 128], e1, b.free, last=(i == 3))
            W4 = W.rearrange("p (i h n) -> p i h n", i=4, h=4)
            B4 = b.ap[:, :].rearrange("p (i h n) -> p i h n", i=4, h=4)
            for i in range(4):
                e2 = tt(dve, W4[:, i], B4[:, i], mcb[:, i, :].unsqueeze(1).broadcast_to([128, 4, 32]), ALU.add, tok,
                        cst["mcb"], pbw, fr)
            b.free = [e2]
            W3 = W.rearrange("p (x n) -> p x n", n=32)
            o_ = 32 * (Q % 2)
            SM, SR = SB_[:, o_:o_ + 16], SB_[:, o_ + 16:o_ + 32]
            e3 = dve.do(lambda e, W3=W3: e.reduce_max(SM, W3, AX), e2)
            e4 = ts(dve, SM, SM, -1e29, ALU.max, e3)
            e5 = tt(dve, W3, W3, SM.unsqueeze(2).broadcast_to([128, 16, 32]), ALU.subtract, e4)
            e6 = a_act(W, W, ACT.Exp, e5)
            e7 = dve.do(lambda e, W3=W3: e.reduce_sum(SR, W3, AX), e6)
            e8 = ts(dve, SR, SR, 1e-30, ALU.max, e7)
            e9 = dve.do(lambda e: e.reciprocal(SR, SR), e8)
            e10 = tt(dve, SR.rearrange("p (i h) -> p i h", i=4), SR.rearrange("p (i h) -> p i h", i=4),
                     gts[:, :, 4 * Q:4 * Q + 4, 0], ALU.mult, e9, cmpt["gate"])
            e11 = tt(dve, W3, W3, SR.unsqueeze(2).broadcast_to([128, 16, 32]), ALU.mult, e10)
            cw[Q] = e11

        def cmp_back(Q):
            W, e11 = SCW[Q % 2], cw[Q]
            b = bank()
            for i in range(4):
                tok = tr(b.ap[:, 128 * i:128 * i + 128], W[:, 128 * i:128 * i + 128], e11, b.free, last=(i == 3))
            c1 = copy(act, PC[:, Q, :], b.ap[:, :], tok, cst["maskb"], cst["maskt"])
            b.free = [c1]
            sf[Q % 2] = [tok]
            pct.append(c1)

        for Q in range(5):
            if Q < 4:
                cmp_front(Q)
            if Q:
                cmp_back(Q - 1)
        e11 = cw[3]
        cmpdone = sf[0] + sf[1] + [e11]

        SBK = [0, 1, 2, 3]
        TPL = ((4, 0), (5, 0), (6, 0), (5, 384))

        def attention(N, qtile, keys, kneed, score_add, weight, value, obank, ostart, odone, first_need):
            pfree, tfree = [first_need] * 2, [first_need] * 3
            ptok, ttok = {}, {}
            sfree = [[], []]
            off = [0, 128, 384, 768]
            toff = PACK

            def meet_values(m, js):
                for j in js:
                    c, w = toff[j], 512 - 128 * j
                    for q in (m, m + 1):
                        b, r0 = obank(q)
                        st_ = ostart(q, b) if j == 0 else False
                        va, vt = value(q, j)
                        tok = mm(b.ap[r0:r0 + 64, 128 * j:512], va, TB[:, q % 3, c:c + w], st_, False,
                                 ttok[q][j], vt, *(b.free if j == 0 else ()), last=True, shared=True)
                if js[-1] == 3:
                    tfree[m % 3] = tfree[(m + 1) % 3] = [tok]
                    odone(m + 1, b, tok)

            for n in range(N + 3):
                if n % 2 == 0 and n >= 4:
                    meet_values(n - 4, (2, 3))
                tks = {}
                if n < N:
                    P_ = PB[:, n % 2, :]
                    mxs, sms, rcs = stat[:, 0, n % 2, :], stat[:, 1, n % 2, :], stat[:, 2, n % 2, :]
                    adder = score_add(n) if score_add else None
                    ex = [None] * 4
                for i in (3, 2, 1, 0):
                    if n < N:
                        b = banks[SBK[i]]
                        w = 128 * (i + 1)
                        mm(b.ap[:, 0:w], qtile(n, i), keys(n)[:, 0:w], True, False, kneed(n), b.free)
                        tok = mm(b.ap[:, w - 128:w], identb[:, :], maskb[:, :], False, True, cst["identb"],
                                 cst["maskb"], last=True)
                        pd = P_[:, off[i]:off[i] + w]
                        if adder is None:
                            m_ = dve.do(lambda e, b=b, w=w, o=mxs[:, i:i + 1]: e.tensor_reduce(
                                o, b.ap[:, 0:w], AX, ALU.max, negate=True), tok, sfree[n % 2])
                            x_ = act.do(lambda e, b=b, w=w, pd=pd, mx=mxs[:, i:i + 1], sm=sms[:, i:i + 1]:
                                        e.activation(pd, b.ap[:, 0:w], ACT.Exp, bias=mx, accum_out=sm),
                                        m_, tok, pfree[n % 2], sfree[n % 2])
                            b.free = [x_]
                        else:
                            ad, atok = adder[:2]
                            a_ = dve.do(lambda e, b=b, w=w, pd=pd, o=mxs[:, i:i + 1], ad=ad:
                                        e.tensor_tensor_reduce(out=pd, in0=b.ap[:, 0:w], in1=ad[:, 0:w],
                                                               scale=-1.0, scalar=3e38, op0=ALU.add, op1=ALU.min,
                                                               accum_out=o),
                                        tok, atok, pfree[n % 2], sfree[n % 2])
                            b.free = [a_]
                            x_ = act.do(lambda e, pd=pd, mx=mxs[:, i:i + 1], sm=sms[:, i:i + 1]:
                                        e.activation(pd, pd, ACT.Exp, bias=mx, scale=-1.0, accum_out=sm), a_,
                                        sfree[n % 2])
                            if i == 0:
                                adder[2](a_)
                        ex[i] = x_
                    if n % 2 == 1 and n >= 3 and i >= 2:
                        meet_values(n - 3, (3 - i,))
                if 1 <= n <= N:
                    m = n - 1
                    for j in (0, 1, 3, 2):
                        bi, o = TPL[j]
                        for ii in range(j, 4):
                            tok = tr(banks[bi].ap[:, o + 128 * (ii - j):o + 128 * (ii - j) + 128],
                                     PB[:, m % 2, off[ii] + 128 * j:off[ii] + 128 * j + 128], ptok[m][ii],
                                     banks[bi].free if o == 0 else None, last=(ii == 3))
                        if j == 1:
                            continue
                        c, w = {0: (0, 512), 3: (512, 512), 2: (1024, 256)}[j]
                        tk = copy(act, TB[:, m % 3, c:c + w], banks[bi].ap[:, 0:w], tok, tfree[m % 3])
                        banks[bi].free = [tk]
                        tks[j] = tk
                        if j == 3:
                            tks[1] = tk
                    pfree[m % 2] = [tok]
                    ttok[m] = tks
                if n < N:
                    r_ = dve.do(lambda e, o=rcs, i_=sms: e.reciprocal(o, i_), ex, sfree[n % 2])
                    if weight is not None:
                        wt, wtok = weight(n)
                        r_ = tt(dve, rcs, rcs, wt, ALU.mult, r_, wtok)
                    pt = []
                    for i in range(4):
                        w = 128 * (i + 1)
                        pd = P_[:, off[i]:off[i] + w]
                        pt.append(ts(dve, pd, pd, rcs[:, i:i + 1], ALU.mult, ex[i], r_))
                    ptok[n] = pt
                    sfree[n % 2] = [pt[-1]]
            return pfree + tfree

        RAT = {}

        def nsa_start(m, b):
            if m % 4 == 0:
                pr = m // 4
                mm(b.ap[:, :], VBK[:, 2 * (pr // 4) + pr % 2, :], PC[:, pr // 2, :], True, False, vct,
                   pct[pr // 2], b.free, shared=True)
            return False

        def nsa_done(m, b, tok):
            if m % 4 == 3:
                RAT[m // 4] = list(split_to(RA, m // 4, b.ap[:, :], act, dve, [], tok))
                b.free = RAT[m // 4]

        ring[0] = 0
        adone = attention(
            32, lambda n, i: X[:, n // 4, 128 * i:128 * i + 128],
            lambda n: Kz[:, (n // 2) % 2, n // 16, n % 2, :],
            lambda n: [qtok[n // 4], ktok[((n // 2) % 2, n // 16, n % 2)]], None,
            lambda n: (gts[:, :, 2 * (n // 4) + n % 2, 1 + (n // 2) % 2], cmpt["gate"]),
            lambda m, j: (VV[:, (m // 2) % 2, 128 * j + 64 * (m // 16):128 * j + 64 * (m // 16) + 64],
                          vtok[(m // 2) % 2]),
            lambda m: (banks[7], 64 * (m % 2)), nsa_start, nsa_done, cmpdone)
        xt = [load(act, X[:, 2 * i:2 * i + 2, :], t["xT"][:, 2 * i:2 * i + 2, :], adone) for i in range(4)]
        xt = [xt[k // 2] for k in range(8)]
        if stop == "nsa":
            return finish_program(nc, ctx, locals())

        gb_bank = {}
        mtok = {}
        sg_free = [[], [], [], []]

        def gate_fin(store, by=None):
            def f(m, b, tok):
                j = m % 4
                if by is not None:
                    g0 = tt(dve, TMP[:, j, :], b.ap[:, :], RST, ALU.mult, tok, by, tmp_free[j], sg_free[j])
                    b.free = [g0]
                    rst_free[0] = [g0]
                    store[m] = a_act(TMP[:, j, :], TMP[:, j, :], ACT.Sigmoid, g0)
                    return
                g1 = a_act(TMP[:, j, :], b.ap[:, :], ACT.Sigmoid, tok, tmp_free[j], sg_free[j])
                b.free = [g1]
                store[m] = g1
            return f

        gt = {}

        def merge_fin(first, base_tok):
            def f(m, b, tok):
                j = m % 4
                if first:
                    o = tt(dve, M[:, m, :], TMP[:, j, :], b.ap[:, :], ALU.mult, tok, gt[m], base_tok)
                    mtok[m] = o
                else:
                    o1 = tt(dve, TMP[:, j, :], TMP[:, j, :], b.ap[:, :], ALU.mult, tok, gt[m])
                    o = tt(pool, M[:, m, :], M[:, m, :], TMP[:, j, :], ALU.add, o1, mtok[m])
                    mtok[m] = o
                    b.free = [o1]
                    tmp_free[j] = [o]
                    return
                b.free = [o]
                tmp_free[j] = [o]
            return f

        def merged(k, free):
            return list(split_to(RH, k, M[:, k, :], act, pool if k % 2 else dve, free, mtok[k]))

        oa = (RA, 0, [RAT[k] for k in range(8)])
        for m in range(8):
            dense("w_gb", m, hx, 8, gate_fin(gt, rms1["r"]))
            if m % 2 == 1:
                dense("w_nsa", m - 1, oa, 8, merge_fin(True, adone))
                dense("w_nsa", m, oa, 8, merge_fin(True, adone))
        ra_free = [(pe.sem, pe.n)]

        UU = PB[:, 0, 0:512]
        UA = PB[:, 0, 512:1024]
        UB = PB[:, 1, 0:512]
        UC = PB[:, 1, 512:1024]
        WP = TB[:, 0, 0:512]
        ICT = TB[:, 1, 0:64]
        cst["wp"] = load(act, WP, t["w_pool"], adone)
        cst["ict"] = load(act, ICT, t["ict"], adone)
        ptk = {}
        pl = {"free": [], "y": {}}

        def fin_u(u, b, tok):
            flush()
            w = (2, 4, 8, 16)[u]
            e1 = tt(dve, UU, b.ap[:, :], RST, ALU.mult, tok, rms1["r"], adone, pl["free"])
            b.free = [e1]
            src, last = UU, e1
            sh, bufs, k = 1, [UA, UB], 0
            while sh < w:
                dst = bufs[k % 2]
                c_ = copy(dve, dst[:, 0:sh], src[:, 0:sh], last, adone, pl["free"])
                last = [tt(dve, dst[:, sh:], src[:, sh:], src[:, 0:512 - sh], ALU.add, last, c_), c_]
                src, sh, k = dst, sh * 2, k + 1
            m1 = tt(dve, src[:, 0:16], src[:, 0:16], ICT[:, 16 * u:16 * u + 16], ALU.mult, last, cst["ict"])
            m2 = ts(dve, src[:, 16:], src[:, 16:], 1.0 / w, ALU.mult, last)
            d = tt(dve, UC, src, UU, ALU.subtract, m1, m2, pl["free"])

            def g():
                b2 = bank()
                tk = mm(b2.ap[:, :], WP[:, 128 * u:128 * u + 128], UC, True, True, d, cst["wp"], b2.free,
                        last=True)
                y = a_act(UU, b2.ap[:, :], ACT.Copy, tk, d, scale=vecs[:, V_PS + u:V_PS + u + 1])
                b2.free = [y]
                hi, lo = split_to(RA, u, UU, act, dve, ra_free, y)
                pl["free"] = [hi, lo, tk]
                pl["y"][u] = [hi, lo]
            pend[0] = g

        for u in range(4):
            dense("w_u", u, hx, 8, fin_u)
        flush()
        ya = (RA, 0, [pl["y"][k] for k in range(4)])
        for m in range(8):
            dense("w_ga", m, hx, 8, gate_fin(gt, rms1["r"]))
            if m == 7:
                h_free = [(pe.sem, pe.n)]
                H = [merged(k, h_free) for k in range(6)]
            if m % 2 == 1:
                dense("w_pp", m // 2, ya, 4, merge_fin(False, None))
        H += [merged(k, h_free) for k in (6, 7)]
        a_free = [(pe.sem, pe.n)]
        HA = {}

        def residual(m, b, tok):
            o = tt(dve, X[:, m, :], X[:, m, :], b.ap[:, :], ALU.add, tok, xt[m])
            b.free = [o]
            xt[m] = o
            if lastx[0]:
                square_in(m, o)
            if lastx[0] == 1:
                HA[m] = scaled(RA, m, vecs[:, VG_MLP + m:VG_MLP + m + 1], o, a_free)
            if lastx[0] == 2:
                square_in2(m, o, ra_free)

        lastx = [1]
        for m in range(8):
            dense("w_out", m, (RH, 0, H), 8, residual)
        lastx[0] = 0
        mread = H
        h_free = [(pe.sem, pe.n)]
        hx = (RA, 0, [HA[k] for k in range(8)])
        if stop == "mix":
            return finish_program(nc, ctx, locals())

        CA = small[:, 8:16]
        cs = a_act(CA, vecs[:, V_C:V_C + 8], ACT.Sigmoid, cst["vecs"])
        cs = tt(dve, CA, CA, vecs[:, V_C:V_C + 8], ALU.mult, cs)
        MROW = PC[:, 0:3, :]
        adab = banks[7]
        ad = {"n": 0, "out": []}

        def ada_unit():
            u = ad["n"]
            if u >= 48:
                return
            ad["n"] += 1
            n = get("ada", u)
            J, k, half = u // 16, (u % 16) // 2, u % 2
            for c in range(2):
                cc = 2 * half + c
                tok = mm(adab.ap[32 * cc:32 * cc + 1, :], CA[:, k:k + 1], RAW[:, n % NRAW, 512 * c:512 * c + 512],
                         k == 0, k == 7, cs, landed[n], *(adab.free if k == 0 else ()), last=(c == 1), shared=True)
            used(n, tok)
            if u % 16 == 15:
                cps = []
                for cc in range(4):
                    cps.append(copy(dve, MROW[32 * cc:32 * cc + 1, J, :], adab.ap[32 * cc:32 * cc + 1, :], tok, adone,
                                    pct))
                adab.free = [cps[-1]]
                for cc in range(4):
                    ad["out"].append(load(act, t["mod"][4 * J + cc:4 * J + cc + 1, :], MROW[32 * cc:32 * cc + 1, J, :], cps[cc]))

        zz = dve.do(lambda e: e.memset(TB[:, 2, 0:1024], 0.0), adone)
        zx = []
        zsem = sem("zsem")
        RB = list(range(7))
        f_free = [h_free]
        tmpi = [0]
        rms2 = {}
        for f in range(4):
            FT = {}

            def fin1(m, b, tok):
                if m == 0:
                    r = rms_row(RB)
                    rms2["r"] = tt(dve, RST, RST, RST, ALU.mult, r)
                i_ = tmpi[0] % 2
                tmpi[0] += 1
                r_ = a_act(TMP[:, i_, :], b.ap[:, :], ACT.Relu, tok, tmp_free[i_])
                v_ = tt(dve, TMP[:, 2 + i_, :], TMP[:, i_, :], b.ap[:, :], ALU.mult, r_, tmp_free[2 + i_])
                b.free = [v_]
                tmp_free[i_] = [v_]
                v_ = tt(dve, TMP[:, 2 + i_, :], TMP[:, 2 + i_, :], RST, ALU.mult, v_, rms2["r"])
                rst_free[0] = [v_]
                hi, lo = split_to(RH, m % 8, TMP[:, 2 + i_, :], act, pool if i_ else dve, f_free[0], v_)
                tmp_free[2 + i_] = [hi, lo]
                FT[m % 8] = [hi, lo]
            for m in range(8):
                dense("w_ff1", f * 8 + m, hx, 8, fin1, RB)
                ada_unit()
                if len(zx) < 2 * NUNIT - 16:
                    u = len(zx)
                    dst, u = (t["xs"], u) if u < NUNIT else (t["ys"], u - NUNIT + 16)
                    src = TB[:, 2, 0:1024]
                    zx.append(sp.dma(lambda e, d=dst[128 * u:128 * u + 128, :]: e.dma_start(d, src), zsem,
                                     16 * (2 * NUNIT - 16), zz))
            if f == 3:
                md = load(act, TMP[0:48, 0, 0:128], t["mod"].rearrange("a b -> (a b)").rearrange("(m p) -> m p", p=128),
                          ad["out"], tmp_free[0])
                b = bank(RB)
                tok = tr(b.ap[:, 0:48], TMP[0:48, 0, 0:128], md, b.free, last=True)
                tmp_free[0] = [tok]
                ADB = RT[:, 512:560]
                cst["adab"] = load(act, ADB, t["adab"], adone)
                md = tt(dve, modt[:, :], b.ap[:, 0:48], ADB, ALU.add, tok, cst["adab"])
                b.free = [md]
                g1s = stt(gsc[:, 0:8], modt[:, 8:16], small[:, 1:2], vecs[:, VG1:VG1 + 8], ALU.add, ALU.mult, md, one)
                g2s = stt(gsc[:, 8:16], modt[:, 32:40], small[:, 1:2], vecs[:, VG2:VG2 + 8], ALU.add, ALU.mult, md, one)
                ggs = tt(dve, gsc[:, 16:24], gsc[:, 0:8], vecs[:, VG_FIN:VG_FIN + 8], ALU.mult, g1s, cst["vecs"])
            fa_ = (RH, 0, [FT[k] for k in range(8)])
            lastx[0] = 2 if f == 3 else 0
            for m in range(8):
                dense("w_ff2", f * 8 + m, fa_, 8, lambda mm_, b, tok: residual(mm_ % 8, b, tok), RB)
                ada_unit()
                if f == 0 and m == 1:
                    kz2 = [dve.do(lambda e, i=i: e.memset(M[:, 4 * i:4 * i + 4, :], 0.0), mread) for i in range(2)]
            f_free = [[(pe.sem, pe.n)]]
        h_free = [(pe.sem, pe.n)]
        a_free = h_free

        b, b2, b3_, b4_ = bank(), bank(), bank(), bank()
        r = mean_root(0, RST, b, sq["acc"])
        for i in range(4):
            tok = mm(b2.ap[:, i:i + 1], SQ2[:, 128 * i:128 * i + 128], onesf[:, 0:1], True, True, b2.free, sq["acc2"],
                     last=(i == 3))
        u = tt(dve, NR[:, 4:8], NR[:, 0:4], NR[:, 0:4], ALU.mult, r)
        u = tt(dve, NR[:, 4:8], NR[:, 4:8], b2.ap[:, 0:4], ALU.mult, u, tok)
        b2.free = [u]
        u = a_act(NR[:, 4:8], NR[:, 4:8], ACT.Sqrt, u, eps, bias=small[:, 0:1], scale=1.0 / D)
        u = dve.do(lambda e: e.reciprocal(NR[:, 4:8], NR[:, 4:8]), u)
        u = tt(dve, NR[:, 4:8], NR[:, 4:8], NR[:, 0:4], ALU.mult, u)
        r12 = spread(4, 3, b3_, u)
        r1 = spread(0, 2, b4_, r)
        H = []
        for k in range(8):
            j = k % 4
            w = stt(TMP[:, j, :], X[:, k, :], gsc[:, 16 + k:17 + k], b3_.ap[:, :], ALU.mult, ALU.mult, r12, xt[k],
                    ggs, tmp_free[j])
            hi = a_act(RH[:, 0, k, :], TMP[:, j, :], ACT.Identity, w, md, h_free, bias=modt[:, k:k + 1])
            lo = stt(RH[:, 1, k, :], TMP[:, j, :], modt[:, k:k + 1], hiF(RH[:, 0, k, :]), ALU.add, ALU.subtract, hi,
                     h_free, md)
            tmp_free[j] = [hi, lo]
            H.append([hi, lo])
        b3_.free = [w]
        for k in range(8):
            xt[k] = stt(X[:, k, :], X[:, k, :], vecs[:, VG_FIN + k:VG_FIN + k + 1], b4_.ap[:, :], ALU.mult, ALU.mult,
                        r1, xt[k], H[k])
        b4_.free = [xt[7]]
        rst_free[0] = [r, r1]
        if stop == "b1":
            return finish_program(nc, ctx, locals())
        dve.need(g1s, md)
        hx = (RH, 0, H)

        QA = PC
        VA = [VV[:, 0, :], VV[:, 1, :], TAB[:, 0, :], TAB[:, 1, :]]
        pcfree = ad["out"]
        q2, k2, v2 = {}, {}, {}

        def fin_q(m, b, tok):
            q2[m] = a_act(QA[:, m, :], b.ap[:, :], ACT.Copy, tok, pcfree, scale=0.125)
            b.free = [q2[m]]

        def fin_z(kz_tok, scale, store):
            def f(m, b, tok):
                a1 = a_act(M[0:64, 2 * m, :], b.ap[0:64, :], ACT.Copy, tok, kz_tok, scale=scale)
                a2 = a_act(M[64:128, 2 * m + 1, :], b.ap[64:128, :], ACT.Copy, tok, kz_tok, scale=scale)
                b.free = [a2]
                store[2 * m], store[2 * m + 1] = a1, a2
            return f

        def fin_v(i, b, tok):
            v2[i] = copy(dve, VA[i], b.ap[:, :], tok, vfree)
            b.free = [v2[i]]

        vfree = [h_free]
        for u in range(4):
            dense("w2_qa", u, hx, 8, fin_q)
        FR = TMP
        nf = {}

        def fin_fa(u, b, tok):
            y = a_act(FR[0:8, 0, :], b.ap[0:8, :], ACT.Identity, tok, tmp_free[0], cst["vecs"],
                      bias=vecs[0:8, V_BF:V_BF + 1])
            b.free = [y]
            ab = a_act(FR[0:8, 1, :], FR[0:8, 0, :], ACT.Abs, y, tmp_free[1])
            ex = a_act(FR[0:8, 1, :], FR[0:8, 1, :], ACT.Exp, ab, scale=-1.0)
            ln = a_act(FR[0:8, 1, :], FR[0:8, 1, :], ACT.Ln, ex, one, bias=small[0:8, 1:2])
            nm = ts(dve, FR[0:8, 0, :], FR[0:8, 0, :], -1.0, ALU.mult, ab, s2=0.0, op1=ALU.max)
            sm_ = tt(dve, FR[0:8, 2, :], FR[0:8, 0, :], FR[0:8, 1, :], ALU.add, nm, ln, tmp_free[2])
            z_ = dve.do(lambda e: e.memset(FR[0:8, 0, :], 0.0), sm_)
            sc = dve.do(lambda e: e.tensor_tensor_scan(FR[0:8, 3, :], FR[0:8, 2, :], FR[0:8, 0, :], 0.0,
                                                       ALU.add, ALU.add), sm_, z_, tmp_free[3])
            nf["d"] = load(act, t["nf"], FR[0:8, 3, :], sc)
            for i in range(4):
                tmp_free[i] = [sc, nf["d"]]
        dense("w2_fa", 0, hx, 8, fin_fa)
        for u in range(4):
            dense("w2_ka", u, hx, 8, fin_z(kz2, 1.0, k2))
        dense_rows("w2_va", 4, hx, fin_v, [0, 1, 2, 3])

        FB = [TMP[:, 0, :], TMP[:, 1, :]]
        fbl = {}
        fbfree = {0: [], 1: []}

        def fb_load(n):
            fbl[n] = load_slot(sp, f"fb{n % 2}", FB[n % 2], t["nf"][n:n + 1, :].broadcast_to([128, 512]), nf["d"], tmp_free[n % 2],
                          fbfree[n % 2])

        fb_load(0)

        def fox_add(n):
            def done(tok):
                fbfree[n % 2] = [tok]
            if n + 1 < 8:
                fb_load(n + 1)
            return FB[n % 2], fbl[n], done

        def fox_done(m, b, tok):
            if m % 2 == 1:
                RAT[m // 2] = list(split_to(RA, m // 2, b.ap[:, :], act, dve, a_free, tok))
                b.free = RAT[m // 2]

        adone2 = attention(
            8, lambda n, i: QA[:, n // 2, 128 * i:128 * i + 128],
            lambda n: M[:, n, :], lambda n: [q2[n // 2], k2[n]], fox_add, None,
            lambda m, j: (VA[j][:, 64 * m:64 * m + 64], v2[j]),
            lambda m: (banks[7], 64 * (m % 2)), lambda m, b: True, fox_done, [h_free])
        for i in range(2):
            tmp_free[i] = [tmp_free[i], fbfree[i]]
        if stop == "fox":
            return finish_program(nc, ctx, locals())

        pcfree = adone2
        vfree = adone2
        KB = PC
        kb2, qz2 = {}, {}

        def fin_kb(m, b, tok):
            kb2[m] = a_act(KB[:, m, :], b.ap[:, :], ACT.Copy, tok, adone2)
            b.free = [kb2[m]]
        for u in range(4):
            dense("w2_qb", u, hx, 8, fin_z(adone2, 0.125, qz2))
        for u in range(4):
            dense("w2_kb", u, hx, 8, fin_kb)
        dense_rows("w2_vb", 4, hx, fin_v, [0, 1, 2, 3])

        sets = [[0, 1, 2], [3, 4, 5]]
        place = [(0, 0), (1, 0), (2, 0), (1, 384)]
        zsp, zst = {}, {}
        spf, taf = [adone2] * 2, [adone2] * 3
        segs = [(0, 0, 512), (1, 512, 512), (2, 1024, 256)]
        ABT = TMP[:, :, :].rearrange("p a n -> p (a n)")[:, 0:1280]
        abf = [tmp_free[0], tmp_free[1], tmp_free[2]]
        avt = {}
        for n in range(10):
            if n < 8:
                h, pr = n, n // 2
                bs = [banks[i] for i in sets[n % 2]]
                SPt = PB[:, n % 2, :]
                for j in (0, 1, 3, 2):
                    bi, o = place[j]
                    w = 512 - 128 * j
                    tok = mm(bs[bi].ap[:, o:o + w], KB[:, pr, 128 * j:128 * j + 128], M[:, h, 128 * j:512],
                             o == 0, False, kb2[pr], qz2[h], *(bs[bi].free if o == 0 else ()), last=True,
                             shared=True)
                ab = []
                for bi, o, w in segs:
                    ab.append(a_act(ABT[:, o:o + w], bs[bi].ap[:, 0:w], ACT.Abs, tok, abf))
                ex = a_act(ABT, ABT, ACT.Exp, ab, scale=-1.0)
                ln = a_act(ABT, ABT, ACT.Ln, ex, one, bias=small[:, 1:2])
                sps = []
                for bi, o, w in segs:
                    sps.append(stt(SPt[:, o:o + w], bs[bi].ap[:, 0:w], 0.0, ABT[:, o:o + w], ALU.max, ALU.add,
                                   ln, tok, spf[n % 2]))
                abf = [sps[-1]]
                mk = []
                for j in range(4):
                    o = PACK[j]
                    mk.append(tt(pool, SPt[:, o:o + 128], SPt[:, o:o + 128], sltm[:, :], ALU.mult, sps,
                                 cst["sltm"]))
                zsp[n], zst[n] = (sps, mk), bs
            if 1 <= n <= 8:
                m = n - 1
                bs = zst[m]
                SPt, TAt = PB[:, m % 2, :], TB[:, m % 3, :]
                sps, mk = zsp[m]
                av = []
                for j in (0, 1, 3, 2):
                    bi, o = place[j]
                    w = 512 - 128 * j
                    mm(bs[bi].ap[:, o:o + w], ntri[:, :], SPt[:, PACK[j]:PACK[j] + w], False, False, mk, sps,
                       cst["ntri"], cst["nones"], shared=True)
                    for jj in range(j + 1, 4):
                        w2 = 512 - 128 * jj
                        mm(bs[bi].ap[:, o + 128 * (jj - j):o + w], nones[:, :], SPt[:, PACK[jj]:PACK[jj] + w2],
                           False, False, shared=True)
                    tok = mm(bs[bi].ap[:, o:o + 128], identb[:, :], maskt[:, :], False, True, cst["maskt"],
                             last=True, shared=True)
                    if j == 1:
                        continue
                    bi, o, w = segs[bi]
                    av.append(a_act(TAt[:, o:o + w], bs[bi].ap[:, 0:w], ACT.Exp, tok, taf[m % 3]))
                    bs[bi].free = [av[-1]]
                spf[m % 2] = [tok]
                avt[m] = av
            if n >= 3 and n % 2 == 1:
                b = banks[6 + (n // 2) % 2]
                for j in range(4):
                    for m in (n - 3, n - 2):
                        r0 = 64 * (m % 2)
                        tok = mm(b.ap[r0:r0 + 64, 128 * j:512], VA[j][:, 64 * m:64 * m + 64],
                                 TB[:, m % 3, PACK[j]:PACK[j] + 512 - 128 * j], j == 0, False, avt[m], v2[j],
                                 *(b.free if j == 0 else ()), last=True, shared=True)
                taf[(n - 3) % 3] = taf[(n - 2) % 3] = [tok]
                k = 4 + (n - 3) // 2
                RAT[k] = list(split_to(RA, k, b.ap[:, :], act, dve, a_free, tok))
                b.free = RAT[k]
        for i in range(3):
            tmp_free[i] = abf
        sdone = spf + taf + [(act.sem, act.n), (dve.sem, dve.n)]
        if stop == "sb":
            return finish_program(nc, ctx, locals())

        fo, so = (RA, 0, [RAT[k] for k in range(4)]), (RA, 4, [RAT[4 + k] for k in range(4)])
        for m in range(0, 8, 2):
            dense("w2_ga", m, hx, 8, gate_fin(gt))
            dense("w2_ga", m + 1, hx, 8, gate_fin(gt))
            dense("w2_fox", m // 2, fo, 4, merge_fin(True, sdone))
            dense("w2_gb", m, hx, 8, gate_fin(gt))
            dense("w2_gb", m + 1, hx, 8, gate_fin(gt))
            if m == 6:
                h_free = [(pe.sem, pe.n)]
                H = [merged(k, h_free) for k in range(6)]
            dense("w2_sb", m // 2, so, 4, merge_fin(False, None))
        ra_free2 = [(pe.sem, pe.n)]
        for i in range(NRAW, NRAW + 8):
            raw_free[i] = ra_free2
        RW = TAB[:, 0, 0:160]
        cst["rw"] = load(act, RW, t["rw"], sdone)
        cst["rk"] = load(act, VV[:, 0, 0:64], t["rk"], sdone)
        H += [merged(k, h_free) for k in (6, 7)]

        def residual2(m, b, tok):
            o = stt(X[:, m, :], b.ap[:, :], modt[:, 16 + m:17 + m], X[:, m, :], ALU.mult, ALU.add, tok, xt[m], md)
            b.free = [o]
            xt[m] = o
            square_in(m, o)
        for m in range(8):
            dense("w2_out", m, (RH, 0, H), 8, residual2)
        if stop == "mix2":
            return finish_program(nc, ctx, locals())

        b, b2 = bank(), bank()
        r = spread(0, 3, b2, mean_root(0, RST, b, sq["acc"]))
        ht = []
        for k in range(8):
            w = stt(M[:, k, :], X[:, k, :], gsc[:, 8 + k:9 + k], b2.ap[:, :], ALU.mult, ALU.mult, r, xt[k], g2s, H[k])
            b2.free = [w]
            ht.append(a_act(M[:, k, :], M[:, k, :], ACT.Identity, w, md, bias=modt[:, 24 + k:25 + k]))
        b = bank()
        for k in range(8):
            tok = mm(b.ap[0:20, :], RW[:, 20 * k:20 * k + 20], M[:, k, :], k == 0, k == 7, ht[k], cst["rw"], b.free,
                     last=(k == 7))
        LT = TMP[0:20, 0, :]
        l1 = a_act(LT, b.ap[0:20, :], ACT.Identity, tok, tmp_free[0], bias=vecs[0:20, V_BF + 1:V_BF + 2])
        b.free = [l1]
        b = bank()
        for i in range(4):
            tok = tr(b.ap[:, 20 * i:20 * i + 20], TMP[0:20, 0, 128 * i:128 * i + 128], l1, b.free, last=(i == 3))
        XT_ = [VV, TAB]
        pos_rows = []
        vt_free = {0: [sdone], 1: [sdone, cst["rw"], tok]}
        HT4 = {}

        def rows_of(i):
            bb = [banks[2 * (i % 2) + 4 * 0], banks[2 * (i % 2) + 1]]
            dst = (PB, TB)[i // 2][:, i % 2, 0:1024]
            cps = []
            for hf in range(2):
                for k in range(4):
                    tk = tr(bb[hf].ap[:, 128 * k:128 * k + 128], M[:, 4 * hf + k, 128 * i:128 * i + 128],
                            ht[4 * hf + k], bb[hf].free, last=(k == 3))
                c = copy(act if hf else dve, dst[:, 512 * hf:512 * hf + 512], bb[hf].ap[:, :], tk, sdone)
                bb[hf].free = [c]
                cps.append(c)
            return dst, cps
        LG = RT[:, 560:640]
        LG3 = LG.rearrange("p (i n) -> p i n", n=20)
        c0 = copy(dve, LG, b.ap[:, 0:80], tok)
        b.free = [c0]
        hrows = [rows_of(i) for i in range(4)]
        for i in range(NRAW + 8, NWIDE):
            raw_free[i] = [(pe.sem, pe.n)]

        R_ = TMP[:, 1:4, :].rearrange("p a n -> p (a n)")
        ro = [0]

        def reg(n):
            a = R_[:, ro[0]:ro[0] + n]
            ro[0] += n
            return a
        w0 = [tmp_free[1], tmp_free[2], tmp_free[3]]
        dve.need(w0)
        last = [c0]

        def v(fn):
            last[0] = dve.do(fn, last[0])
            return last[0]

        def vtt(o, a, b_, op):
            return v(lambda e: e.tensor_tensor(o, a, b_, op))

        W4_ = RW4 = VV[:, 0, 0:64]
        dve.need(cst["rk"])
        RK4 = VV[:, 0, 0:16].rearrange("p (i n) -> p i n", n=4)
        E128 = VV[:, 0, 16:32]
        JJ = VV[:, 0, 32:39]

        def b3(a, n):
            return a.unsqueeze(2).broadcast_to([128, 4, n])

        def first_max(src, n):
            mx, oh, m2 = reg(4), reg(16), reg(4)
            oh3 = oh.rearrange("p (i n) -> p i n", n=4)
            v(lambda e: e.reduce_max(mx, src, AX))
            vtt(oh3, src, b3(mx, 4), ALU.is_equal)
            vtt(oh3, oh3, RK4, ALU.mult)
            v(lambda e: e.reduce_max(m2, oh3, AX))
            vtt(oh3, oh3, b3(m2, 4), ALU.is_equal)
            return mx, oh3
        G3, E3 = LG3[:, :, 0:4], LG3[:, :, 4:20]
        gm, gh = first_max(G3, 4)
        em = reg(64)
        es = reg(16).rearrange("p (i n) -> p i n", n=4)
        em4 = em.rearrange("p (i g e) -> p i g e", i=4, g=4)
        E4 = E3.rearrange("p i (g e) -> p i g e", g=4)
        vtt(em4, E4, gh.unsqueeze(3).broadcast_to([128, 4, 4, 4]), ALU.mult)
        v(lambda e: e.reduce_sum(es, em4.rearrange("p i g e -> p i e g"), AX))
        m1, o1 = first_max(es, 4)
        e2_ = reg(16).rearrange("p (i n) -> p i n", n=4)
        v(lambda e: e.scalar_tensor_tensor(e2_, o1, NEG, es, ALU.mult, ALU.add))
        m2, o2 = first_max(e2_, 4)
        OE = [reg(64), reg(64)]
        for kk, oo in enumerate((o1, o2)):
            vtt(OE[kk].rearrange("p (i g e) -> p i g e", i=4, g=4), gh.unsqueeze(3).broadcast_to([128, 4, 4, 4]),
                oo.unsqueeze(2).broadcast_to([128, 4, 4, 4]), ALU.mult)
        vtt(MB[:, 0:64], OE[0], OE[1], ALU.add)
        b = bank(list(range(4, 8)))
        mbt = last[0]
        for i in range(4):
            for ii in range(i + 1):
                mm(b.ap[:, 16 * i:16 * i + 16], trib[:, :] if ii == i else onesb[:, :],
                   MB[:, 16 * ii:16 * ii + 16], ii == 0 and i == 0, False, mbt, cst["trib"], cst["onesb"], b.free,
                   shared=True)
        for ii in range(4):
            tok = mm(b.ap[:, 64:80], onesb[:, :], MB[:, 16 * ii:16 * ii + 16], False, ii == 3, last=(ii == 3),
                     shared=True)
        rank = reg(80)
        last[0] = copy(dve, rank, b.ap[:, 0:80], tok)
        b.free = [last[0]]
        NE = rank[:, 64:80]
        xe, xa, xi = reg(16), reg(16), reg(16)
        v(lambda e: e.tensor_scalar(xe, NE, 128.5, None, ALU.is_gt))
        for lim in (256.5, 384.5):
            v(lambda e, lim=lim: e.scalar_tensor_tensor(xe, NE, lim, xe, ALU.is_gt, ALU.add))
        v(lambda e: e.memset(xa, 0.0))
        v(lambda e: e.tensor_tensor_scan(xi, xe, xa, 0.0, ALU.add, ALU.add))
        base = reg(16)
        vtt(base, xi, xe, ALU.subtract)
        v(lambda e: e.tensor_scalar(base, base, 128.0, 1920.0, ALU.mult, ALU.add))
        vtt(base, base, E128, ALU.subtract)
        vl = reg(64)
        POSF = reg(8)
        R3, V3 = rank[:, 0:64].rearrange("p (i e) -> p i e", i=4), vl.rearrange("p (i e) -> p i e", i=4)
        v(lambda e: e.scalar_tensor_tensor(V3, R3, 127.5, base.unsqueeze(1).broadcast_to([128, 4, 16]),
                                           ALU.is_gt, ALU.mult))
        vtt(V3, V3, R3, ALU.add)
        vtt(V3, V3, E128.unsqueeze(1).broadcast_to([128, 4, 16]), ALU.add)
        for kk in range(2):
            vtt(OE[kk], OE[kk], vl, ALU.mult)
            v(lambda e, kk=kk: e.reduce_sum(POSF[:, 4 * kk:4 * kk + 4], OE[kk].rearrange("p (i n) -> p i n", n=16), AX))
        pos_t = v(lambda e: e.tensor_copy(POS[:, :], POSF))
        ej, cj = reg(8), reg(112).rearrange("p (j e) -> p j e", j=7)
        v(lambda e: e.tensor_tensor(cj[0:1], xi[0:1, :].unsqueeze(1).broadcast_to([1, 7, 16]),
                                    JJ[0:1, :].unsqueeze(2).broadcast_to([1, 7, 16]), ALU.is_lt))
        v(lambda e: e.reduce_sum(ej[0:1, 0:7], cj[0:1], AX))
        v(lambda e: e.tensor_scalar(ej[0:1, 0:7], ej[0:1, 0:7], 15.0, None, ALU.min))
        v(lambda e: e.tensor_copy(ej[0:1, 7:8], xi[0:1, 15:16]))
        late["tok"] = v(lambda e: e.tensor_copy(EXI[0:1, 0:8], ej[0:1, 0:8]))
        gx = reg(16).rearrange("p (i n) -> p i n", n=4)
        gs = reg(4)
        vtt(gx, G3, b3(gm, 4), ALU.subtract)
        last[0] = a_act(gx, gx, ACT.Exp, last[0])
        v(lambda e: e.reduce_sum(gs, gx, AX))
        v(lambda e: e.reciprocal(gs, gs))
        ex = reg(16).rearrange("p (i n) -> p i n", n=4)
        vtt(ex, es, b3(m1, 4), ALU.subtract)
        last[0] = a_act(ex, ex, ACT.Exp, last[0])
        zs = reg(4)
        v(lambda e: e.reduce_sum(zs, ex, AX))
        v(lambda e: e.reciprocal(zs, zs))
        vtt(ex, ex, b3(zs, 4), ALU.mult)
        pk = reg(8).rearrange("p (k i) -> p k i", k=2)
        px = reg(16).rearrange("p (i n) -> p i n", n=4)
        for kk, oo in enumerate((o1, o2)):
            vtt(px, ex, oo, ALU.mult)
            v(lambda e, o=pk[:, kk, :]: e.reduce_sum(o, px, AX))
        ps_ = reg(4)
        vtt(ps_, pk[:, 0, :], pk[:, 1, :], ALU.add)
        v(lambda e: e.reciprocal(ps_, ps_))
        vtt(ps_, ps_, gs, ALU.mult)
        WK = RT[:, 640:648].rearrange("p (k i) -> p k i", k=2)
        for kk in range(2):
            vtt(WK[:, kk, :], pk[:, kk, :], ps_, ALU.mult)
        wk_tok = last[0]
        ssem = sem("scatter")
        for i in range(4):
            for kk in range(2):
                c = 4 * kk + i
                sct = [pool.dma(lambda e, c=c, i=i: e.indirect_dma_start(
                    t["xs"], bass.IndirectOffsetOnAxis(ap=POS[:, c:c + 1], axis=0), hrows[i][0], None),
                    ssem, 32 * i + 16 * kk + 16, pos_t, hrows[i][1], zx)]
        if stop == "route":
            return finish_program(nc, ctx, locals())

        G2, GF, G2B = flat(TAB[:, :, :]), flat(VV[:, :, :]), flat(PC[:, 2:4, :])
        one_row = lambda a: a.rearrange("(o n) -> o n", o=1).broadcast_to([128, 1024])
        free = [sdone, (pe.sem, pe.n), (dve.sem, dve.n)]
        g2r = load_slot(act, "g2r", G2, one_row(t["mod"][10:12, :].rearrange("a b -> (a b)")), free)
        g2b = load_slot(act, "g2b", G2B, one_row(t["g2b"]), free)
        gfb = load_slot(act, "gfb", GF, one_row(t["final_g"]), free)
        g2 = tt(dve, G2, G2, G2B, ALU.add, g2r, g2b)

        lo_engine[0] = lambda n: pool if n % 3 == 2 else dve
        xin = [PB[:, 0, 0:1024], PB[:, 1, 0:1024]]
        yout = [TB[:, 0, 0:1024], TB[:, 1, 0:1024]]
        xin_f, yout_f = [sct, sct], [sct, sct]
        XH = [RH[:, :, 0:2, :], RH[:, :, 2:4, :]]
        AH = [RH[:, :, 4, :], RH[:, :, 5, :]]
        hfree = [(pe.sem, pe.n)]
        xh_f, ah_f = [hfree, hfree], [hfree, hfree]
        GU = [PC[:, 0, :], PC[:, 1, :]]
        gu_f = [sdone, sdone]
        xl, xht, aht, yst = {}, {}, {}, []

        def load_x(u):
            xl[u] = load_slot(act, f"x{u % 2}{u // 16}", xin[u % 2], t["xs"][128 * u:128 * u + 128, :], sct, xin_f[u % 2])

        def prep(u):
            tk = []
            for hf in range(2):
                b = banks[hf]
                for k in range(4):
                    c = (4 * hf + k) * 128
                    tok = tr(b.ap[:, 128 * k:128 * k + 128], xin[u % 2][:, c:c + 128], xl[u], b.free, last=(k == 3))
                d = XH[u % 2]
                hi = copy(act, d[:, 0, hf, :], b.ap[:, :], tok, xh_f[u % 2])
                lo = tt(dve, d[:, 1, hf, :], b.ap[:, :], hiF(d[:, 0, hf, :]), ALU.subtract, hi, xh_f[u % 2])
                b.free = [lo]
                tk.append([hi, lo])
            xin_f[u % 2] = [tok]
            xht[u] = tk

        def up(u, name, b):
            d = XH[u % 2]
            for c in range(4):
                n = get(name, (u, c))
                s, lo_t, hi_t = parts[n]
                for kk in range(2):
                    k = 2 * c + kk
                    xh, xlo = (d[:, x, k // 4, 128 * (k % 4):128 * (k % 4) + 128] for x in (0, 1))
                    wh, wl = (RS[:, s, x, 512 * kk:512 * kk + 512] for x in (0, 1))
                    mm(b.ap[:, :], xh, wh, k == 0, False, hi_t, xht[u][k // 4], *(b.free if k == 0 else ()))
                    mm(b.ap[:, :], xlo, wh, False, False)
                    tok = mm(b.ap[:, :], xh, wl, False, k == 7, lo_t, last=(kk == 1))
                used(n, tok)
            return tok

        def down(u):
            bb = [banks[5], banks[6]]
            d = AH[u % 2]
            for c in range(4):
                n = get("w_down", (u, c))
                s, lo_t, hi_t = parts[n]
                for hf in range(2):
                    b = bb[hf]
                    xh, xlo = (d[:, x, 128 * c:128 * c + 128] for x in (0, 1))
                    wh, wl = (RS[:, s, x, 512 * hf:512 * hf + 512] for x in (0, 1))
                    mm(b.ap[:, :], xh, wh, c == 0, False, hi_t, aht[u], *(b.free if c == 0 else ()))
                    mm(b.ap[:, :], xlo, wh, False, False)
                    tok = mm(b.ap[:, :], xh, wl, False, c == 3, lo_t, last=True)
                    if c == 3:
                        cp = tt(dve, yout[u % 2][:, 512 * hf:512 * hf + 512], b.ap[:, :],
                                G2[:, 512 * hf:512 * hf + 512], ALU.mult, tok, g2, yout_f[u % 2])
                        b.free = [cp]
                        cps.append(cp)
                used(n, tok)
            ah_f[u % 2] = [tok]
            yst.append(load_slot(act, f"y{u % 2}{u // 16}", t["ys"][128 * u:128 * u + 128, :], yout[u % 2], cps[-2:], zx))
            yout_f[u % 2] = [yst[-1]]

        cps = []

        def experts(u0, u1):
            load_x(u0)
            load_x(u0 + 1)
            prep(u0)
            for u in range(u0, u1):
                tg = up(u, "w_gate", banks[2])
                G_ = GU[u % 2]
                s1 = a_act(G_, banks[2].ap[:, :], ACT.Silu, tg, gu_f[u % 2])
                banks[2].free = [s1]
                if u + 1 < u1:
                    prep(u + 1)
                tu = up(u, "w_up", banks[3])
                xh_f[u % 2] = [tu]
                s2 = tt(dve, G_, G_, banks[3].ap[:, :], ALU.mult, s1, tu)
                banks[3].free = [s2]
                if u + 2 < u1:
                    load_x(u + 2)
                if u > u0:
                    down(u - 1)
                b = banks[4]
                for k in range(4):
                    tok = tr(b.ap[:, 128 * k:128 * k + 128], G_[:, 128 * k:128 * k + 128], s2, b.free, last=(k == 3))
                gu_f[u % 2] = [tok]
                hi = copy(act, AH[u % 2][:, 0, :], b.ap[:, :], tok, ah_f[u % 2])
                lo = tt(dve, AH[u % 2][:, 1, :], b.ap[:, :], hiF(AH[u % 2][:, 0, :]), ALU.subtract, hi, ah_f[u % 2])
                b.free = [lo]
                aht[u] = [hi, lo]
            down(u1 - 1)

        experts(0, 16)
        base_st = list(yst)
        base_raw = list(zip(raw_sem, raw_n))
        queues = (pe, act, dve, pool, sp)
        for q in queues:
            q.branch(EXI[0:1, 7:8], late["tok"])
        yst.clear()
        experts(16, NUNIT)
        sp.need([tuple(slots[k]) for k in ("x01", "x11", "y01", "y11")], list(zip(raw_sem, raw_n)))
        for q in queues:
            q.join()
        yst = [sp.bump(), base_st]
        yout_f = [yst, yst]

        outs = []
        bufs = [[PC[:, 0:2, :], PC[:, 2:4, :]], [TMP[:, 0:2, :], TMP[:, 2:4, :]]]
        bufs = [[x.rearrange("p a b -> p (a b)") for x in p_] for p_ in bufs]
        bufs += [[PB[:, 0, 0:1024], PB[:, 1, 0:1024]], [TB[:, 0, 0:1024], TB[:, 1, 0:1024]]]
        yall = [yst, gu_f, xin_f, yout_f, [(act.sem, act.n), (dve.sem, dve.n), (pe.sem, pe.n)]]
        gat = {}
        for i in range(4):
            gs_ = sem(f"gat{i}")
            for kk in range(2):
                c = 4 * kk + i
                gat[i] = pool.dma(lambda e, c=c, d=bufs[i][kk]: e.indirect_dma_start(
                    d, None, t["ys"], bass.IndirectOffsetOnAxis(ap=POS[:, c:c + 1], axis=0)), gs_, 16 * kk + 16, yall)
        xps = {}

        def x_rows(i):
            bb = [banks[2 * i], banks[2 * i + 1]]
            for hf in range(2):
                for k in range(4):
                    tk = tr(bb[hf].ap[:, 128 * k:128 * k + 128], X[:, 4 * hf + k, 128 * i:128 * i + 128],
                            xt[4 * hf + k], bb[hf].free, last=(k == 3))
            xps[i] = (bb, tk)

        for i in range(4):
            x_rows(i)
        root0 = a_act(small[:, 24:25], small[:, 1:2], ACT.Sqrt, one)
        fin = {}

        def normed_out(i):
            A_, B_ = bufs[i]
            ss = small[:, 16 + i:17 + i]
            q3 = dve.do(lambda e: e.reciprocal(ss, ss), fin[i])
            if i < 2:
                q4 = a_act(A_, A_, ACT.Copy, q3, scale=ss)
                q5 = tt(pool, B_, A_, GF, ALU.mult, q4, gfb)
                outs.append(load(sp, t["out"][0, 128 * i:128 * i + 128, :], B_, q5))
                return
            for hf in range(2):
                h = slice(512 * hf, 512 * hf + 512)
                q4 = stt(B_[:, h], A_[:, h], ss, GF[:, h], ALU.mult, ALU.mult, q3, gfb)
                outs.append(load(sp, t["out"][0, 128 * i:128 * i + 128, h], B_[:, h], q4))

        for i in range(4):
            A_, B_ = bufs[i]
            bb, tk = xps[i]
            y1 = []
            for hf in range(2):
                h = slice(512 * hf, 512 * hf + 512)
                y1.append(stt(A_[:, h], A_[:, h], WK[:, 0, i:i + 1], bb[hf].ap[:, :], ALU.mult, ALU.add, gat[i], tk,
                              wk_tok))
            y2 = stt(A_, B_, WK[:, 1, i:i + 1], A_, ALU.mult, ALU.add, y1)
            ss = small[:, 16 + i:17 + i]
            q1 = a_act(B_, A_, ACT.Square, y2, accum_out=ss)
            fin[i] = a_act(ss, ss, ACT.Sqrt, q1, bias=small[:, 0:1], scale=1.0 / D)
            if i >= 1:
                normed_out(i - 1)
        normed_out(3)
        sp.need(outs, yst, every, base_raw)
        return finish_program(nc, ctx, locals())


def finish_program(nc, ctx, env):
    sp, pe, act, dve, pool = (env[n] for n in ("sp", "pe", "act", "dve", "pool"))
    if env["stop"] is not None:
        for q in (pe, act, dve, pool):
            sp.need((q.sem, q.n))
        sp.need(env["every"])
        sp.need(list(zip(env["raw_sem"], env["raw_n"])))
        if "sct" in env:
            sp.need(env["sct"])
        fin = ctx.enter_context(nc.semaphore("s_fin"))
        o = env["t"]["out"][0, 0:128, 0:128]
        sp.dma(lambda e: e.dma_start(o, env["identf"][:, :]), fin, 16)
        sp.need((fin, 16))
    block = ctx.enter_context(nc.Block())
    for q, name in ((sp, "sync"), (pe, "tensor"), (act, "scalar"), (dve, "vector"), (pool, "gpsimd")):
        def body(eng, q=q):
            q.emit(eng)
        {"sync": block.sync, "tensor": block.tensor, "scalar": block.scalar, "vector": block.vector,
         "gpsimd": block.gpsimd}[name](body)


def tiles(w, pad=0):
    w = np.asarray(w)
    if pad:
        w = np.concatenate([w, np.zeros((w.shape[0], pad), w.dtype)], axis=1)
    K, N = w.shape[0] // 128, w.shape[1] // 128
    per = 8 // K
    a = w.reshape(K, 128, N // per, per, 128).transpose(2, 1, 3, 0, 4)
    return np.ascontiguousarray(a).reshape(N // per, 128, 1024)


def rows(w):
    w = np.asarray(w)
    K = w.shape[0] // 256
    return np.ascontiguousarray(w.reshape(K, 2, 128, 512).transpose(0, 2, 1, 3)).reshape(K, 128, 1024)


def cols(v, n):
    return np.asarray(v).reshape(n, 128).T


def constants():
    f = np.float32
    c = {}
    c["identf"] = np.eye(128, dtype=f)
    r = np.zeros((128, 128), f)
    for b in range(2):
        for d in range(64):
            if d < 32:
                r[64 * b + d + 32, 64 * b + d] = -1
            else:
                r[64 * b + d - 32, 64 * b + d] = 1
    c["rotT"] = r
    c["onesf"] = np.ones((128, 128), f)
    i, j = np.arange(128)[:, None], np.arange(128)[None, :]
    c["ntri"] = -(i >= j).astype(f)
    c["nones"] = -np.ones((128, 128), f)
    c["sltm"] = (i < j).astype(f)
    c["maskb"] = np.where(j > i, NEG, 0.0).astype(f)
    c["maskt"] = np.where(i >= j, NEG, 0.0).astype(f)
    inv = np.power(f(10000.0), -np.arange(0, 64, 2, dtype=f) / f(64)).astype(f)

    def table(pos):
        ang = (pos.astype(f)[:, None] * inv[None, :]).astype(f)
        ang = np.concatenate([ang, ang], axis=-1)
        return np.cos(ang).T.astype(f), np.sin(ang).T.astype(f)
    co, si = table(np.arange(S))
    c["tab"] = np.stack([np.concatenate([co, co]), np.concatenate([si, si])], axis=1)
    co, si = table(np.arange(CMP) * 16 + 31)
    c["ctb"] = np.concatenate([np.tile(co, (2, 2)), np.tile(si, (2, 2))], axis=1)
    tt_ = np.arange(S).reshape(4, 128).T[:, :, None]
    n = np.arange(32)[None, None, :]
    c["mcb"] = np.where((16 * n + 31 > tt_) | (n == 31), NEG, 0.0).astype(f).reshape(128, 128)
    c["ict"] = np.tile(np.concatenate([1.0 / np.minimum(np.arange(16) + 1, w) for w in (2, 4, 8, 16)]).astype(f), (128, 1))
    rk = np.zeros((128, 64), f)
    rk[:, 0:16] = np.tile(np.array([4, 3, 2, 1], f), 4)
    rk[:, 16:32] = 128 * np.arange(16)
    rk[:, 32:39] = np.arange(7) + 0.5
    c["rk"] = rk
    return c


def layout(i):
    a = {}
    a["xT"] = np.ascontiguousarray(np.asarray(i["x"])[0].T.reshape(8, 128, S).transpose(1, 0, 2))
    w = np.asarray(i["w_in"])[0]
    u, q, kc, vc, ks, vs, kw, vw, g, gm = np.split(w, np.cumsum([512, 1024, 128, 128, 128, 128, 128, 128, 48]), axis=1)
    a["w_qkv"] = tiles(np.concatenate([q, ks, kw, kc, vc, vs, vw, g], axis=1), pad=80)
    ck = [np.asarray(i[n])[0].reshape(4, 4, 128, 256).transpose(0, 2, 1, 3).reshape(4, 128, 1024)
          for n in ("w_ck1", "w_cv1")]
    a["w_c"] = np.concatenate(ck)
    c2 = np.asarray(i["w_ck2"])[0].reshape(2, 128, 64).transpose(1, 0, 2)
    v2 = np.asarray(i["w_cv2"])[0].reshape(2, 128, 64).transpose(1, 0, 2)
    a["cw2"] = np.concatenate([c2, c2, v2], axis=2)
    a["pe2"] = np.concatenate([np.asarray(i[n])[0].reshape(16, 128).T for n in ("pe_k", "pe_v")], axis=1)
    a["w_ga"], a["w_gb"] = tiles(gm[:, :1024]), tiles(gm[:, 1024:])
    a["w_nsa"] = tiles(i["w_proj_nsa"][0])
    a["w_u"] = tiles(u)
    a["w_pool"] = np.ascontiguousarray(np.asarray(i["w_pool"])[0].transpose(1, 0, 2).reshape(128, 512))
    a["w_pp"] = tiles(i["w_proj_pool"][0])
    a["w_out"] = tiles(i["w_out"][0])
    a["w_ff1"] = tiles(i["w_ff1"][0])
    f2 = np.asarray(i["w_ff2"])[0]
    a["w_ff2"] = np.concatenate([tiles(f2[1024 * f:1024 * f + 1024]) for f in range(4)])
    aw = np.asarray(i["ada_w_2"])[0].reshape(8, 128, 3, 2, 1024).transpose(2, 0, 3, 1, 4)
    a["ada"] = np.ascontiguousarray(aw).reshape(48, 128, 1024)
    a["adab"] = cols(i["ada_b_2"][0], 48)
    a["g2b"] = np.asarray(i["ada_b_2"])[0, 5120:6144]
    w = np.asarray(i["w_in_2"])[0]
    sp_ = np.split(w, [512, 1024, 1536, 1544, 2056, 2568, 3080, 4104], axis=1)
    for n, x in zip(("qa", "ka", "va", "fa", "qb", "kb", "vb", "ga", "gb"), sp_):
        a["w2_" + n] = rows(x) if n in ("va", "vb") else tiles(x, pad=120 if n == "fa" else 0)
    a["w2_fox"], a["w2_sb"] = tiles(i["w_branch_fox_2"][0]), tiles(i["w_branch_sb_2"][0])
    a["w2_out"] = tiles(i["w_out_2"][0])
    vec = np.zeros((128, 64), np.float32)
    vec[:, 0:8], vec[:, 8:16] = cols(i["norm_mix"][0], 8), cols(i["norm_mlp"][0], 8)
    vec[:, 16:24], vec[:, 24:28] = cols(i["norm_final"], 8), cols(i["pool_scale"][0], 4)
    vec[:, 28:36], vec[:, 36:44] = cols(i["norm1_g_2"][0], 8), cols(i["norm2_g_2"][0], 8)
    vec[:, 44:52] = cols(i["c_2"][0], 8)
    vec[0:8, 52] = np.asarray(i["b_forget_2"])[0]
    vec[0:4, 53], vec[4:20, 53] = np.asarray(i["router_group_b_2"])[0], np.asarray(i["router_expert_b_2"])[0]
    a["vecs"] = vec
    rw = np.concatenate([np.asarray(i["router_group_w_2"])[0], np.asarray(i["router_expert_w_2"])[0]], axis=1)
    a["rw"] = rw.reshape(8, 128, 20).transpose(1, 0, 2).reshape(128, 160)
    for n, k in (("w_gate", "expert_w_gate_2"), ("w_up", "expert_w_up_2")):
        x = np.asarray(i[k])[0].reshape(16, 4, 2, 128, 512).transpose(0, 1, 3, 2, 4)
        a[n] = np.ascontiguousarray(x).reshape(16, 4, 128, 1024)
    a["w_down"] = np.asarray(i["expert_w_down_2"])[0].reshape(16, 4, 128, 1024)
    a["final_g"] = np.asarray(i["final_g_2"])
    a.update(constants())
    return {k: np.ascontiguousarray(v) for k, v in a.items()}


def build(nc, arrays, stop=None):
    t = {}
    for name, a in arrays.items():
        t[name] = nc.dram_tensor(f"in_{name}", a.shape, mybir.dt.from_np(a.dtype), kind="ExternalInput").ap()
    t["out"] = nc.dram_tensor("out_0", (1, S, D), F32, kind="ExternalOutput").ap()
    t["xs"] = nc.dram_tensor("xs", (NUNIT * 128, D), F32, kind="Internal").ap()
    t["ys"] = nc.dram_tensor("ys", (NUNIT * 128, D), F32, kind="Internal").ap()
    t["mod"] = nc.dram_tensor("mod", (12, 512), F32, kind="Internal").ap()
    t["nf"] = nc.dram_tensor("nf", (8, 512), F32, kind="Internal").ap()
    program(nc, t, stop)


def kernel(**inputs):
    import concourse.bacc as bacc
    from concourse.bass_utils import run_bass_kernel_spmd

    nc = bacc.Bacc("TRN2", target_bir_lowering=False, num_devices=1)
    arrays = layout(inputs)
    build(nc, arrays)
    r = run_bass_kernel_spmd(nc, [{f"in_{k}": v for k, v in arrays.items()}], core_ids=[0])
    return r.results[0]["out_0"]
```
